# Optimizing a Trainium2 kernel written in Bass

```python
import math
import jax, jax.numpy as jnp
from jax import lax
import numpy as np

D_MODEL = 1024
BATCH = 1
SEQ = 512
DEPTH = 2

N_MIXERS = 2
N_HGRN_LAYERS = (DEPTH + 1) // 2
N_HYENA_LAYERS = DEPTH // 2
HG_EXPAND = 128
HG_HEADS = D_MODEL // HG_EXPAND
HG_DK = HG_EXPAND
HG_DV = D_MODEL // HG_HEADS
HG_CHUNK = 64
HY_SHORT_CONV = 3
HY_FILTER_WIDTH = 64
HY_FILTER_INNER = 2
HY_EMB_DIM = 33
HY_BANDS = (HY_EMB_DIM - 1) // 2
HY_MAX_DECAY = math.log(1e-2) / 0.3
HY_MIN_DECAY = math.log(1e-2) / 1.5
D_FF = 4 * D_MODEL
NORM_EPS = 1e-6

kernel_name = "hybrid_hgrn2_hyena_adaln_encoder"

def rms_norm(x, g):
    xf = x.astype(jnp.float32)
    y = xf * lax.rsqrt(jnp.mean(xf * xf, axis=-1, keepdims=True) + NORM_EPS)
    return (y * g.astype(jnp.float32)).astype(x.dtype)

def adaln_params(c, w, b):
    m = jax.nn.silu(c) @ w + b
    shift, scale, gate = jnp.split(m[:, None, :], 3, axis=-1)
    return shift, scale, gate

def gla_chunk_scan(q, k, v, log_f):
    n, L, H, DK = q.shape
    DV = v.shape[-1]
    C = HG_CHUNK
    nc = L // C

    def to_chunks(a):
        return a.reshape(n, nc, C, H, a.shape[-1]).transpose(1, 0, 3, 2, 4)

    qc, kc, vc, gc = to_chunks(q), to_chunks(k), to_chunks(v), to_chunks(log_f)
    bc = jnp.cumsum(gc, axis=-2)
    lower = jnp.tril(jnp.ones((C, C), dtype=bool))[:, :, None]

    def step(S, inp):
        qt, kt, vt, bt = inp
        rel = bt[:, :, :, None, :] - bt[:, :, None, :, :]
        decay = jnp.where(lower, jnp.exp(jnp.where(lower, rel, 0.0)), 0.0)
        attn = jnp.einsum('nhtd,nhsd,nhtsd->nhts', qt, kt, decay)
        o = (jnp.einsum('nhts,nhsv->nhtv', attn, vt)
             + jnp.einsum('nhtd,nhdv->nhtv', qt * jnp.exp(bt), S))
        b_end = bt[:, :, -1:, :]
        S = (jnp.exp(b_end[:, :, 0, :])[..., None] * S
             + jnp.einsum('nhsd,nhsv->nhdv', kt * jnp.exp(b_end - bt), vt))
        return S, o

    S0 = jnp.zeros((n, H, DK, DV), jnp.float32)
    _, o = lax.scan(step, S0, (qc, kc, vc, bc))
    return o.transpose(1, 0, 3, 2, 4).reshape(n, L, H, DV)

def hgrn2_mixer(h, w_in, lower_bound, norm_g, w_out):
    B, L, _ = h.shape
    proj = (h @ w_in).astype(jnp.float32)
    q, i, z_fwd, z_bwd, gate = jnp.split(proj, 5, axis=-1)
    q = jax.nn.silu(q)
    z = jnp.stack([z_fwd, z_bwd], axis=0)
    lb = lower_bound.astype(jnp.float32)[:, None, None, :]
    log_f = jnp.log(lb + (1.0 - lb) * jax.nn.sigmoid(z))
    k = (1.0 - lb) * jax.nn.sigmoid(-z)
    q2 = jnp.concatenate([q, q[:, ::-1]], axis=0)
    v2 = jnp.concatenate([i, i[:, ::-1]], axis=0)
    k2 = jnp.concatenate([k[0], k[1][:, ::-1]], axis=0)
    g2 = jnp.concatenate([log_f[0], log_f[1][:, ::-1]], axis=0)
    heads = lambda a: a.reshape(2 * B, L, HG_HEADS, -1)
    o = gla_chunk_scan(heads(q2), heads(k2), heads(v2), heads(g2))
    o = o[:B] + o[B:, ::-1]
    o = o * lax.rsqrt(jnp.mean(o * o, axis=-1, keepdims=True) + NORM_EPS)
    o = o * norm_g.astype(jnp.float32) * jax.nn.silu(gate.reshape(B, L, HG_HEADS, HG_DV))
    return (o.reshape(B, L, D_MODEL) @ w_out.astype(jnp.float32)).astype(h.dtype)

def short_conv_centred(u, w, b):
    up = jnp.pad(u, ((0, 0), (1, 1), (0, 0)))
    return up[:, :-2] * w[0] + up[:, 1:-1] * w[1] + up[:, 2:] * w[2] + b

def hyena_filter(L, w_in, w_mid, b, freq, w_out):
    f32 = jnp.float32
    t = jnp.linspace(0.0, 1.0, L, dtype=f32)[:, None]
    bands = jnp.linspace(1e-4, HY_BANDS - 1.0, HY_BANDS, dtype=f32)
    ang = (2.0 * math.pi / L) * jnp.arange(L, dtype=f32)[:, None] * bands
    emb = jnp.concatenate([t, jnp.cos(ang), -jnp.sin(ang)], axis=-1)
    freq = freq.astype(f32)
    b = b.astype(f32)
    hdn = jnp.sin(freq * (emb @ w_in.astype(f32) + b[0]))
    for m in range(HY_FILTER_INNER):
        hdn = jnp.sin(freq * (hdn @ w_mid[m].astype(f32) + b[m + 1]))
    hf = (hdn @ w_out.astype(f32)).reshape(L, 2, D_MODEL)
    deltas = jnp.abs(jnp.linspace(HY_MIN_DECAY, HY_MAX_DECAY, D_MODEL, dtype=f32))
    hf = hf * jnp.exp(-t * deltas)[:, None, :]
    h_fwd, h_bwd = hf[:, 0], hf[:, 1]
    return jnp.concatenate([h_fwd, jnp.zeros((1, D_MODEL), f32), h_bwd[:0:-1]], axis=0)

def hyena_mixer(h, w_in, b_in, conv_w, conv_b, f_w_in, f_w_mid, f_b, f_freq, f_w_out, skip, w_out):
    B, L, _ = h.shape
    u = short_conv_centred(h @ w_in + b_in, conv_w, conv_b)
    x0, x1, v = jnp.split(u, 3, axis=-1)
    z = (x1 * v).astype(jnp.float32)
    filt = hyena_filter(L, f_w_in, f_w_mid, f_b, f_freq, f_w_out)
    zf = jnp.fft.rfft(z, n=2 * L, axis=1)
    hf = jnp.fft.rfft(filt, axis=0)
    y = jnp.fft.irfft(zf * hf[None], n=2 * L, axis=1)[:, :L]
    y = y + skip.astype(jnp.float32) * z
    y = (x0.astype(jnp.float32) * y).astype(h.dtype)
    return y @ w_out

def setup_inputs(seed: int = 0) -> dict:
    key = jax.random.key(seed)
    ks = jax.random.split(key, 24)
    D, NA, NB, W = D_MODEL, N_HGRN_LAYERS, N_HYENA_LAYERS, HY_FILTER_WIDTH
    nrm = lambda k, s: jax.random.normal(k, s, jnp.float32)
    return {
        "x": nrm(ks[0], (BATCH, SEQ, D)),
        "c": nrm(ks[1], (BATCH, D)),
        "ada_w": nrm(ks[2], (DEPTH, 2, D, 3 * D)) * (0.5 * D ** -0.5),
        "ada_b": nrm(ks[3], (DEPTH, 2, 3 * D)) * 0.02,
        "norm_g": 1.0 + 0.02 * nrm(ks[4], (DEPTH, 2, D)),
        "hg_w_in": nrm(ks[5], (NA, D, 5 * D)) * D ** -0.5,
        "hg_lower_bounds": nrm(ks[6], (2, NA, D)) * 0.1,
        "hg_norm_g": 1.0 + 0.02 * nrm(ks[7], (NA, HG_DV)),
        "hg_w_out": nrm(ks[8], (NA, D, D)) * D ** -0.5,
        "hy_w_in": nrm(ks[9], (NB, D, 3 * D)) * D ** -0.5,
        "hy_b_in": nrm(ks[10], (NB, 3 * D)) * 0.02,
        "hy_conv_w": nrm(ks[11], (NB, HY_SHORT_CONV, 3 * D)) * HY_SHORT_CONV ** -0.5,
        "hy_conv_b": nrm(ks[12], (NB, 3 * D)) * 0.02,
        "hy_filt_w_in": nrm(ks[13], (NB, HY_EMB_DIM, W)) * HY_EMB_DIM ** -0.5,
        "hy_filt_w_mid": nrm(ks[14], (NB, HY_FILTER_INNER, W, W)) * W ** -0.5,
        "hy_filt_b": nrm(ks[15], (NB, HY_FILTER_INNER + 1, W)) * 0.1,
        "hy_filt_freq": 1.0 + 0.1 * nrm(ks[16], (NB, W)),
        "hy_filt_w_out": nrm(ks[17], (NB, W, 2 * D)) * (0.05 * W ** -0.5),
        "hy_skip": nrm(ks[18], (NB, D)),
        "hy_w_out": nrm(ks[19], (NB, D, D)) * D ** -0.5,
        "mlp_w1": nrm(ks[20], (DEPTH, D, D_FF)) * D ** -0.5,
        "mlp_w2": nrm(ks[21], (DEPTH, D_FF, D)) * D_FF ** -0.5,
        "final_g": 1.0 + 0.02 * nrm(ks[22], (D,)),
    }

def reference(x, c, ada_w, ada_b, norm_g, hg_w_in, hg_lower_bounds, hg_norm_g, hg_w_out,
              hy_w_in, hy_b_in, hy_conv_w, hy_conv_b, hy_filt_w_in, hy_filt_w_mid, hy_filt_b,
              hy_filt_freq, hy_filt_w_out, hy_skip, hy_w_out, mlp_w1, mlp_w2, final_g):
    lbs = jax.nn.softmax(hg_lower_bounds.astype(jnp.float32), axis=1)
    lbs = jnp.cumsum(lbs, axis=1) - lbs[:, :1]
    for i in range(DEPTH):
        j = i // N_MIXERS
        shift, scale, gate = adaln_params(c, ada_w[i, 0], ada_b[i, 0])
        hn = rms_norm(x, norm_g[i, 0]) * (1.0 + scale) + shift
        if i % N_MIXERS == 0:
            mix = hgrn2_mixer(hn, hg_w_in[j], lbs[:, j], hg_norm_g[j], hg_w_out[j])
        else:
            mix = hyena_mixer(hn, hy_w_in[j], hy_b_in[j], hy_conv_w[j], hy_conv_b[j],
                              hy_filt_w_in[j], hy_filt_w_mid[j], hy_filt_b[j], hy_filt_freq[j],
                              hy_filt_w_out[j], hy_skip[j], hy_w_out[j])
        x = x + gate * mix
        shift, scale, gate = adaln_params(c, ada_w[i, 1], ada_b[i, 1])
        hn = rms_norm(x, norm_g[i, 1]) * (1.0 + scale) + shift
        x = x + gate * (jnp.square(jax.nn.relu(hn @ mlp_w1[i])) @ mlp_w2[i])
    return rms_norm(x, final_g)


_drawn_inputs = setup_inputs


def setup_inputs(seed=0):
    import zlib

    import numpy as np

    out = dict(_drawn_inputs(seed))
    spreads = {}
    factors = {'norm_g': 3.208,
     'hg_norm_g': 8.0,
     'hy_b_in': 5.838,
     'hy_conv_b': 5.377,
     'hy_filt_freq': 5.112,
     'final_g': 2.834}
    for name, (base, spread) in spreads.items():
        noise = np.random.default_rng([zlib.crc32(name.encode()), seed]).standard_normal(out[name].shape)
        drawn = base * np.exp(spread * noise) if base else spread * noise
        out[name] = __import__('jax').numpy.asarray(drawn.astype(out[name].dtype))
    for name, factor in factors.items():
        out[name] = (out[name] * factor).astype(out[name].dtype)
    return out
```

```python
import math
from contextlib import ExitStack

import numpy as np

import concourse.bass as bass
from concourse import mybir

F32 = mybir.dt.float32
F32R = mybir.dt.float32r
U8 = mybir.dt.uint8
ALU = mybir.AluOpType
ACT = mybir.ActivationFunctionType

P = 128
D = 1024
L = 512
KT = D // P
TT = L // P
HEADS = 8
D_FF = 4 * D
CHUNKS = D_FF // D
EPS = 1e-6
FW = 64
EMB = 33
BANDS = (EMB - 1) // 2
LEVELS = [1 << n for n in range(7)]
GROUPS = 4
GC = D // GROUPS
FT = L // 4 // P * 2
ADA_HALF = 3 * D // 2

S_HG_IN = 0
S_HG_OUT = S_HG_IN + 5 * HEADS
S_MLP0 = S_HG_OUT + KT
S_HY_IN = S_MLP0 + 16 * CHUNKS
S_HY_OUT = S_HY_IN + 6 * GROUPS
S_MLP1 = S_HY_OUT + KT
N_SLABS = S_MLP1 + 16 * CHUNKS
STAGE_SLOTS = 6

HY_ORDER = ((1, 0), (2, 0), (1, 1), (2, 1), (0, 0), (0, 1))

TOKEN_TILES = [0, 256, 1, 257]

A_C, A_ADA_B = 0, 8
B_NORM_G, B_FINAL_G, B_LOWER, B_HEAD_G = 0, 32, 40, 56
TWO_PI_HIGH = 6.28125
TWO_PI_LOW = 2.0 * math.pi - TWO_PI_HIGH
ROUNDER = 12582912.0


class At:

    def __init__(self, c, i=None, k=0):
        self.c, self.i, self.k = c, i, k

    def __add__(self, n):
        return At(self.c + n, self.i, self.k)

    def __mul__(self, n):
        return At(self.c * n, self.i, self.k * n)

    def half(self):
        assert self.k % 2 == 0
        return At(self.c // 2, self.i, self.k // 2)

    @property
    def odd(self):
        assert self.k % 2 == 0
        return self.c % 2

    @property
    def v(self):
        return self.c if self.i is None or self.k == 0 else self.i * self.k + self.c


def view(tile, offset, *dims):
    whole = tile[:]
    return bass.AP(tensor=whole.tensor, offset=offset, ap=[list(whole.ap[0])] + [list(d) for d in dims])


def transform_tables():
    p = np.arange(P)
    omega = np.pi * (2 * np.arange(256) + 1) / 1024
    forward = np.zeros((P, 4, 2, 256))
    for j, start in enumerate(TOKEN_TILES):
        phase = (start + 2 * p)[:, None] * omega[None]
        forward[:, j, 0], forward[:, j, 1] = np.cos(phase), np.sin(phase)
    inverse = np.zeros((P, 2, 2, 2, 256))
    for m in range(2):
        for parity in range(2):
            phase = omega[m * P + p][:, None] * (parity + 2 * np.arange(256))[None]
            inverse[:, m, 0, parity], inverse[:, m, 1, parity] = np.cos(phase) / 512, np.sin(phase) / 512
    return forward.astype(np.float32), inverse.astype(np.float32)


def filter_constants():
    f = np.float32
    t = np.linspace(0.0, 1.0, L, dtype=f)[:, None]
    bands = np.linspace(1e-4, BANDS - 1.0, BANDS, dtype=f)
    ang = f(2.0 * math.pi / L) * np.arange(L, dtype=f)[:, None] * bands
    emb = np.concatenate([t, np.cos(ang), -np.sin(ang)], axis=-1).astype(f)
    rates = np.abs(np.linspace(math.log(1e-2) / 1.5, math.log(1e-2) / 0.3, D, dtype=f))
    times = np.stack([-t[start + 2 * np.arange(P), 0] for start in TOKEN_TILES], axis=1)
    return np.ascontiguousarray(emb.T), rates, np.ascontiguousarray(times.astype(f))


def level_masks():
    s, t = np.arange(P)[:, None], np.arange(P)[None]
    return np.stack([((s // (2 * h)) == (t // (2 * h))) & ((s // h) != (t // h)) for h in LEVELS],
                    axis=1).astype(np.float32)


def hybrid_encoder(nc, x, c, ada_w, ada_b, norm_g, hg_w_in, hg_lower_bounds, hg_norm_g, hg_w_out,
                   hy_w_in, hy_b_in, hy_conv_w, hy_conv_b, hy_filt_w_in, hy_filt_w_mid, hy_filt_b,
                   hy_filt_freq, hy_filt_w_out, hy_skip, hy_w_out, mlp_w1, mlp_w2, final_g,
                   fwd_table, inv_table, emb_t, decay_rates, minus_times, masks, identity, out):
    spectrum = nc.dram_tensor("filter_spectrum", (GROUPS, P, 2, 4, GC), F32, kind="Internal").ap()

    with ExitStack() as ctx:
        def sb(name, shape, dt=F32, stack=ctx):
            return stack.enter_context(nc.sbuf_tensor(name, shape, dt))

        def sem(name):
            return ctx.enter_context(nc.semaphore(name))

        bank = [ctx.enter_context(nc.psum_tensor(f"bank{b}", [P, 512], F32)) for b in range(8)]

        xT = sb("xT", [P, KT, L])
        a_hi = sb("a_hi", [P, KT, L], F32R)
        a_lo = sb("a_lo", [P, KT, L], F32R)
        stage = sb("stage", [P, STAGE_SLOTS, KT, P])
        w_hi = sb("w_hi", [P, 2, KT, P], F32R)
        w_lo = sb("w_lo", [P, 2, KT, P], F32R)
        ident = sb("ident", [P, P])
        ones = sb("ones", [P, P])
        mean_d = sb("mean_d", [P, P])
        mean_head = sb("mean_head", [P, P])
        eps = sb("eps", [P, 1])
        p_a = sb("p_a", [P, 104])
        p_b = sb("p_b", [P, 57])
        p_c = sb("p_c", [P, 120])
        mod = sb("mod", [P, 4, 24])
        gain = sb("gain", [P, 4, 8])
        c_sig = sb("c_sig", [P, 8])
        c_silu = sb("c_silu", [P, 8])
        lb = sb("lb", [P, 16])
        one_m_lb = sb("one_m_lb", [P, 16])
        lb_tmp = sb("lb_tmp", [P, 4, 16])
        sum_sq = sb("sum_sq", [P, L])
        sq = sb("sq", [P, 2, L])
        std = sb("std", [P, L])
        rstd = sb("rstd", [P, L])
        tmp_a = sb("tmp_a", [P, 2, L])
        tmp_b = sb("tmp_b", [P, 2, L])

        with ExitStack() as st:
            x_nat = stage[:, 0:4].rearrange("p t k n -> p t (k n)")
            rows_a = sb("rows_a", [104, P], stack=st)
            rows_b = sb("rows_b", [57, P], stack=st)
            rows_c = sb("rows_c", [120, P], stack=st)
            rows_d = sb("rows_d", [4, FW], stack=st)
            p_d = sb("p_d", [FW, 4], stack=st)
            embT = sb("embT", [EMB, L], stack=st)
            f_w_in = sb("f_w_in", [EMB, FW], stack=st)
            f_w_mid = sb("f_w_mid", [FW, 2, FW], stack=st)
            f_w_out = sb("f_w_out", [FW, 2, D], stack=st)
            w_even = sb("w_even", [FW, D], stack=st)
            hidden, angle, turns = sum_sq[0:FW], tmp_b[0:FW], (std[0:FW], rstd[0:FW])
            rates = sq[:].rearrange("p a n -> p (a n)")
            minus_t = sb("minus_t", [P, 4], stack=st)
            skip_row = sb("skip_row", [1, D], stack=st)
            taps0 = tmp_b[0:1].rearrange("p a n -> p (a n)")
            decay = stage[:, 4:6].rearrange("p t k n -> p t (k n)")
            taps = sb("taps", [P, 2, 4, D], stack=st)
            tab_s = sb("tab_s", [P, 4, 2, 256], stack=st)
            even_s = tmp_a
            h_out = sb("h_out", [P, 4, L], stack=st)
            ada_w0 = sb("ada_w0", [P, 2, ADA_HALF], stack=st)
            ada_acc0 = sb("ada_acc0", [P, 2, ADA_HALF], stack=st)

        h_hi = sb("h_hi", [P, KT, L], F32R)
        h_lo = sb("h_lo", [P, KT, L], F32R)

        with ExitStack() as st:
            KK = [sb(f"KK{b}", [P, 2, L], stack=st) for b in range(2)]
            QQ = [sb(f"QQ{b}", [P, 2, L], stack=st) for b in range(2)]
            gates = sb("gates", [P, 3, L], stack=st)
            own = sb("own", [P, L], stack=st)
            values = [sb(f"values{b}", [P, TT, P], stack=st) for b in range(2)]
            out_gate = sb("out_gate", [P, L], stack=st)
            block_gates = {h: sb(f"block_gates{h}", [P, 3, L // h], stack=st) for h in LEVELS[1:] + [128]}
            scores = sb("scores", [P, TT, L], stack=st)
            q_sig, g_sig = sq[:, 0], sq[:, 1]
            q_silu = sb("q_silu", [P, L], stack=st)
            i_T = sb("i_T", [P, L], stack=st)
            f_pos = sb("f_pos", [P, L], stack=st)
            f_neg = sb("f_neg", [P, L], stack=st)
            mask = sb("mask", [P, len(LEVELS), P], U8, stack=st)
            ada_w1 = sb("ada_w1", [P, 1, ADA_HALF], stack=st)
            ada_acc1 = sb("ada_acc1", [P, ADA_HALF], stack=st)

        with ExitStack() as st:
            ada_w2 = sb("ada_w2", [P, 2, ADA_HALF], stack=st)
            ada_acc2 = sb("ada_acc2", [P, ADA_HALF], stack=st)

        with ExitStack() as st:
            tab_f = sb("tab_f", [P, 4, 2, 256], stack=st)
            tab_i = sb("tab_i", [P, 2, 2, 2, 256], stack=st)
            group_params = [sb(f"group_params{b}", [P, 5, 3, 2], stack=st) for b in range(2)]
            padded = [sb(f"padded{b}", [P, L + 2], stack=st) for b in range(3)]
            conv = [sb(f"conv{b}", [P, L], stack=st) for b in range(2)]
            z = [sb(f"z{b}", [P, L], stack=st) for b in range(2)]
            x0 = sb("x0", [P, 2, L], stack=st)
            z_t = [sb(f"z_t{b}", [P, 4, GC], stack=st) for b in range(2)]
            H = [sb(f"H{b}", [P, 4, GC], stack=st) for b in range(2)]
            ZH = sb("ZH", [P, 4, GC], stack=st)
            even_z = std[:].rearrange("p (a n) -> p a n", a=2)
            Z = tmp_a[:].rearrange("p b (a n) -> p (b a) n", a=2)
            Y = sq[:].rearrange("p b (a n) -> p (b a) n", a=2)
            folded = sb("folded", [P, 2, 2, 2, GC], stack=st)

        with ExitStack() as st:
            o_nat = sb("o_nat", [P, TT, D], stack=st)

        weight_landed = [sem(f"weight_landed{j}") for j in range(STAGE_SLOTS)]
        weight_cast, weight_split = sem("weight_cast"), sem("weight_split")
        slab_done = sem("slab_done")
        evicted = [sem("evicted_even"), sem("evicted_odd")]
        sq_ready, sum_ready, mean_ready, std_ready, rstd_ready = map(sem, (
            "sq_ready", "sum_ready", "mean_ready", "std_ready", "rstd_ready"))
        scaled_ready, full_ready, a_hi_ready, a_lo_ready = map(sem, (
            "scaled_ready", "full_ready", "a_hi_ready", "a_lo_ready"))
        relu_sq_ready, h_hi_ready, h_lo_ready = map(sem, ("relu_sq_ready", "h_hi_ready", "h_lo_ready"))
        ada_landed = [sem("ada_landed0"), sem("ada_landed1")]
        ada_summed, ada_columns, mod_ready, gain_ready = map(sem, (
            "ada_summed", "ada_columns", "mod_ready", "gain_ready"))
        consts_set, rows_landed, ident_landed, x_landed, filt_landed = map(sem, (
            "consts_set", "rows_landed", "ident_landed", "x_landed", "filt_landed"))
        rows_turned, params_ready, c_sig_ready, c_silu_ready = map(sem, (
            "rows_turned", "params_ready", "c_sig_ready", "c_silu_ready"))
        lb_step, lb_exp = sem("lb_step"), sem("lb_exp")
        x_turned, x_ready = sem("x_turned"), sem("x_ready")
        w_even_ready, pre_sine, angle_step, hidden_ready = map(sem, (
            "w_even_ready", "pre_sine", "angle_step", "hidden_ready"))
        taps_raw, decay_ready, taps_ready, tap0_step = map(sem, (
            "taps_raw", "decay_ready", "taps_ready", "tap0_step"))
        spec_parts, spec_even, spec_ready, spec_stored = map(sem, (
            "spec_parts", "spec_even", "spec_ready", "spec_stored"))
        q_sig_ready, q_ready, i_turned, values_ready = map(sem, (
            "q_sig_ready", "q_ready", "i_turned", "values_ready"))
        f_pos_ready, gate_ready, key_ready, query_ready, own_ready = map(sem, (
            "f_pos_ready", "gate_ready", "key_ready", "query_ready", "own_ready"))
        g_sig_ready, own_sum_ready = sem("g_sig_ready"), sem("own_sum_ready")
        level_scores, diag_scores, level_keys, level_queries, level_gates = map(sem, (
            "level_scores", "diag_scores", "level_keys", "level_queries", "level_gates"))
        far_scores, far_copied, mixed, mixed_sq, head_mean, head_std, head_rstd = map(sem, (
            "far_scores", "far_copied", "mixed", "mixed_sq", "head_mean", "head_std", "head_rstd"))
        normed_ready, gated_ready, o_hi_ready, o_lo_ready = map(sem, (
            "normed_ready", "gated_ready", "o_hi_ready", "o_lo_ready"))
        mask_landed, mask_set = sem("mask_landed"), sem("mask_set")
        tables_landed, H_landed0, H_landed1, pad_set, group_ready = map(sem, (
            "tables_landed", "H_landed0", "H_landed1", "pad_set", "group_ready"))
        conv_step, z_ready, z_turned, z_t_ready = map(sem, ("conv_step", "z_ready", "z_turned", "z_t_ready"))
        z_parts, z_even, Z_ready, ZH_ready, Y_ready, folded_ready = map(sem, (
            "z_parts", "z_even", "Z_ready", "ZH_ready", "Y_ready", "folded_ready"))
        y_ready, y_gated, y_hi_ready, y_lo_ready = map(sem, ("y_ready", "y_gated", "y_hi_ready", "y_lo_ready"))
        o_turned, o_copied, stored = map(sem, ("o_turned", "o_copied", "stored"))

        hg_in, hy_in = hg_w_in[0], hy_w_in[0]

        def columns(w, first):
            return w[:, first:first + P].rearrange("(k p) n -> p k n", p=P)

        block = ctx.enter_context(nc.Block())

        @block.sync
        def _(sp):
            for dst, src in (
                (rows_a[A_C:A_C + 8], c.rearrange("a (n p) -> (a n) p", p=P)),
                (rows_a[A_ADA_B:104], ada_b.rearrange("i s (n p) -> (i s n) p", p=P)),
                (rows_b[B_NORM_G:32], norm_g.rearrange("i s (n p) -> (i s n) p", p=P)),
                (rows_b[B_FINAL_G:40], final_g.rearrange("(n p) -> n p", p=P)),
                (rows_b[B_LOWER:56], hg_lower_bounds.rearrange("i s (n p) -> (i s n) p", p=P)),
                (rows_b[B_HEAD_G:57], hg_norm_g),
                (rows_c[0:72], hy_conv_w.rearrange("i s (n p) -> (i s n) p", p=P)),
                (rows_c[72:96], hy_b_in.rearrange("i (n p) -> (i n) p", p=P)),
                (rows_c[96:120], hy_conv_b.rearrange("i (n p) -> (i n) p", p=P)),
                (rows_d[0:3], hy_filt_b[0]),
                (rows_d[3:4], hy_filt_freq),
            ):
                sp.dma_start(dst, src).then_inc(rows_landed, 16)
            sp.dma_start(ident[:], identity).then_inc(ident_landed, 16)
            for dst, src in (
                (embT[:], emb_t), (f_w_in[:], hy_filt_w_in[0]),
                (f_w_mid[:], hy_filt_w_mid[0].rearrange("m a b -> a m b")),
                (f_w_out[:], hy_filt_w_out[0].rearrange("w (s d) -> w s d", s=2)),
                (rates, decay_rates.partition_broadcast(P)), (minus_t[:], minus_times),
                (skip_row[:], hy_skip), (tab_s[:], fwd_table),
            ):
                sp.dma_start(dst, src).then_inc(filt_landed, 16)

            def load_ada(m, piece, buffer):
                q = 16 * m + piece
                half, k = piece // 8, piece % 8
                slots = buffer[:].shape[1]
                if q >= slots:
                    sp.wait_ge(ada_summed, q - slots + 1)
                src = ada_w[m // 2, m % 2, k * P:(k + 1) * P, half * ADA_HALF:(half + 1) * ADA_HALF]
                sp.dma_start(buffer[:, piece % slots], src).then_inc(ada_landed[q % 2], 16)

            def load_slab(s, slot, src, wait=None):
                if wait is not None:
                    sp.wait_ge(weight_split, wait)
                sp.dma_start(stage[:, slot], src).then_inc(weight_landed[slot], 16)

            for piece in range(4):
                load_ada(0, piece, ada_w0)
            sp.dma_start(x_nat, x[0].rearrange("(t p) d -> p t d", p=P)).then_inc(x_landed, 16)
            for piece in range(4, 16):
                load_ada(0, piece, ada_w0)

            sp.wait_ge(x_turned, KT)
            sp.wait_ge(taps_ready, 16)
            for j in range(5):
                load_slab(j, j, columns(hg_in, j * D))
            sp.wait_ge(spec_stored, 16 * 8)
            sp.wait_ge(gain_ready, 1)
            sp.dma_start(scores[:, 0:2].rearrange("p a n -> p (a n)")[:, 0:len(LEVELS) * P],
                         masks.rearrange("p l n -> p (l n)")).then_inc(mask_landed, 16)

            for h in range(1, HEADS):
                for j in range(5):
                    s = 5 * h + j
                    load_slab(s, j, columns(hg_in, j * D + h * P), s - 4)
                for piece in (2 * h - 2, 2 * h - 1):
                    load_ada(1, piece, ada_w1)
            for piece in (14, 15):
                load_ada(1, piece, ada_w1)
            for n in range(KT):
                s = S_HG_OUT + n
                load_slab(s, n % 4, columns(hg_w_out[0], n * P), s - 3)

            def mlp(i, s0, with_ada):
                for ch in range(CHUNKS):
                    for n in range(16):
                        s = s0 + 16 * ch + n
                        q = 16 * ch + n
                        if with_ada and q % 2 == 0:
                            load_ada(2 + q // 32, q // 2 % 16, ada_w2)
                        if n < 8:
                            src = columns(mlp_w1[i], ch * D + n * P)
                        else:
                            src = columns(mlp_w2[i, ch * D:(ch + 1) * D], (n - 8) * P)
                        load_slab(s, n % 4, src, s - 3)

            sp.wait_ge(o_lo_ready, HEADS)
            sp.wait_ge(ada_columns, 4)
            mlp(0, S_MLP0, True)

            for g in range(GROUPS):
                for j, (seg, n) in enumerate(HY_ORDER):
                    s = S_HY_IN + 6 * g + j
                    wait = s - 5 if g else (s - 3 if j < 4 else s - 5)
                    load_slab(s, j, columns(hy_in, seg * D + g * GC + n * P), wait)
                if g == 0:
                    sp.wait_ge(gain_ready, 4)
                    sp.dma_start(tab_f[:], fwd_table).then_inc(tables_landed, 16)
                    sp.dma_start(tab_i[:], inv_table).then_inc(tables_landed, 16)
                for h in ((), (0,), (1,), (2, 3))[g]:
                    for m in range(2):
                        if h:
                            sp.wait_ge(ZH_ready, 4 * (h - 1) + 2 * m + 2)
                        sp.dma_start(H[m][:], spectrum[h, :, m]).then_inc((H_landed0, H_landed1)[m], 16)
            for n in range(KT):
                s = S_HY_OUT + n
                load_slab(s, n % 4, columns(hy_w_out[0], n * P), s - 3)
            mlp(1, S_MLP1, False)

            for half in range(2):
                sp.wait_ge(o_copied, 4 * (half + 1))
                cols = slice(half * 512, half * 512 + 512)
                sp.dma_start(out[0].rearrange("(t p) d -> p t d", p=P)[:, :, cols],
                             o_nat[:, :, cols]).then_inc(stored, 16)
            sp.wait_ge(stored, 32)

        @block.gpsimd
        def _(pool):
            def split_slab(s, slot, landed):
                side = s % 2
                pool.wait_ge(weight_landed[slot], 16 * landed)
                if s >= 2:
                    pool.wait_ge(slab_done, s - 1)
                nc.gpsimd.tensor_scalar(w_hi[:, side], stage[:, slot], 1.0, 0.0, ALU.mult,
                                        ALU.add).then_inc(weight_cast, 1)
                pool.wait_ge(weight_cast, s + 1)
                nc.gpsimd.tensor_tensor(w_lo[:, side], stage[:, slot], w_hi[:, side].bitcast(F32),
                                        ALU.subtract).then_inc(weight_split, 1)

            loads = [0] * STAGE_SLOTS
            for s in range(N_SLABS):
                if s < S_HG_OUT:
                    slot = s % 5
                elif S_HY_IN <= s < S_HY_OUT:
                    slot = (s - S_HY_IN) % 6
                else:
                    slot = s % 4
                loads[slot] += 1
                split_slab(s, slot, loads[slot])

        @block.tensor
        def _(pe):
            def product(dst, pairs, after=None):
                for n, (lhs, rhs) in enumerate(pairs):
                    ins = pe.matmul(dst, lhs, rhs, start=n == 0, stop=n == len(pairs) - 1)
                return ins

            def slab(s, hi, lo, ready=None, between=()):
                side = s % 2
                pe.wait_ge(weight_split, s + 1)
                if s >= 2:
                    pe.wait_ge(evicted[side], s // 2)
                acc = bank[side][:]
                for k in range(KT):
                    if ready is not None:
                        pe.wait_ge(ready[0], ready[1] + k + 1)
                        pe.wait_ge(ready[2], ready[1] + k + 1)
                    pe.matmul(acc, w_hi[:, side, k], hi[:, k], start=k == 0, stop=False)
                    pe.matmul(acc, w_lo[:, side, k], hi[:, k], start=False, stop=False)
                    ins = pe.matmul(acc, w_hi[:, side, k], lo[:, k], start=False, stop=k == KT - 1)
                    if k == KT - 1:
                        ins.then_inc(slab_done, 1)
                    for work in between.get(k, ()) if between else ():
                        work()

            def ada_column(m, half, acc):
                pe.wait_ge(ada_summed, 16 * m + 8 * half + 8)
                if m or half:
                    pe.wait_ge(mod_ready, 2 * m + half)
                for n in range(12):
                    ins = pe.matmul(bank[6][:, 24 * m + 12 * half + n:24 * m + 12 * half + n + 1],
                                    acc[:, n * P:(n + 1) * P], ones[:, 0:1],
                                    start=True, stop=True)
                ins.then_inc(ada_columns, 1)

            def norm_mean(m):
                pe.wait_ge(sum_ready, 8 * (m + 1))
                if m == 1:
                    pe.wait_ge(head_std, HEADS)
                pe.matmul(bank[7][:], mean_d[:], sum_sq[:], start=True, stop=True).then_inc(mean_ready, 1)

            pe.wait_ge(ident_landed, 16)
            pe.wait_ge(rows_landed, 16 * 11)
            pe.wait_ge(consts_set, 5)
            for n, rows in enumerate((rows_a, rows_b, rows_c, rows_d)):
                r, w = rows[:].shape
                pe.transpose(bank[2 + n][0:w, 0:r], rows[:], ident[0:r, 0:r]).then_inc(rows_turned, 1)
            pe.wait_ge(filt_landed, 16 * 8)
            pe.wait_ge(params_ready, 4)
            pe.matmul(bank[4][0:FW], f_w_in[:], embT[:], start=True, stop=True).then_inc(pre_sine, 1)
            def turn_x(k):
                if k == 0:
                    pe.wait_ge(x_landed, 16)
                if k >= 2:
                    pe.wait_ge(x_ready, k - 1)
                for t in range(TT):
                    ins = pe.transpose(bank[2 + k % 2][:, t * P:(t + 1) * P], x_nat[:, t, k * P:(k + 1) * P],
                                       ident[:])
                ins.then_inc(x_turned, 1)

            for m in range(2):
                pe.wait_ge(hidden_ready, m + 1)
                pe.matmul(bank[4][0:FW], f_w_mid[:, m], hidden, start=True, stop=True).then_inc(pre_sine, 1)
                for k in range(4 * m, 4 * m + 4):
                    turn_x(k)
            pe.wait_ge(hidden_ready, 3)
            pe.wait_ge(w_even_ready, 2)
            n = 0
            for j, start in enumerate(TOKEN_TILES):
                for part in range(2):
                    for half in range(2):
                        if n >= 2:
                            pe.wait_ge(taps_ready, n - 1)
                        pe.matmul(bank[4 + n % 2][:], hidden[:, start:start + 255:2],
                                  (w_even[:] if part == 0 else f_w_out[:, 1])[:, half * 512:half * 512 + 512],
                                  start=True, stop=True).then_inc(taps_raw, 1)
                        n += 1
            pe.wait_ge(x_ready, 8)
            pe.wait_ge(taps_ready, 16)
            pe.wait_ge(tap0_step, 2)
            n = 0
            for half in range(2):
                for m in range(2):
                    if n:
                        pe.wait_ge(spec_ready, 4 * n)
                    for part in range(2):
                        for odd in range(2):
                            ins = product(bank[2 + 2 * part + odd][:], [
                                (tab_s[:, 2 * odd + j, part, m * P:(m + 1) * P],
                                 taps[:, part, 2 * odd + j, half * 512:half * 512 + 512]) for j in range(2)])
                            ins.then_inc(spec_parts, 1)
                    n += 1
            ada_column(0, 0, ada_acc0[:, 0])
            ada_column(0, 1, ada_acc0[:, 1])
            norm_mean(0)
            pe.wait_ge(spec_ready, 16)

            def turn_values(h):
                pe.wait_ge(evicted[(5 * h + 1) % 2], (5 * h + 1) // 2 + 1)
                if h >= 2:
                    pe.wait_ge(far_copied, 3 * h - 5)
                for t in range(TT):
                    ins = pe.transpose(bank[4][:, t * P:(t + 1) * P], i_T[:, t * P:(t + 1) * P], ident[:])
                ins.then_inc(i_turned, 1)

            def own_scores(h):
                pe.wait_ge(own_ready, h + 1)
                if h:
                    pe.wait_ge(far_copied, 3 * h)
                for t in range(TT):
                    ins = pe.matmul(bank[2][:, t * P:(t + 1) * P], own[:, t * P:(t + 1) * P], ones[:],
                                    start=True, stop=True)
                ins.then_inc(level_scores, 1)

            def level(h, n):
                width = LEVELS[n]
                if n == 0:
                    pe.wait_ge(query_ready, 2 * h + 2)
                    pe.wait_ge(key_ready, 2 * h + 2)
                else:
                    pe.wait_ge(level_keys, 8 * h + n)
                    pe.wait_ge(level_queries, 8 * h + n)
                    pe.wait_ge(diag_scores, 8 * h + n)
                halves = ([2 * width, 64 // width], [1, width])
                for t in range(TT):
                    for back in range(2):
                        at = t * P + (0 if back else width)
                        ins = pe.matmul(view(bank[3 - n % 2], at, *halves), KK[h % 2][:, back, t * P:(t + 1) * P],
                                        view(QQ[h % 2], (1 - back) * L + at, *halves), start=True, stop=True)
                ins.then_inc(level_scores, 1)

            def far_128(h):
                pe.wait_ge(level_keys, 8 * h + 7)
                pe.wait_ge(level_queries, 8 * h + 7)
                pe.wait_ge(values_ready, h + 2 if h + 1 < HEADS else HEADS)
                for n, (s, t, back) in enumerate(((0, 1, 0), (1, 0, 1), (2, 3, 0), (3, 2, 1))):
                    ins = pe.matmul(bank[4][:, n * P:(n + 1) * P], KK[h % 2][:, back, s * P:(s + 1) * P],
                                    QQ[h % 2][:, 1 - back, t * P:(t + 1) * P], start=True, stop=True)
                ins.then_inc(far_scores, 1)

            def far_256(h):
                pe.wait_ge(level_keys, 8 * h + 8)
                pe.wait_ge(level_queries, 8 * h + 8)
                pe.wait_ge(diag_scores, 8 * h + 8)
                for n in range(4):
                    back = n // 2
                    ins = pe.matmul(bank[2 + back][:, n % 2 * 256:n % 2 * 256 + 256],
                                    KK[h % 2][:, back, n * P:(n + 1) * P],
                                    QQ[h % 2][:, 1 - back, (1 - back) * 256:(1 - back) * 256 + 256],
                                    start=True, stop=True)
                    if n % 2:
                        ins.then_inc(far_scores, 1)

            def mix(h):
                pe.wait_ge(far_copied, 3 * h + 3)
                pe.wait_ge(diag_scores, 8 * h + 8)
                if h:
                    pe.wait_ge(normed_ready, h)
                product(bank[5][:], [(values[h % 2][:, t], scores[:, t]) for t in range(TT)]).then_inc(mixed, 1)

            def head_square(h):
                pe.wait_ge(mixed_sq, h + 1)
                if h:
                    pe.wait_ge(head_std, h)
                pe.matmul(bank[7][:], mean_head[:], std[:], start=True, stop=True).then_inc(head_mean, 1)

            for g in range(HEADS + 1):
                h = g - 1
                works = []
                if h >= 0:
                    works = [lambda: own_scores(h)] + [lambda n=n: level(h, n) for n in range(7)] + [
                        lambda: far_128(h), lambda: far_256(h), lambda: mix(h), lambda: head_square(h)]
                places = {3 * n + 2 + (1 if n > 7 else 0): w for n, w in enumerate(works)}
                if g == HEADS:
                    for w in works:
                        w()
                    continue
                for j in range(5):
                    between = {}
                    if (g, j) == (5, 0):
                        places[4] = lambda: ada_column(1, 0, ada_acc1)
                    for k in range(KT):
                        here = [places[8 * j + k]] if 8 * j + k in places else []
                        if 8 * j + k == 19:
                            here = [lambda: turn_values(g)] + here
                        between[k] = here
                    ready = (a_hi_ready, 0, a_lo_ready) if (g, j) == (0, 0) else None
                    slab(5 * g + j, a_hi, a_lo, ready, between)
            for n in range(KT):
                slab(S_HG_OUT + n, h_hi, h_lo, (o_hi_ready, 0, o_lo_ready) if n == 0 else None)
                if n == 3:
                    ada_column(1, 1, ada_acc1)
            norm_mean(1)

            def mlp(i, s0, with_ada):
                for ch in range(CHUNKS):
                    for n in range(8):
                        slab(s0 + 16 * ch + n, a_hi, a_lo,
                             (a_hi_ready, 8 * (2 * i + 1), a_lo_ready) if ch == n == 0 else None)
                        if with_ada and ch and n == 0:
                            ada_column(2 + (ch - 1) // 2, (ch - 1) % 2, ada_acc2)
                    for n in range(8):
                        slab(s0 + 16 * ch + 8 + n, h_hi, h_lo,
                             (h_hi_ready, 8 * (CHUNKS * i + ch), h_lo_ready) if n == 0 else None)
                if with_ada:
                    ada_column(3, 1, ada_acc2)
                norm_mean(2 * i + 2)

            mlp(0, S_MLP0, True)

            def turn_z(g, n):
                pe.wait_ge(z_ready, 2 * g + n + 1)
                if g or n:
                    pe.wait_ge(z_t_ready, 2 * g + n)
                for j, start in enumerate(TOKEN_TILES):
                    ins = pe.transpose(bank[4][:, j * P:(j + 1) * P], z[n][:, start:start + 255:2], ident[:])
                ins.then_inc(z_turned, 1)

            def forward(g, m):
                if m == 0:
                    pe.wait_ge(z_t_ready, 2 * g + 2)
                if g == m == 0:
                    pe.wait_ge(tables_landed, 32)
                if g or m:
                    pe.wait_ge(z_even, 2 * g + m)
                    pe.wait_ge(Z_ready, 2 * (2 * g + m))
                for odd in range(2):
                    for part in range(2):
                        ins = product(bank[2 + odd][:, part * GC:(part + 1) * GC], [
                            (tab_f[:, 2 * odd + j, part, m * P:(m + 1) * P], z_t[g % 2][:, 2 * odd + j])
                            for j in range(2)])
                    ins.then_inc(z_parts, 1)

            def inverse(g, n):
                pe.wait_ge(folded_ready, 4 * g + 4)
                if g == 0 and n == 1:
                    pe.wait_ge(mod_ready, 8)
                if g:
                    pe.wait_ge(y_gated, 2 * g - 1 + n)
                for parity in range(2):
                    ins = product(bank[5 + n][:, parity * 256:parity * 256 + 256], [
                        (folded[:, m, parity, part, n * P:(n + 1) * P], tab_i[:, m, part, parity])
                        for m in range(2) for part in range(2)])
                ins.then_inc(y_ready, 1)

            for g in range(GROUPS + 1):
                h = g - 1
                if g < GROUPS:
                    places = {10: lambda: None}
                    if h >= 0:
                        places = {2: lambda: forward(h, 0), 12: lambda: forward(h, 1),
                                  30: lambda: inverse(h, 0), 33: lambda: inverse(h, 1)}
                    places[26] = lambda: turn_z(g, 0)
                    places[43] = lambda: turn_z(g, 1)
                    for j in range(6):
                        between = {k: [places[8 * j + k]] for k in range(KT) if 8 * j + k in places}
                        slab(S_HY_IN + 6 * g + j, a_hi, a_lo,
                             (a_hi_ready, 16, a_lo_ready) if (g, j) == (0, 0) else None, between)
                else:
                    forward(h, 0)
                    forward(h, 1)
                    inverse(h, 0)
                    inverse(h, 1)
            for n in range(KT):
                slab(S_HY_OUT + n, h_hi, h_lo, (y_hi_ready, 0, y_lo_ready) if n == 0 else None)
            norm_mean(3)
            mlp(1, S_MLP1, False)

            for k in range(KT):
                pe.wait_ge(full_ready, 32 + k + 1)
                if k >= 2:
                    pe.wait_ge(o_copied, k - 1)
                for t in range(TT):
                    ins = pe.transpose(bank[2 + k % 2][:, t * P:(t + 1) * P], tmp_b[:, k % 2, t * P:(t + 1) * P],
                                       ident[:])
                ins.then_inc(o_turned, 1)

        @block.scalar
        def _(act):
            def run(out_, in_, func, **kw):
                return nc.scalar.activation(out_, in_, func, **kw)

            def square_x(m, k):
                j = 8 * m + k
                if j >= 2:
                    act.wait_ge(sum_ready, j - 1)
                run(sq[:, k % 2], xT[:, k], ACT.Square).then_inc(sq_ready, 1)

            def norm_std(m):
                act.wait_ge(mean_ready, m + 1)
                run(std[:], bank[7][:], ACT.Sqrt, bias=eps[:, 0:1]).then_inc(std_ready, 1)

            def norm_apply(m):
                for k in range(KT):
                    j = 8 * m + k
                    act.wait_ge(scaled_ready, j + 1)
                    run(a_hi[:, k], tmp_a[:, k % 2], ACT.Identity, bias=mod[:, m, k:k + 1]).then_inc(a_hi_ready, 1)
                    if j >= 2:
                        act.wait_ge(a_lo_ready, j - 1)
                    run(tmp_b[:, k % 2], tmp_a[:, k % 2], ACT.Identity,
                        bias=mod[:, m, k:k + 1]).then_inc(full_ready, 1)

            def evict_wait(s):
                act.wait_ge(slab_done, s + 1)

            act.wait_ge(params_ready, 1)
            run(c_sig[:], p_a[:, A_C:A_C + 8], ACT.Sigmoid).then_inc(c_sig_ready, 1)
            act.wait_ge(lb_step, 1)
            run(lb_tmp[:, 1], lb_tmp[:, 0], ACT.Exp).then_inc(lb_exp, 1)

            def sine(layer):
                act.wait_ge(angle_step, 6 * layer + 6)
                run(hidden, angle[:, 1], ACT.Sin).then_inc(hidden_ready, 1)

            def take_x(k):
                act.wait_ge(x_turned, k + 1)
                nc.scalar.copy(xT[:, k], bank[2 + k % 2][:]).then_inc(x_ready, 1)

            sine(0)
            for k in range(4):
                take_x(k)
            sine(1)
            for k in range(4, 8):
                take_x(k)
            sine(2)
            for j in range(4):
                if j >= 2:
                    act.wait_ge(taps_ready, 4 * (j - 1))
                run(decay[:, j % 2], rates, ACT.Exp, scale=minus_t[:, j:j + 1]).then_inc(decay_ready, 1)
            for k in range(KT):
                if k == 0:
                    act.wait_ge(x_ready, 8)
                    act.wait_ge(decay_ready, 4)
                square_x(0, k)
            for n in range(8):
                act.wait_ge(spec_parts, 4 * (n // 2) + 2 * (n % 2) + 1)
                if n >= 2:
                    act.wait_ge(spec_ready, 2 * (n - 1))
                nc.scalar.copy(even_s[:, n % 2], bank[2 + 2 * (n % 2)][:]).then_inc(spec_even, 1)
                if n % 2:
                    half, m = n // 4, n // 2 % 2
                    act.wait_ge(spec_ready, 2 * (n + 1))
                    for gg in range(2):
                        act.dma_start(spectrum[2 * half + gg, :, m],
                                      h_out[:, :, gg * GC:(gg + 1) * GC]).then_inc(spec_stored, 16)
            norm_std(0)
            act.wait_ge(gain_ready, 1)
            norm_apply(0)

            def head_inputs(g):
                s = 5 * g
                b = g % 2
                evict_wait(s)
                if g:
                    act.wait_ge(evicted[(s - 5) % 2], (s - 5) // 2 + 1)
                else:
                    act.wait_ge(spec_stored, 16 * 8)
                run(q_sig, bank[s % 2][:], ACT.Sigmoid).then_inc(q_sig_ready, 1)
                evict_wait(s + 1)
                if g:
                    act.wait_ge(i_turned, g)
                nc.scalar.copy(i_T[:], bank[(s + 1) % 2][:]).then_inc(evicted[(s + 1) % 2], 1)
                for way in range(2):
                    evict_wait(s + 2 + way)
                    n = 2 * g + way
                    if n:
                        act.wait_ge(gate_ready, 3 * g + (1 if way else 0))
                        act.wait_ge(key_ready, n)
                    run(f_pos[:], bank[(s + 2 + way) % 2][:], ACT.Sigmoid).then_inc(f_pos_ready, 1)
                    run(f_neg[:], bank[(s + 2 + way) % 2][:], ACT.Sigmoid,
                        scale=-1.0).then_inc(evicted[(s + 2 + way) % 2], 1)
                    if way == 0:
                        act.wait_ge(i_turned, g + 1)
                        if g >= 2:
                            act.wait_ge(mixed, g - 1)
                        nc.scalar.copy(values[b][:], bank[4][:].rearrange("p (t n) -> p t n", t=TT)).then_inc(
                            values_ready, 1)

            def head_gate(g):
                s = 5 * g
                evict_wait(s + 4)
                if g:
                    act.wait_ge(evicted[(s - 1) % 2], (s - 1) // 2 + 1)
                run(g_sig, bank[(s + 4) % 2][:], ACT.Sigmoid).then_inc(g_sig_ready, 1)

            def head_far(h):
                act.wait_ge(far_scores, 3 * h + 1)
                if h:
                    act.wait_ge(mixed, h)
                nc.scalar.copy(view(scores, P, [2 * L + 256, 2], [L - P, 2], [1, P]),
                               bank[4][:].rearrange("p (a b n) -> p a b n", a=2, b=2)).then_inc(far_copied, 1)
                for back in range(2):
                    act.wait_ge(far_scores, 3 * h + 2 + back)
                    nc.scalar.copy(view(scores, 256 if back == 0 else 2 * L, [L, 2], [1, 256]),
                                   bank[2 + back][:].rearrange("p (a n) -> p a n", a=2)).then_inc(far_copied, 1)

            def head_norm(h):
                act.wait_ge(mixed, h + 1)
                if h:
                    act.wait_ge(head_mean, h)
                run(std[:], bank[5][:], ACT.Square).then_inc(mixed_sq, 1)
                act.wait_ge(head_mean, h + 1)
                if h:
                    act.wait_ge(head_rstd, h)
                run(sum_sq[:], bank[7][:], ACT.Sqrt, bias=eps[:, 0:1]).then_inc(head_std, 1)

            def head_split(h):
                act.wait_ge(gated_ready, h + 1)
                nc.scalar.copy(h_hi[:, h], tmp_b[:, h % 2]).then_inc(o_hi_ready, 1)

            for g in range(HEADS + 1):
                if g < HEADS:
                    head_inputs(g)
                if g:
                    head_far(g - 1)
                    head_norm(g - 1)
                    head_split(g - 1)
                if g < HEADS:
                    head_gate(g)

            def norm(m, s0):
                for n in range(KT):
                    s = s0 + n
                    act.wait_ge(evicted[s % 2], s // 2 + 1)
                    square_x(m, n)
                norm_std(m)
                if m < 4:
                    act.wait_ge(gain_ready, m + 1)
                    norm_apply(m)

            norm(1, S_HG_OUT)

            def mlp(i, s0):
                for ch in range(CHUNKS):
                    for n in range(8):
                        s, j = s0 + 16 * ch + n, 8 * (CHUNKS * i + ch) + n
                        evict_wait(s)
                        if n >= 2:
                            act.wait_ge(h_hi_ready, j - 1)
                        run(tmp_a[:, n % 2], bank[s % 2][:], ACT.Relu).then_inc(evicted[s % 2], 1)
                        act.wait_ge(evicted[s % 2], s // 2 + 1)
                        if n >= 2:
                            act.wait_ge(h_lo_ready, j - 1)
                        run(tmp_b[:, n % 2], tmp_a[:, n % 2], ACT.Square).then_inc(relu_sq_ready, 1)
                norm(2 * i + 2, s0 + 16 * CHUNKS - 8)

            mlp(0, S_MLP0)

            def take_z(g, n):
                act.wait_ge(z_turned, 2 * g + n + 1)
                if g >= 2:
                    act.wait_ge(z_parts, 4 * (g - 1))
                nc.scalar.copy(z_t[g % 2][:, :, n * P:(n + 1) * P],
                               bank[4][:].rearrange("p (j n) -> p j n", j=4)).then_inc(z_t_ready, 1)

            def even_part(h, m):
                act.wait_ge(z_parts, 2 * (2 * h + m) + 1)
                if h or m:
                    act.wait_ge(Z_ready, 2 * (2 * h + m))
                nc.scalar.copy(even_z, bank[2][:].rearrange("p (a n) -> p a n", a=2)).then_inc(z_even, 1)

            def y_high(h, n):
                act.wait_ge(y_gated, 2 * h + n + 1)
                nc.scalar.copy(h_hi[:, 2 * h + n], tmp_b[:, n]).then_inc(y_hi_ready, 1)

            act.wait_ge(pad_set, 3)
            for g in range(GROUPS + 1):
                for j in range(6 if g < GROUPS else 0):
                    s = S_HY_IN + 6 * g + j
                    seg, n = HY_ORDER[j]
                    evict_wait(s)
                    act.wait_ge(group_ready, g + 1)
                    prior = 6 * g + (-4, -4, 0, 1, -1, 4)[j]
                    if prior >= 0:
                        act.wait_ge(conv_step, 3 * (prior + 1))
                    run(padded[seg][:, 1:L + 1], bank[s % 2][:], ACT.Identity,
                        bias=group_params[g % 2][:, 3, seg, n:n + 1]).then_inc(evicted[s % 2], 1)
                    if g and j == 0:
                        even_part(g - 1, 0)
                    if g and j == 2:
                        even_part(g - 1, 1)
                    if j == 3:
                        take_z(g, 0)
                    if g and j == 5:
                        y_high(g - 1, 0)
                        y_high(g - 1, 1)
                    if j == 5:
                        take_z(g, 1)
                if g == GROUPS:
                    even_part(g - 1, 0)
                    even_part(g - 1, 1)
                    y_high(g - 1, 0)
                    y_high(g - 1, 1)
            norm(3, S_HY_OUT)
            mlp(1, S_MLP1)
            for k in range(KT):
                act.wait_ge(o_turned, k + 1)
                nc.scalar.copy(o_nat[:, :, k * P:(k + 1) * P],
                               bank[2 + k % 2][:].rearrange("p (t n) -> p t n", t=TT)).then_inc(o_copied, 1)

        @block.vector
        def _(dve):
            tt, ts, stt = nc.vector.tensor_tensor, nc.vector.tensor_scalar, nc.vector.scalar_tensor_tensor

            def ada_piece(m, piece, buffer, acc):
                half, k = piece // 8, piece % 8
                q = 16 * m + piece
                dve.wait_ge(ada_landed[q % 2], 16 * (q // 2 + 1))
                if q:
                    dve.wait_ge(ada_summed, q)
                if k == 0 and (m == 3 or m and half):
                    dve.wait_ge(ada_columns, 2 * m + half)
                w = buffer[:, piece % buffer[:].shape[1]]
                if k == 0:
                    ins = ts(acc[:], w, c_silu[:, 0:1], None, ALU.mult)
                else:
                    ins = stt(out=acc[:], in0=w, scalar=c_silu[:, k:k + 1], in1=acc[:], op0=ALU.mult, op1=ALU.add)
                ins.then_inc(ada_summed, 1)

            def take_mod(m, half):
                dve.wait_ge(ada_columns, 2 * m + half + 1)
                b0 = A_ADA_B + 24 * m + 12 * half
                tt(mod[:, m, 12 * half:12 * half + 12], bank[6][:, 24 * m + 12 * half:24 * m + 12 * half + 12], p_a[:, b0:b0 + 12],
                   ALU.add).then_inc(mod_ready, 1)
                if half:
                    dve.wait_ge(mod_ready, 2 * m + 2)
                    stt(out=gain[:, m], in0=mod[:, m, 8:16], scalar=1.0,
                        in1=p_b[:, B_NORM_G + 8 * m:B_NORM_G + 8 * m + 8], op0=ALU.add,
                        op1=ALU.mult).then_inc(gain_ready, 1)

            def add_square(m, k):
                dve.wait_ge(sq_ready, 8 * m + k + 1)
                if k == 0:
                    ins = nc.vector.tensor_copy(sum_sq[:], sq[:, 0])
                else:
                    dve.wait_ge(sum_ready, 8 * m + k)
                    ins = tt(sum_sq[:], sum_sq[:], sq[:, k % 2], ALU.add)
                ins.then_inc(sum_ready, 1)

            def norm_rstd(m):
                dve.wait_ge(std_ready, m + 1)
                nc.vector.reciprocal(rstd[:], std[:]).then_inc(rstd_ready, 1)
                dve.wait_ge(rstd_ready, m + 1)

            def norm_apply(m):
                def scale(k):
                    if k >= 2:
                        dve.wait_ge(full_ready, 8 * m + k - 1)
                    stt(out=tmp_a[:, k % 2], in0=xT[:, k], scalar=gain[:, m, k:k + 1], in1=rstd[:],
                        op0=ALU.mult, op1=ALU.mult).then_inc(scaled_ready, 1)

                def low(k):
                    dve.wait_ge(full_ready, 8 * m + k + 1)
                    dve.wait_ge(a_hi_ready, 8 * m + k + 1)
                    tt(a_lo[:, k], tmp_b[:, k % 2], a_hi[:, k].bitcast(F32), ALU.subtract).then_inc(a_lo_ready, 1)

                scale(0)
                for k in range(KT):
                    if k + 1 < KT:
                        scale(k + 1)
                    low(k)

            for n, (tile, value) in enumerate(((ones, 1.0), (mean_d, 1.0 / D), (mean_head, 1.0 / P), (eps, EPS))):
                nc.vector.memset(tile[:], value).then_inc(consts_set, 1)
            dve.wait_ge(filt_landed, 16 * 8)
            nc.vector.memset(lb_tmp[:], 0.0).then_inc(consts_set, 1)
            for n, dst in enumerate((p_a, p_b, p_c, p_d)):
                dve.wait_ge(rows_turned, n + 1)
                w, r = dst[:].shape
                nc.vector.tensor_copy(dst[:], bank[2 + n][0:w, 0:r]).then_inc(params_ready, 1)
            dve.wait_ge(params_ready, 4)
            dve.wait_ge(consts_set, 5)
            bounds = p_b[:, B_LOWER:B_LOWER + 16]
            tt(lb_tmp[:, 0], bounds, bounds, ALU.subtract).then_inc(lb_step, 1)
            dve.wait_ge(c_sig_ready, 1)
            tt(c_silu[:], p_a[:, A_C:A_C + 8], c_sig[:], ALU.mult).then_inc(c_silu_ready, 1)
            dve.wait_ge(lb_exp, 1)
            nc.vector.reciprocal(lb_tmp[:, 2], lb_tmp[:, 1]).then_inc(lb_step, 1)
            dve.wait_ge(lb_step, 2)
            tt(lb_tmp[:, 3], lb_tmp[:, 1], lb_tmp[:, 2], ALU.mult).then_inc(lb_step, 1)
            dve.wait_ge(lb_step, 3)
            tt(lb[:], lb_tmp[:, 3], lb_tmp[:, 3], ALU.subtract).then_inc(lb_step, 1)
            dve.wait_ge(lb_step, 4)
            ts(one_m_lb[:], lb[:], -1.0, 1.0, ALU.mult, ALU.add).then_inc(lb_step, 1)
            dve.wait_ge(c_silu_ready, 1)
            tt(w_even[:], f_w_out[:, 0], f_w_out[:, 1], ALU.add).then_inc(w_even_ready, 1)
            dve.wait_ge(w_even_ready, 1)
            tt(f_w_out[:, 1], f_w_out[:, 0], f_w_out[:, 1], ALU.subtract).then_inc(w_even_ready, 1)

            def reduce_angle(layer):
                dve.wait_ge(pre_sine, layer + 1)
                n = 6 * layer
                steps = (
                    lambda: ts(angle[:, 0], bank[4][0:FW], p_d[:, layer:layer + 1], p_d[:, 3:4], ALU.add, ALU.mult),
                    lambda: ts(turns[0], angle[:, 0], 1.0 / (2.0 * math.pi), ROUNDER, ALU.mult, ALU.add),
                    lambda: ts(turns[1], turns[0], ROUNDER, None, ALU.subtract),
                    lambda: stt(out=angle[:, 1], in0=turns[1], scalar=-TWO_PI_HIGH, in1=angle[:, 0],
                                op0=ALU.mult, op1=ALU.add),
                    lambda: stt(out=turns[0], in0=turns[1], scalar=-TWO_PI_LOW,
                                in1=angle[:, 1], op0=ALU.mult, op1=ALU.add),
                    lambda: ts(angle[:, 1], turns[0], 3.1415925, -3.1415925, ALU.min, ALU.max),
                )
                for step in steps:
                    if n:
                        dve.wait_ge(angle_step, n)
                    step().then_inc(angle_step, 1)
                    n += 1

            for layer in range(3):
                if layer:
                    dve.wait_ge(hidden_ready, layer)
                reduce_angle(layer)
                ada_piece(0, 2 * layer, ada_w0, ada_acc0[:, 0])
                ada_piece(0, 2 * layer + 1, ada_w0, ada_acc0[:, 0])
            piece = 6
            n = 0
            for j in range(4):
                dve.wait_ge(decay_ready, j + 1)
                for part in range(2):
                    for half in range(2):
                        dve.wait_ge(taps_raw, n + 1)
                        cols = slice(half * 512, half * 512 + 512)
                        tt(taps[:, part, j, cols], bank[4 + n % 2][:], decay[:, j % 2, cols],
                           ALU.mult).then_inc(taps_ready, 1)
                        n += 1
                for _ in range(2):
                    ada_piece(0, piece, ada_w0, ada_acc0[:, piece // 8])
                    piece += 1
            dve.wait_ge(taps_ready, 16)
            tt(taps0, taps[0:1, 0, 0], taps[0:1, 1, 0], ALU.add).then_inc(tap0_step, 1)
            dve.wait_ge(tap0_step, 1)
            stt(out=taps[0:1, 0, 0], in0=taps0, scalar=0.5, in1=skip_row[:], op0=ALU.mult,
                op1=ALU.add).then_inc(tap0_step, 1)
            for k in range(KT):
                add_square(0, k)
            n = 0
            for quarter in range(4):
                for part in range(2):
                    dve.wait_ge(spec_even, 2 * quarter + part + 1)
                    dve.wait_ge(spec_parts, 4 * quarter + 2 * part + 2)
                    if quarter and part == 0:
                        dve.wait_ge(spec_stored, 32 * quarter)
                    for minus in range(2):
                        tt(h_out[:, 2 * minus + part], even_s[:, part], bank[3 + 2 * part][:],
                           ALU.subtract if minus else ALU.add).then_inc(spec_ready, 1)
            for piece in range(14, 16):
                ada_piece(0, piece, ada_w0, ada_acc0[:, piece // 8])
            take_mod(0, 0)
            take_mod(0, 1)
            norm_rstd(0)
            norm_apply(0)

            def q_input(g):
                s = 5 * g
                dve.wait_ge(q_sig_ready, g + 1)
                tt(q_silu[:], bank[s % 2][:], q_sig, ALU.mult).then_inc(evicted[s % 2], 1)
                dve.wait_ge(evicted[s % 2], s // 2 + 1)

            def gate_input(g, way):
                s, b, col = 5 * g + 2 + way, g % 2, 8 * way + g
                if way == 0 and g >= 2:
                    dve.wait_ge(far_scores, 3 * (g - 1))
                    dve.wait_ge(level_scores, 8 * (g - 1))
                dve.wait_ge(f_pos_ready, 2 * g + way + 1)
                for place in ((1,) if way == 0 else (0, 2)):
                    ts(gates[:, place], f_pos[:], one_m_lb[:, col:col + 1], lb[:, col:col + 1], ALU.mult,
                       ALU.add).then_inc(gate_ready, 1)
                dve.wait_ge(evicted[s % 2], s // 2 + 1)
                ts(KK[b][:, way], f_neg[:], one_m_lb[:, col:col + 1], None, ALU.mult).then_inc(key_ready, 1)
                dve.wait_ge(gate_ready, 3 * g + (1 if way == 0 else 3))
                tt(QQ[b][:, 1 - way], q_silu[:], gates[:, 1 if way == 0 else 0],
                   ALU.mult).then_inc(query_ready, 1)

            def own_input(g):
                b = g % 2
                dve.wait_ge(key_ready, 2 * g + 2)
                tt(tmp_a[:, 0], KK[b][:, 0], KK[b][:, 1], ALU.add).then_inc(own_sum_ready, 1)
                dve.wait_ge(own_sum_ready, g + 1)
                if g:
                    dve.wait_ge(level_scores, 8 * g - 7)
                tt(own[:], q_silu[:], tmp_a[:, 0], ALU.mult).then_inc(own_ready, 1)

            def gate_output(g):
                s = 5 * g + 4
                dve.wait_ge(g_sig_ready, g + 1)
                stt(out=out_gate[:], in0=bank[s % 2][:], scalar=p_b[:, B_HEAD_G:B_HEAD_G + 1], in1=g_sig,
                    op0=ALU.mult, op1=ALU.mult).then_inc(evicted[s % 2], 1)
                dve.wait_ge(evicted[s % 2], s // 2 + 1)

            diag = view(scores, 0, [L + P, TT], [1, P])

            def take_level(h, n):
                dve.wait_ge(level_scores, 8 * h + n + 1)
                if n == 0:
                    if h:
                        dve.wait_ge(mixed, h)
                    ins = nc.vector.tensor_copy(diag, bank[2][:].rearrange("p (t n) -> p t n", t=TT))
                else:
                    dve.wait_ge(diag_scores, 8 * h + n)
                    m = view(mask, (n - 1) * P, [0, TT], [1, P])
                    ins = nc.vector.copy_predicated(diag, m,
                                                    bank[3 - (n - 1) % 2][:].rearrange("p (t n) -> p t n", t=TT))
                ins.then_inc(diag_scores, 1)

            def carry(h, n):
                b = h % 2
                width = 1 << n
                blocks = L // width
                t = gates if n == 0 else block_gates[width]
                if n:
                    dve.wait_ge(level_gates, 7 * h + n)
                    dve.wait_ge(level_keys, 8 * h + n)
                    dve.wait_ge(level_queries, 8 * h + n)
                if n == 7:
                    dve.wait_ge(far_scores, 3 * h + 1)
                else:
                    dve.wait_ge(level_scores, 8 * h + n + 2)
                dims = ([2 * width, 256 // width], [L + width, 2], [1, width])
                gate_dims = ([2, 256 // width], [blocks - 1, 2], [0, width])
                tt(view(KK[b], 0, *dims), view(KK[b], 0, *dims), view(t, blocks + 1, *gate_dims),
                   ALU.mult).then_inc(level_keys, 1)
                tt(view(QQ[b], 0, *dims), view(QQ[b], 0, *dims), view(t, 1, *gate_dims),
                   ALU.mult).then_inc(level_queries, 1)
                if n < 7:
                    tt(block_gates[2 * width][:], t[:, :, 0:blocks:2], t[:, :, 1:blocks:2],
                       ALU.mult).then_inc(level_gates, 1)

            def head_output(h, g):
                dve.wait_ge(head_std, h + 1)
                nc.vector.reciprocal(rstd[:], sum_sq[:]).then_inc(head_rstd, 1)
                dve.wait_ge(head_rstd, h + 1)
                tt(tmp_a[:, 1], bank[5][:], rstd[:], ALU.mult).then_inc(normed_ready, 1)
                dve.wait_ge(normed_ready, h + 1)
                tt(tmp_b[:, h % 2], tmp_a[:, 1], out_gate[:], ALU.mult).then_inc(gated_ready, 1)
                if g < HEADS:
                    own_input(g)
                    dve.wait_ge(gated_ready, h + 1)
                    gate_output(g)
                dve.wait_ge(gated_ready, h + 1)
                dve.wait_ge(o_hi_ready, h + 1)
                tt(h_lo[:, h], tmp_b[:, h % 2], h_hi[:, h].bitcast(F32), ALU.subtract).then_inc(o_lo_ready, 1)

            dve.wait_ge(mask_landed, 16)
            dve.wait_ge(spec_stored, 16 * 8)
            nc.vector.tensor_copy(mask[:].rearrange("p l n -> p (l n)"),
                                  scores[:, 0:2].rearrange("p a n -> p (a n)")[:, 0:len(LEVELS) * P]).then_inc(
                mask_set, 1)
            dve.wait_ge(mask_set, 1)
            for g in range(HEADS + 1):
                h = g - 1
                inputs = [lambda: q_input(g), None, lambda: gate_input(g, 0), lambda: gate_input(g, 1),
                          lambda: (own_input(g), gate_output(g))] if g < HEADS else [None] * 5
                if h < 0:
                    for work in inputs:
                        if work:
                            work()
                    continue
                for n in range(8):
                    take_level(h, n)
                    if n:
                        carry(h, n - 1)
                    if n == 1 and inputs[0]:
                        inputs[0]()
                    if n == 4:
                        if h == 4:
                            take_mod(1, 0)
                        ada_piece(1, 2 * h, ada_w1, ada_acc1)
                    if n == 6 and inputs[2]:
                        inputs[2]()
                carry(h, 7)
                if inputs[3]:
                    inputs[3]()
                ada_piece(1, 2 * h + 1, ada_w1, ada_acc1)
                head_output(h, g)

            def residual(m, s, n):
                dve.wait_ge(slab_done, s + 1)
                stt(out=xT[:, n], in0=bank[s % 2][:], scalar=mod[:, m, 16 + n:17 + n], in1=xT[:, n],
                    op0=ALU.mult, op1=ALU.add).then_inc(evicted[s % 2], 1)

            def norm(m, gate, s0):
                for n in range(KT):
                    residual(gate, s0 + n, n)
                    if n:
                        add_square(m, n - 1)
                    if m == 1 and n == 4:
                        take_mod(1, 1)
                add_square(m, 7)
                norm_rstd(m)
                if m < 4:
                    norm_apply(m)

            norm(1, 0, S_HG_OUT)

            def mlp(i, s0, with_ada):
                for ch in range(CHUNKS):
                    for n in range(8):
                        s, j = s0 + 16 * ch + n, 8 * (CHUNKS * i + ch) + n
                        dve.wait_ge(evicted[s % 2], s // 2 + 1)
                        r = tmp_a[:, n % 2]
                        tt(h_hi[:, n], r, r, ALU.mult).then_inc(h_hi_ready, 1)
                        dve.wait_ge(h_hi_ready, j + 1)
                        dve.wait_ge(relu_sq_ready, j + 1)
                        tt(h_lo[:, n], tmp_b[:, n % 2], h_hi[:, n].bitcast(F32), ALU.subtract).then_inc(h_lo_ready, 1)
                        if with_ada and n % 2 == 1:
                            if ch and n == 1:
                                take_mod(2 + (ch - 1) // 2, (ch - 1) % 2)
                            q = 8 * ch + n // 2
                            ada_piece(2 + q // 16, q % 16, ada_w2, ada_acc2)
                    for n in range(8):
                        residual(2 * i + 1, s0 + 16 * ch + 8 + n, n)
                        if ch == CHUNKS - 1 and n:
                            add_square(2 * i + 2, n - 1)
                        if with_ada and n % 2 == 1:
                            q = 8 * ch + 4 + n // 2
                            ada_piece(2 + q // 16, q % 16, ada_w2, ada_acc2)
                m = 2 * i + 2
                add_square(m, 7)
                if with_ada:
                    take_mod(3, 1)
                norm_rstd(m)
                if m < 4:
                    norm_apply(m)

            mlp(0, S_MLP0, True)

            for seg in range(3):
                nc.vector.memset(view(padded[seg], 0, [L + 1, 2]), 0.0).then_inc(pad_set, 1)

            def convolve(g, j):
                s = S_HY_IN + 6 * g + j
                seg, n = HY_ORDER[j]
                par = group_params[g % 2]
                dst = x0[:, n] if seg == 0 else conv[seg - 1][:]
                dve.wait_ge(evicted[s % 2], s // 2 + 1)
                if seg and 2 * g + n:
                    dve.wait_ge(z_ready, 2 * g + n)
                if seg == 0 and g:
                    dve.wait_ge(y_gated, 2 * g - 1 + n)
                c0 = 3 * (6 * g + j)
                ts(dst, padded[seg][:, 0:L], par[:, 0, seg, n:n + 1], par[:, 4, seg, n:n + 1], ALU.mult,
                   ALU.add).then_inc(conv_step, 1)
                for tap in (1, 2):
                    dve.wait_ge(conv_step, c0 + tap)
                    stt(out=dst, in0=padded[seg][:, tap:tap + L], scalar=par[:, tap, seg, n:n + 1], in1=dst,
                        op0=ALU.mult, op1=ALU.add).then_inc(conv_step, 1)
                dve.wait_ge(conv_step, c0 + 3)

            def make_z(g, n):
                if g:
                    dve.wait_ge(z_turned, 2 * g + n - 1)
                tt(z[n][:], conv[0][:], conv[1][:], ALU.mult).then_inc(z_ready, 1)

            def spectral(h, m):
                n = 2 * h + m
                dve.wait_ge((H_landed0, H_landed1)[m], 16 * (h + 1))
                dve.wait_ge(z_even, n + 1)
                dve.wait_ge(z_parts, 2 * n + 2)
                odd = bank[3][:].rearrange("p (a n) -> p a n", a=2)
                tt(Z[:, 0:2], even_z, odd, ALU.add).then_inc(Z_ready, 1)
                tt(Z[:, 2:4], even_z, odd, ALU.subtract).then_inc(Z_ready, 1)
                dve.wait_ge(Z_ready, 2 * n + 2)
                tt(ZH[:], Z, H[m][:], ALU.mult).then_inc(ZH_ready, 1)
                dve.wait_ge(ZH_ready, 2 * n + 1)
                tt(Y[:, 0:4:2], ZH[:, 0:4:2], ZH[:, 1:4:2], ALU.subtract).then_inc(Y_ready, 1)
                dve.wait_ge(Y_ready, 2 * n + 1)
                swapped = view(H[m], GC, [2 * GC, 2], [-GC, 2], [1, GC])
                tt(ZH[:].rearrange("p (a b) n -> p a b n", a=2), Z.rearrange("p (a b) n -> p a b n", a=2), swapped,
                   ALU.mult).then_inc(ZH_ready, 1)
                dve.wait_ge(ZH_ready, 2 * n + 2)
                tt(Y[:, 1:4:2], ZH[:, 0:4:2], ZH[:, 1:4:2], ALU.add).then_inc(Y_ready, 1)
                dve.wait_ge(Y_ready, 2 * n + 2)
                if h and m == 0:
                    dve.wait_ge(y_ready, 2 * h)
                tt(folded[:, m, 0], Y[:, 0:2], Y[:, 2:4], ALU.add).then_inc(folded_ready, 1)
                tt(folded[:, m, 1], Y[:, 0:2], Y[:, 2:4], ALU.subtract).then_inc(folded_ready, 1)

            def gate_y(h, n):
                dve.wait_ge(y_ready, 2 * h + n + 1)
                by_parity = [[1, 2], [2, 256]]
                tt(view(tmp_b, n * L, *by_parity), bank[5 + n][:].rearrange("p (a n) -> p a n", a=2),
                   view(x0, n * L, *by_parity), ALU.mult).then_inc(y_gated, 1)

            def low_y(h, n):
                dve.wait_ge(y_gated, 2 * h + n + 1)
                dve.wait_ge(y_hi_ready, 2 * h + n + 1)
                k = 2 * h + n
                tt(h_lo[:, k], tmp_b[:, n], h_hi[:, k].bitcast(F32), ALU.subtract).then_inc(y_lo_ready, 1)

            for g in range(GROUPS + 1):
                h = g - 1
                if g < GROUPS:
                    nc.vector.tensor_copy(group_params[g % 2][:],
                                          view(p_c, 2 * g, [24, 5], [8, 3], [1, 2])).then_inc(group_ready, 1)
                    dve.wait_ge(group_ready, g + 1)
                    convolve(g, 0)
                    if g:
                        spectral(h, 0)
                    convolve(g, 1)
                    make_z(g, 0)
                    convolve(g, 2)
                    if g:
                        spectral(h, 1)
                    convolve(g, 3)
                    make_z(g, 1)
                    if g:
                        gate_y(h, 0)
                        gate_y(h, 1)
                    convolve(g, 4)
                    convolve(g, 5)
                    if g:
                        low_y(h, 0)
                        low_y(h, 1)
                else:
                    spectral(h, 0)
                    spectral(h, 1)
                    gate_y(h, 0)
                    gate_y(h, 1)
                    low_y(h, 0)
                    low_y(h, 1)
            norm(3, 2, S_HY_OUT)
            mlp(1, S_MLP1, False)

            for k in range(KT):
                if k >= 2:
                    dve.wait_ge(o_turned, k - 1)
                stt(out=tmp_b[:, k % 2], in0=xT[:, k], scalar=p_b[:, B_FINAL_G + k:B_FINAL_G + k + 1], in1=rstd[:],
                    op0=ALU.mult, op1=ALU.mult).then_inc(full_ready, 1)


INPUTS = ["x", "c", "ada_w", "ada_b", "norm_g", "hg_w_in", "hg_lower_bounds", "hg_norm_g", "hg_w_out",
          "hy_w_in", "hy_b_in", "hy_conv_w", "hy_conv_b", "hy_filt_w_in", "hy_filt_w_mid", "hy_filt_b",
          "hy_filt_freq", "hy_filt_w_out", "hy_skip", "hy_w_out", "mlp_w1", "mlp_w2", "final_g"]


def kernel(**inputs):
    import concourse.bacc as bacc
    from concourse.bass_utils import run_bass_kernel_spmd

    nc = bacc.Bacc("TRN2", target_bir_lowering=False, num_devices=1)
    arrays = {name: np.ascontiguousarray(inputs[name]) for name in INPUTS}
    forward, inverse = transform_tables()
    emb_t, rates, times = filter_constants()
    arrays |= {"fwd_table": forward, "inv_table": inverse, "emb_t": emb_t, "decay_rates": rates,
               "minus_times": times, "masks": level_masks(), "identity": np.eye(P, dtype=np.float32)}
    tensors = [nc.dram_tensor(n, a.shape, mybir.dt.from_np(a.dtype), kind="ExternalInput").ap()
               for n, a in arrays.items()]
    out = nc.dram_tensor("out", (1, L, D), F32, kind="ExternalOutput").ap()
    hybrid_encoder(nc, *tensors, out)
    result = run_bass_kernel_spmd(nc, [arrays], core_ids=[0])
    return result.results[0]["out"]
```

```python
import math
from contextlib import ExitStack

import numpy as np

import concourse.bass as bass
from concourse import mybir

F32 = mybir.dt.float32
F32R = mybir.dt.float32r
U8 = mybir.dt.uint8
ALU = mybir.AluOpType
ACT = mybir.ActivationFunctionType

P = 128
D = 1024
L = 512
KT = D // P
TT = L // P
HEADS = 8
D_FF = 4 * D
CHUNKS = D_FF // D
EPS = 1e-6
FW = 64
EMB = 33
BANDS = (EMB - 1) // 2
LEVELS = [1 << n for n in range(7)]
GROUPS = 4
GC = D // GROUPS
FT = L // 4 // P * 2

S_HG_IN = 0
S_HG_OUT = S_HG_IN + 5 * HEADS
S_MLP0 = S_HG_OUT + KT
S_HY_IN = S_MLP0 + 16 * CHUNKS
S_HY_OUT = S_HY_IN + 6 * GROUPS
S_MLP1 = S_HY_OUT + KT
N_SLABS = S_MLP1 + 16 * CHUNKS
STAGE_SLOTS = 6

HY_ORDER = ((1, 0), (2, 0), (1, 1), (2, 1), (0, 0), (0, 1))

TOKEN_TILES = [0, 256, 1, 257]

A_C, A_ADA_B = 0, 8
B_NORM_G, B_FINAL_G, B_LOWER, B_HEAD_G = 0, 32, 40, 56
TWO_PI_HIGH = 6.28125
TWO_PI_LOW = 2.0 * math.pi - TWO_PI_HIGH
ROUNDER = 12582912.0


class At:

    def __init__(self, i, k=1, c=0):
        self.i, self.k, self.c = i, k, c

    def __add__(self, n):
        return At(self.i, self.k, self.c + n)

    def __sub__(self, n):
        return self + -n

    def __mul__(self, n):
        return At(self.i, self.k * n, self.c * n)

    def __floordiv__(self, n):
        assert self.k % n == 0
        return At(self.i, self.k // n, self.c // n)

    def __mod__(self, n):
        assert self.k % n == 0
        return self.c % n

    def __ge__(self, n):
        assert self.c >= n or self.c + self.k >= n
        return True

    __radd__, __rmul__ = __add__, __mul__


def v(x):
    return x.i * x.k + x.c if isinstance(x, At) else x


def view(tile, offset, *dims):
    whole = tile[:]
    return bass.AP(tensor=whole.tensor, offset=offset, ap=[list(whole.ap[0])] + [list(d) for d in dims])


def transform_tables():
    p = np.arange(P)
    omega = np.pi * (2 * np.arange(256) + 1) / 1024
    forward = np.zeros((P, 4, 2, 256))
    for j, start in enumerate(TOKEN_TILES):
        phase = (start + 2 * p)[:, None] * omega[None]
        forward[:, j, 0], forward[:, j, 1] = np.cos(phase), np.sin(phase)
    inverse = np.zeros((P, 2, 2, 2, 256))
    for m in range(2):
        for parity in range(2):
            phase = omega[m * P + p][:, None] * (parity + 2 * np.arange(256))[None]
            inverse[:, m, 0, parity], inverse[:, m, 1, parity] = np.cos(phase) / 512, np.sin(phase) / 512
    return forward.astype(np.float32), inverse.astype(np.float32)


def filter_constants():
    f = np.float32
    t = np.linspace(0.0, 1.0, L, dtype=f)[:, None]
    bands = np.linspace(1e-4, BANDS - 1.0, BANDS, dtype=f)
    ang = f(2.0 * math.pi / L) * np.arange(L, dtype=f)[:, None] * bands
    emb = np.concatenate([t, np.cos(ang), -np.sin(ang)], axis=-1).astype(f)
    rates = np.abs(np.linspace(math.log(1e-2) / 1.5, math.log(1e-2) / 0.3, D, dtype=f))
    times = np.stack([-t[start + 2 * np.arange(P), 0] for start in TOKEN_TILES], axis=1)
    return np.ascontiguousarray(emb.T), rates, np.ascontiguousarray(times.astype(f))


def level_masks():
    s, t = np.arange(P)[:, None], np.arange(P)[None]
    return np.stack([((s // (2 * h)) == (t // (2 * h))) & ((s // h) != (t // h)) for h in LEVELS],
                    axis=1).astype(np.float32)


def hybrid_encoder(nc, x, c, ada_w, ada_b, norm_g, hg_w_in, hg_lower_bounds, hg_norm_g, hg_w_out,
                   hy_w_in, hy_b_in, hy_conv_w, hy_conv_b, hy_filt_w_in, hy_filt_w_mid, hy_filt_b,
                   hy_filt_freq, hy_filt_w_out, hy_skip, hy_w_out, mlp_w1, mlp_w2, final_g,
                   fwd_table, inv_table, emb_t, decay_rates, minus_times, masks, identity, out):
    spectrum = nc.dram_tensor("filter_spectrum", (GROUPS, P, 2, 4, GC), F32, kind="Internal").ap()

    with ExitStack() as ctx:
        def sb(name, shape, dt=F32, stack=ctx):
            return stack.enter_context(nc.sbuf_tensor(name, shape, dt))

        def sem(name):
            return ctx.enter_context(nc.semaphore(name))

        bank = [ctx.enter_context(nc.psum_tensor(f"bank{b}", [P, 512], F32)) for b in range(8)]

        xT = sb("xT", [P, KT, L])
        a_hi = sb("a_hi", [P, KT, L], F32R)
        a_lo = sb("a_lo", [P, KT, L], F32R)
        stage = sb("stage", [P, STAGE_SLOTS, KT, P])
        w_hi = sb("w_hi", [P, 2, KT, P], F32R)
        w_lo = sb("w_lo", [P, 2, KT, P], F32R)
        ident = sb("ident", [P, P])
        ones = sb("ones", [P, P])
        mean_d = sb("mean_d", [P, P])
        mean_head = sb("mean_head", [P, P])
        eps = sb("eps", [P, 1])
        p_a = sb("p_a", [P, 104])
        p_b = sb("p_b", [P, 57])
        p_c = sb("p_c", [P, 120])
        mod = sb("mod", [P, 96])
        gain = sb("gain", [P, 4, 8])
        c_sig = sb("c_sig", [P, 8])
        c_silu = sb("c_silu", [P, 8])
        lb = sb("lb", [P, 16])
        one_m_lb = sb("one_m_lb", [P, 16])
        lb_tmp = sb("lb_tmp", [P, 4, 16])
        sum_sq = sb("sum_sq", [P, L])
        sq = sb("sq", [P, 2, L])
        std = sb("std", [P, L])
        std_cols = sb("std_cols", [P, TT])
        rstd_cols = sb("rstd_cols", [P, TT])
        tmp_a = sb("tmp_a", [P, 2, L])
        tmp_b = sb("tmp_b", [P, 2, L])

        with ExitStack() as st:
            x_nat = stage[:, 0:4].rearrange("p t k n -> p t (k n)")
            rows_a = sb("rows_a", [104, P], stack=st)
            rows_b = sb("rows_b", [57, P], stack=st)
            rows_c = sb("rows_c", [120, P], stack=st)
            rows_d = sb("rows_d", [4, FW], stack=st)
            p_d = sb("p_d", [FW, 4], stack=st)
            embT = sb("embT", [EMB, L], stack=st)
            f_w_in = sb("f_w_in", [EMB, FW], stack=st)
            f_w_mid = sb("f_w_mid", [FW, 2, FW], stack=st)
            f_w_out = sb("f_w_out", [FW, 2, D], stack=st)
            w_even = sb("w_even", [FW, D], stack=st)
            taps_tmp = sb("taps_tmp", [FW, L], stack=st)
            hidden, angle, turns = sum_sq[0:FW], tmp_b[0:FW], (std[0:FW], taps_tmp[:])
            rates = sq[:].rearrange("p a n -> p (a n)")
            minus_t = sb("minus_t", [P, 4], stack=st)
            skip_row = sb("skip_row", [1, D], stack=st)
            taps0 = tmp_b[0:1].rearrange("p a n -> p (a n)")
            decay = stage[:, 4:6].rearrange("p t k n -> p t (k n)")
            taps = sb("taps", [P, 2, 4, D], stack=st)
            tab_s = sb("tab_s", [P, 4, 2, 256], stack=st)
            even_s = tmp_a
            h_out = sb("h_out", [P, 4, L], stack=st)
            ada_w0 = sb("ada_w0", [P, 4, D], stack=st)
            ada_acc0 = sb("ada_acc0", [P, 2, D], stack=st)

        h_hi = sb("h_hi", [P, KT, L], F32R)
        h_lo = sb("h_lo", [P, KT, L], F32R)

        with ExitStack() as st:
            KK = [sb(f"KK{b}", [P, 2, L], stack=st) for b in range(2)]
            QQ = [sb(f"QQ{b}", [P, 2, L], stack=st) for b in range(2)]
            joined = [stage[:, 5, 4 * b:4 * b + 4].rearrange("p k n -> p (k n)") for b in range(2)]
            gates = sb("gates", [P, 3, L], stack=st)
            own = sb("own", [P, L], stack=st)
            values = [sb(f"values{b}", [P, TT, P], stack=st) for b in range(2)]
            out_gate = sb("out_gate", [P, L], stack=st)
            block_gates = {h: sb(f"block_gates{h}", [P, 3, L // h], stack=st) for h in LEVELS[1:] + [128]}
            scores = sb("scores", [P, TT, L], stack=st)
            q_sig, g_sig = sq[:, 0], sq[:, 1]
            q_silu = sb("q_silu", [P, L], stack=st)
            i_T = sb("i_T", [P, L], stack=st)
            f_pos = sb("f_pos", [P, L], stack=st)
            f_neg = sb("f_neg", [P, L], stack=st)
            mask = sb("mask", [P, len(LEVELS), P], U8, stack=st)
            ada_w1 = sb("ada_w1", [P, 2, D], stack=st)
            ada_acc1 = sb("ada_acc1", [P, 1, D], stack=st)

        with ExitStack() as st:
            ada_w2 = sb("ada_w2", [P, 8, D], stack=st)
            ada_acc2 = sb("ada_acc2", [P, 2, D], stack=st)

        with ExitStack() as st:
            tab_f = sb("tab_f", [P, 4, 2, 256], stack=st)
            tab_i = sb("tab_i", [P, 2, 2, 2, 256], stack=st)
            group_params = [sb(f"group_params{b}", [P, 5, 3, 2], stack=st) for b in range(2)]
            padded = [sb(f"padded{b}", [P, L + 2], stack=st) for b in range(3)]
            conv = [sb(f"conv{b}", [P, L], stack=st) for b in range(2)]
            z = [sb(f"z{b}", [P, L], stack=st) for b in range(2)]
            x0 = sb("x0", [P, 2, L], stack=st)
            z_t = [sb(f"z_t{b}", [P, 4, GC], stack=st) for b in range(2)]
            H = [sb(f"H{b}", [P, 4, GC], stack=st) for b in range(2)]
            ZH = sb("ZH", [P, 4, GC], stack=st)
            even_z = std[:].rearrange("p (a n) -> p a n", a=2)
            Z = tmp_a[:].rearrange("p b (a n) -> p (b a) n", a=2)
            Y = sq[:].rearrange("p b (a n) -> p (b a) n", a=2)
            folded = sb("folded", [P, 2, 2, 2, GC], stack=st)

        with ExitStack() as st:
            o_nat = sb("o_nat", [P, TT, D], stack=st)

        weight_landed = [sem(f"weight_landed{j}") for j in range(STAGE_SLOTS)]
        weight_cast, weight_split = sem("weight_cast"), sem("weight_split")
        half_done, slab_done = sem("half_done"), sem("slab_done")
        evicted = [sem("evicted_even"), sem("evicted_odd")]
        sq_ready, sum_ready, mean_ready, std_ready, rstd_ready, rstd_spread = map(sem, (
            "sq_ready", "sum_ready", "mean_ready", "std_ready", "rstd_ready", "rstd_spread"))
        scaled_ready, a_hi_ready, a_lo_ready, final_ready = map(sem, (
            "scaled_ready", "a_hi_ready", "a_lo_ready", "final_ready"))
        relu_sq_ready, h_hi_ready, h_lo_ready = map(sem, ("relu_sq_ready", "h_hi_ready", "h_lo_ready"))
        ada_landed = [sem(f"ada_landed{n}") for n in range(8)]
        ada_summed, ada_columns, mod_ready, gain_ready = map(sem, (
            "ada_summed", "ada_columns", "mod_ready", "gain_ready"))
        consts_set, rows_landed, ident_landed, x_landed, filt_landed = map(sem, (
            "consts_set", "rows_landed", "ident_landed", "x_landed", "filt_landed"))
        rows_turned, params_ready, c_sig_ready, c_silu_ready = map(sem, (
            "rows_turned", "params_ready", "c_sig_ready", "c_silu_ready"))
        lb_step, lb_exp = sem("lb_step"), sem("lb_exp")
        x_turned, x_ready = sem("x_turned"), sem("x_ready")
        w_even_ready, pre_sine, angle_step, hidden_ready = map(sem, (
            "w_even_ready", "pre_sine", "angle_step", "hidden_ready"))
        taps_raw, decay_ready, taps_ready, tap0_step = map(sem, (
            "taps_raw", "decay_ready", "taps_ready", "tap0_step"))
        spec_parts, spec_even, spec_ready, spec_stored = map(sem, (
            "spec_parts", "spec_even", "spec_ready", "spec_stored"))
        q_sig_ready, q_ready, i_turned, values_ready = map(sem, (
            "q_sig_ready", "q_ready", "i_turned", "values_ready"))
        f_pos_ready, gate_ready, key_ready, query_ready, own_ready = map(sem, (
            "f_pos_ready", "gate_ready", "key_ready", "query_ready", "own_ready"))
        g_sig_ready, own_sum_ready, keys_joined = map(sem, ("g_sig_ready", "own_sum_ready", "keys_joined"))
        level_scores, diag_scores, level_keys, level_queries, level_gates = map(sem, (
            "level_scores", "diag_scores", "level_keys", "level_queries", "level_gates"))
        far_scores, far_copied, mixed, mixed_sq, head_mean, head_std, head_rstd, head_spread = map(sem, (
            "far_scores", "far_copied", "mixed", "mixed_sq", "head_mean", "head_std", "head_rstd", "head_spread"))
        normed_ready, gated_ready, o_hi_ready, o_lo_ready = map(sem, (
            "normed_ready", "gated_ready", "o_hi_ready", "o_lo_ready"))
        mask_landed, mask_set = sem("mask_landed"), sem("mask_set")
        tables_landed, H_landed0, H_landed1, pad_set, group_ready = map(sem, (
            "tables_landed", "H_landed0", "H_landed1", "pad_set", "group_ready"))
        conv_step, z_ready, z_turned, z_t_ready = map(sem, ("conv_step", "z_ready", "z_turned", "z_t_ready"))
        z_parts, z_even, Z_ready, ZH_ready, Y_ready, folded_ready = map(sem, (
            "z_parts", "z_even", "Z_ready", "ZH_ready", "Y_ready", "folded_ready"))
        y_ready, y_gated, y_hi_ready, y_lo_ready = map(sem, ("y_ready", "y_gated", "y_hi_ready", "y_lo_ready"))
        o_turned, o_copied, stored = map(sem, ("o_turned", "o_copied", "stored"))

        hg_in, hy_in = hg_w_in[0], hy_w_in[0]

        def columns(w, first):
            return w[:, bass.ds(v(first), P)].rearrange("(k p) n -> p k n", p=P)

        block = ctx.enter_context(nc.Block())

        @block.sync
        def _(sp):
            for dst, src in (
                (rows_a[A_C:A_C + 8], c.rearrange("a (n p) -> (a n) p", p=P)),
                (rows_a[A_ADA_B:104], ada_b.rearrange("i s (n p) -> (i s n) p", p=P)),
                (rows_b[B_NORM_G:32], norm_g.rearrange("i s (n p) -> (i s n) p", p=P)),
                (rows_b[B_FINAL_G:40], final_g.rearrange("(n p) -> n p", p=P)),
                (rows_b[B_LOWER:56], hg_lower_bounds.rearrange("i s (n p) -> (i s n) p", p=P)),
                (rows_b[B_HEAD_G:57], hg_norm_g),
                (rows_c[0:72], hy_conv_w.rearrange("i s (n p) -> (i s n) p", p=P)),
                (rows_c[72:96], hy_b_in.rearrange("i (n p) -> (i n) p", p=P)),
                (rows_c[96:120], hy_conv_b.rearrange("i (n p) -> (i n) p", p=P)),
                (rows_d[0:3], hy_filt_b[0]),
                (rows_d[3:4], hy_filt_freq),
            ):
                sp.dma_start(dst, src).then_inc(rows_landed, 16)
            sp.dma_start(ident[:], identity).then_inc(ident_landed, 16)
            for dst, src in (
                (embT[:], emb_t), (f_w_in[:], hy_filt_w_in[0]),
                (f_w_mid[:], hy_filt_w_mid[0].rearrange("m a b -> a m b")),
                (f_w_out[:], hy_filt_w_out[0].rearrange("w (s d) -> w s d", s=2)),
                (rates, decay_rates.partition_broadcast(P)), (minus_t[:], minus_times),
                (skip_row[:], hy_skip), (tab_s[:], fwd_table),
            ):
                sp.dma_start(dst, src).then_inc(filt_landed, 16)

            def load_ada(q, buffer, first):
                m, third, k = q // 24, q // 8 % 3, q % 8
                slots = buffer[:].shape[1]
                if q >= first + slots:
                    sp.wait_ge(ada_summed, q - slots + 1)
                src = ada_w[m // 2, m % 2, k * P:(k + 1) * P, third * D:(third + 1) * D]
                sp.dma_start(buffer[:, (q - first) % slots], src).then_inc(ada_landed[q % 8], 16)

            def load_slab(s, slot, src, wait=None):
                if wait is not None:
                    sp.wait_ge(weight_split, v(2 * wait))
                sp.dma_start(stage[:, slot], src).then_inc(weight_landed[slot], 16)

            for q in range(4):
                load_ada(q, ada_w0, 0)
            sp.dma_start(x_nat, x[0].rearrange("(t p) d -> p t d", p=P)).then_inc(x_landed, 16)
            for q in range(4, 16):
                load_ada(q, ada_w0, 0)

            sp.wait_ge(x_turned, KT)
            for j in range(5):
                if j == 4:
                    sp.wait_ge(taps_ready, 16)
                load_slab(j, j, columns(hg_in, j * D))
            sp.wait_ge(spec_stored, 16 * 8)
            sp.wait_ge(ada_columns, 2)
            sp.dma_start(scores[:, 0:2].rearrange("p a n -> p (a n)")[:, 0:len(LEVELS) * P],
                         masks.rearrange("p l n -> p (l n)")).then_inc(mask_landed, 16)
            for q in range(16, 18):
                load_ada(q, ada_w1, 16)
            def load_hg_out(n):
                load_slab(S_HG_OUT + n, n % 4, columns(hg_w_out[0], n * P), S_HG_OUT + n - 3)

            for h in range(1, HEADS + 1):
                for j in range(5 if h < HEADS else 0):
                    s = 5 * h + j
                    load_slab(s, j, columns(hg_in, j * D + h * P), s - 4)
                for n in range(4 if h == HEADS else 0):
                    load_hg_out(n)
                for n in range(4):
                    q = 16 + 4 * (h - 1) + n + 2
                    if q < 48:
                        load_ada(q, ada_w1, 16)
            for n in range(4, KT):
                load_hg_out(n)

            def mlp_slab(i, s0, ch, n):
                s = 16 * ch + (s0 + n)
                if n < 8:
                    src = columns(mlp_w1[i], D * ch + n * P)
                else:
                    src = columns(mlp_w2[i, bass.ds(v(D * ch), D)], (n - 8) * P)
                load_slab(s, n % 4, src, s - 3)

            sp.wait_ge(o_lo_ready, HEADS)
            sp.wait_ge(ada_columns, 6)
            for ch in range(CHUNKS):
                for n in range(16):
                    if ch < CHUNKS - 1:
                        load_ada(48 + 16 * ch + n, ada_w2, 48)
                    mlp_slab(0, S_MLP0, ch, n)

            for g in range(GROUPS):
                for j, (seg, n) in enumerate(HY_ORDER):
                    s = S_HY_IN + 6 * g + j
                    wait = s - 5 if g else (s - 3 if j < 4 else s - 5)
                    load_slab(s, j, columns(hy_in, seg * D + g * GC + n * P), wait)
                if g == 0:
                    sp.wait_ge(ada_columns, 12)
                    sp.dma_start(tab_f[:], fwd_table).then_inc(tables_landed, 16)
                    sp.dma_start(tab_i[:], inv_table).then_inc(tables_landed, 16)
                for h in ((), (0,), (1,), (2, 3))[g]:
                    for m in range(2):
                        if h:
                            sp.wait_ge(ZH_ready, 4 * (h - 1) + 2 * m + 2)
                        sp.dma_start(H[m][:], spectrum[h, :, m]).then_inc((H_landed0, H_landed1)[m], 16)
            for n in range(KT):
                s = S_HY_OUT + n
                load_slab(s, n % 4, columns(hy_w_out[0], n * P), s - 3)
            with sp.Fori(0, CHUNKS) as ch:
                for n in range(16):
                    mlp_slab(1, S_MLP1, At(ch), n)

            for half in range(2):
                sp.wait_ge(o_copied, 4 * (half + 1))
                cols = slice(half * 512, half * 512 + 512)
                sp.dma_start(out[0].rearrange("(t p) d -> p t d", p=P)[:, :, cols],
                             o_nat[:, :, cols]).then_inc(stored, 16)
            sp.wait_ge(stored, 32)

        @block.gpsimd
        def _(pool):
            def split_slab(s, slot, landed):
                side = s % 2
                pool.wait_ge(weight_landed[slot], v(landed * 16))
                for half in range(2):
                    k = slice(4 * half, 4 * half + 4)
                    if s >= 2:
                        pool.wait_ge((half_done, slab_done)[half], v(s - 1))
                    if isinstance(s, At):
                        pool.nop(nofuse=True)
                    nc.gpsimd.tensor_scalar(w_hi[:, side, k], stage[:, slot, k], 1.0, 0.0, ALU.mult,
                                            ALU.add).then_inc(weight_cast, 1)
                    pool.wait_ge(weight_cast, v(2 * s + half + 1))
                    nc.gpsimd.tensor_tensor(w_lo[:, side, k], stage[:, slot, k], w_hi[:, side, k].bitcast(F32),
                                            ALU.subtract).then_inc(weight_split, 1)

            for k in range(KT):
                pool.wait_ge(sq_ready, k + 1)
                if k == 0:
                    pool.wait_ge(taps_raw, 16)
                    ins = nc.gpsimd.tensor_scalar(sum_sq[:], sq[:, 0], 1.0, 0.0, ALU.mult, ALU.add)
                else:
                    pool.wait_ge(sum_ready, k)
                    ins = nc.gpsimd.tensor_tensor(sum_sq[:], sum_sq[:], sq[:, k % 2], ALU.add)
                ins.then_inc(sum_ready, 1)
            landed = [0] * STAGE_SLOTS

            def split_phase(first, end, slots, body):
                with pool.Fori(0, (end - first) // body) as i:
                    for n in range(body):
                        split_slab(At(i, body, first + n), n % slots,
                                   At(i, body // slots, landed[n % slots] + n // slots + 1))
                for slot in range(slots):
                    landed[slot] += (end - first) // slots

            for s in range(10):
                split_slab(s, s % 5, s // 5 + 1)
            landed[0:5] = [2] * 5
            split_phase(10, S_HG_OUT, 5, 10)
            split_phase(S_HG_OUT, S_HY_IN, 4, 4)
            split_phase(S_HY_IN, S_HY_OUT, 6, 6)
            split_phase(S_HY_OUT, N_SLABS, 4, 4)

        @block.tensor
        def _(pe):
            def product(dst, pairs, after=None):
                for n, (lhs, rhs) in enumerate(pairs):
                    ins = pe.matmul(dst, lhs, rhs, start=n == 0, stop=n == len(pairs) - 1)
                return ins

            def k_tile(s, k, hi, lo):
                side = s % 2
                if k % 4 == 0:
                    pe.wait_ge(weight_split, v(2 * s + k // 4 + 1))
                if k == 0 and s >= 2:
                    pe.wait_ge(evicted[side], v(s // 2))
                acc = bank[side][:]
                pe.matmul(acc, w_hi[:, side, k], hi[:, k], start=k == 0, stop=False)
                pe.matmul(acc, w_lo[:, side, k], hi[:, k], start=False, stop=False)
                ins = pe.matmul(acc, w_hi[:, side, k], lo[:, k], start=False, stop=k == KT - 1)
                if k % 4 == 3:
                    ins.then_inc((half_done, slab_done)[k // 4], 1)

            def slab(s, hi, lo, between={}):
                for k in range(KT):
                    k_tile(s, k, hi, lo)
                    for work in between.get(k, ()):
                        work()

            def first_pair(s, hi, lo, hi_ready, lo_ready, before, between={}):
                for k in range(KT):
                    pe.wait_ge(hi_ready, v(before + k + 1))
                    pe.wait_ge(lo_ready, v(before + k + 1))
                    for n in range(2):
                        k_tile(s + n, k, hi, lo)
                        for work in between.get(2 * k + n, ()):
                            work()

            def ada_column(c, acc):
                pe.wait_ge(ada_summed, v(8 * (c + 1)))
                if c >= 1:
                    pe.wait_ge(mod_ready, v(c))
                for n in range(8):
                    ins = pe.matmul(bank[6][:, n:n + 1], acc[:, n * P:(n + 1) * P], ones[:, 0:1],
                                    start=True, stop=True)
                ins.then_inc(ada_columns, 1)

            def token_means(squares, weight):
                for t in range(TT):
                    ins = pe.matmul(bank[7][:, t:t + 1], squares[:, t * P:(t + 1) * P], weight[:, 0:1],
                                    start=True, stop=True)
                return ins

            def spread():
                for t in range(TT):
                    ins = pe.matmul(bank[7][:, t * P:(t + 1) * P], view(rstd_cols, t, [0, P]), ident[:],
                                    start=True, stop=True)
                return ins

            def norm_mean(m):
                pe.wait_ge(sum_ready, 8 * (m + 1))
                if m == 1:
                    pe.wait_ge(gated_ready, HEADS)
                if m:
                    pe.wait_ge(scaled_ready, 8 * m)
                token_means(sum_sq, mean_d).then_inc(mean_ready, 1)
                pe.wait_ge(rstd_ready, m + 1)
                spread().then_inc(rstd_spread, 1)

            pe.wait_ge(ident_landed, 16)
            pe.wait_ge(rows_landed, 16 * 11)
            pe.wait_ge(consts_set, 5)
            for n, rows in enumerate((rows_a, rows_b, rows_c, rows_d)):
                r, w = rows[:].shape
                pe.transpose(bank[2 + n][0:w, 0:r], rows[:], ident[0:r, 0:r]).then_inc(rows_turned, 1)
            pe.wait_ge(filt_landed, 16 * 8)
            pe.wait_ge(params_ready, 4)
            pe.matmul(bank[4][0:FW], f_w_in[:], embT[:], start=True, stop=True).then_inc(pre_sine, 1)
            def turn_x(k):
                if k == 0:
                    pe.wait_ge(x_landed, 16)
                if k >= 2:
                    pe.wait_ge(x_ready, k - 1)
                for t in range(TT):
                    ins = pe.transpose(bank[2 + k % 2][:, t * P:(t + 1) * P], x_nat[:, t, k * P:(k + 1) * P],
                                       ident[:])
                ins.then_inc(x_turned, 1)

            for m in range(2):
                pe.wait_ge(hidden_ready, m + 1)
                pe.matmul(bank[4][0:FW], f_w_mid[:, m], hidden, start=True, stop=True).then_inc(pre_sine, 1)
                for k in range(4 * m, 4 * m + 4):
                    turn_x(k)
            pe.wait_ge(hidden_ready, 3)
            pe.wait_ge(w_even_ready, 2)
            n = 0
            for j, start in enumerate(TOKEN_TILES):
                for part in range(2):
                    for half in range(2):
                        if n >= 2:
                            pe.wait_ge(taps_ready, n - 1)
                        pe.matmul(bank[4 + n % 2][:], hidden[:, start:start + 255:2],
                                  (w_even[:] if part == 0 else f_w_out[:, 1])[:, half * 512:half * 512 + 512],
                                  start=True, stop=True).then_inc(taps_raw, 1)
                        n += 1
            pe.wait_ge(x_ready, 8)
            pe.wait_ge(taps_ready, 16)
            pe.wait_ge(tap0_step, 2)
            n = 0
            for half in range(2):
                for m in range(2):
                    if n:
                        pe.wait_ge(spec_ready, 4 * n)
                    for part in range(2):
                        for odd in range(2):
                            ins = product(bank[2 + 2 * part + odd][:], [
                                (tab_s[:, 2 * odd + j, part, m * P:(m + 1) * P],
                                 taps[:, part, 2 * odd + j, half * 512:half * 512 + 512]) for j in range(2)])
                            ins.then_inc(spec_parts, 1)
                    n += 1
            pe.wait_ge(sum_ready, 8)
            token_means(sum_sq, mean_d).then_inc(mean_ready, 1)
            ada_column(0, ada_acc0[:, 0])
            ada_column(1, ada_acc0[:, 1])
            pe.wait_ge(rstd_ready, 1)
            spread().then_inc(rstd_spread, 1)
            pe.wait_ge(spec_ready, 16)

            def turn_values(h):
                pe.wait_ge(evicted[(5 * h + 1) % 2], (5 * h + 1) // 2 + 1)
                if h >= 2:
                    pe.wait_ge(far_copied, 3 * h - 5)
                for t in range(TT):
                    ins = pe.transpose(bank[4][:, t * P:(t + 1) * P], i_T[:, t * P:(t + 1) * P], ident[:])
                ins.then_inc(i_turned, 1)

            def own_scores(h):
                pe.wait_ge(own_ready, h + 1)
                if h:
                    pe.wait_ge(far_copied, 3 * h)
                for t in range(TT):
                    ins = pe.matmul(bank[2][:, t * P:(t + 1) * P], own[:, t * P:(t + 1) * P], ones[:],
                                    start=True, stop=True)
                ins.then_inc(level_scores, 1)

            def level(h, n):
                width = LEVELS[n]
                pe.wait_ge(keys_joined, 7 * h + n + 1)
                if n == 0:
                    pe.wait_ge(query_ready, 2 * h + 2)
                else:
                    pe.wait_ge(level_queries, 8 * h + n)
                    pe.wait_ge(diag_scores, 8 * h + n)
                for t in range(TT):
                    queries = view(QQ[h % 2], t * P, [2 * width, 64 // width], [L + width, 2], [1, width])
                    ins = pe.matmul(bank[3 - n % 2][:, t * P:(t + 1) * P], joined[n % 2][:, t * P:(t + 1) * P],
                                    queries, start=True, stop=True)
                ins.then_inc(level_scores, 1)

            def far_128(h):
                pe.wait_ge(level_keys, 8 * h + 7)
                pe.wait_ge(level_queries, 8 * h + 7)
                pe.wait_ge(values_ready, h + 2 if h + 1 < HEADS else HEADS)
                for n, (s, t, back) in enumerate(((0, 1, 0), (1, 0, 1), (2, 3, 0), (3, 2, 1))):
                    ins = pe.matmul(bank[4][:, n * P:(n + 1) * P], KK[h % 2][:, back, s * P:(s + 1) * P],
                                    QQ[h % 2][:, 1 - back, t * P:(t + 1) * P], start=True, stop=True)
                ins.then_inc(far_scores, 1)

            def far_256(h):
                pe.wait_ge(level_keys, 8 * h + 8)
                pe.wait_ge(level_queries, 8 * h + 8)
                pe.wait_ge(diag_scores, 8 * h + 8)
                for n in range(4):
                    back = n // 2
                    ins = pe.matmul(bank[2 + back][:, n % 2 * 256:n % 2 * 256 + 256],
                                    KK[h % 2][:, back, n * P:(n + 1) * P],
                                    QQ[h % 2][:, 1 - back, (1 - back) * 256:(1 - back) * 256 + 256],
                                    start=True, stop=True)
                    if n % 2:
                        ins.then_inc(far_scores, 1)

            def mix(h):
                pe.wait_ge(far_copied, 3 * h + 3)
                pe.wait_ge(diag_scores, 8 * h + 8)
                if h:
                    pe.wait_ge(normed_ready, h)
                product(bank[5][:], [(values[h % 2][:, t], scores[:, t]) for t in range(TT)]).then_inc(mixed, 1)

            def head_square(h):
                pe.wait_ge(mixed_sq, h + 1)
                if h:
                    pe.wait_ge(gated_ready, h)
                token_means(std, mean_head).then_inc(head_mean, 1)

            def spread_head(h):
                pe.wait_ge(head_rstd, h + 1)
                spread().then_inc(head_spread, 1)

            for g in range(HEADS + 1):
                h = g - 1
                places = {}

                def put(place, work):
                    places.setdefault(place, []).append(work)

                if h >= 0:
                    put(1 if g < HEADS else 0, lambda: own_scores(h))
                    for n in range(7):
                        put(3 * n + 2, lambda n=n: level(h, n))
                    for place, work in ((24, far_128), (28, far_256), (31, mix), (33, head_square), (36, spread_head)):
                        put(place, lambda work=work: work(h))
                if g >= 3 and g % 2:
                    put(0, lambda: ada_column(2 + (g - 3) // 2, ada_acc1[:, 0]))
                if g < HEADS:
                    places.setdefault(19, []).insert(0, lambda: turn_values(g))
                    if g == 0:
                        first_pair(0, a_hi, a_lo, a_hi_ready, a_lo_ready, 0)
                    for j in range(0 if g else 2, 5):
                        slab(5 * g + j, a_hi, a_lo, {k: places.get(8 * j + k, ()) for k in range(KT)})
                else:
                    tiles = [(S_HG_OUT + n, k) for k in range(KT - 1) for n in range(2)]
                    for place in range(40):
                        if place % 2 == 0 and tiles:
                            k_tile(*tiles.pop(0), h_hi, h_lo)
                        for work in places.get(place, ()):
                            work()
            pe.wait_ge(o_hi_ready, HEADS)
            pe.wait_ge(o_lo_ready, HEADS)
            for n in range(2):
                k_tile(S_HG_OUT + n, KT - 1, h_hi, h_lo)
            for n in range(2, KT):
                slab(S_HG_OUT + n, h_hi, h_lo)
                if n == 2:
                    ada_column(5, ada_acc1[:, 0])
            norm_mean(1)

            def chunk(i, s0, ch, with_ada):
                s = s0 + 16 * ch
                if isinstance(ch, int) and ch == 0:
                    first_pair(s, a_hi, a_lo, a_hi_ready, a_lo_ready, 8 * (2 * i + 1))
                else:
                    for n in range(2):
                        slab(s + n, a_hi, a_lo)
                    if with_ada:
                        ada_column(2 * ch + 5, ada_acc2[:, 1])
                for n in range(2, 8):
                    slab(s + n, a_hi, a_lo)
                first_pair(s + 8, h_hi, h_lo, h_hi_ready, h_lo_ready, 8 * ch + 8 * CHUNKS * i)
                if with_ada and not (isinstance(ch, int) and ch == CHUNKS - 1):
                    ada_column(2 * ch + 6, ada_acc2[:, 0])
                for n in range(2, 8):
                    slab(s + 8 + n, h_hi, h_lo)

            def mlp(i, s0, with_ada):
                chunk(i, s0, 0, with_ada)
                with pe.Fori(1, CHUNKS - 1 if with_ada else CHUNKS) as ch:
                    chunk(i, s0, At(ch), with_ada)
                if with_ada:
                    chunk(i, s0, CHUNKS - 1, with_ada)
                norm_mean(2 * i + 2)

            mlp(0, S_MLP0, True)

            def turn_z(g, n):
                pe.wait_ge(z_ready, 2 * g + n + 1)
                if g or n:
                    pe.wait_ge(z_t_ready, 2 * g + n)
                for j, start in enumerate(TOKEN_TILES):
                    ins = pe.transpose(bank[4][:, j * P:(j + 1) * P], z[n][:, start:start + 255:2], ident[:])
                ins.then_inc(z_turned, 1)

            def forward(g, m):
                if m == 0:
                    pe.wait_ge(z_t_ready, 2 * g + 2)
                if g == m == 0:
                    pe.wait_ge(tables_landed, 32)
                if g or m:
                    pe.wait_ge(z_even, 2 * g + m)
                    pe.wait_ge(Z_ready, 2 * (2 * g + m))
                for odd in range(2):
                    for part in range(2):
                        ins = product(bank[2 + odd][:, part * GC:(part + 1) * GC], [
                            (tab_f[:, 2 * odd + j, part, m * P:(m + 1) * P], z_t[g % 2][:, 2 * odd + j])
                            for j in range(2)])
                    ins.then_inc(z_parts, 1)

            def inverse(g, n):
                pe.wait_ge(folded_ready, 4 * g + 4)
                if g == 0 and n == 1:
                    pe.wait_ge(mod_ready, 12)
                if g:
                    pe.wait_ge(y_gated, 2 * g - 1 + n)
                for parity in range(2):
                    ins = product(bank[5 + n][:, parity * 256:parity * 256 + 256], [
                        (folded[:, m, parity, part, n * P:(n + 1) * P], tab_i[:, m, part, parity])
                        for m in range(2) for part in range(2)])
                ins.then_inc(y_ready, 1)

            for g in range(GROUPS + 1):
                h = g - 1
                places = {26: [lambda: turn_z(g, 0)], 43: [lambda: turn_z(g, 1)]}
                if h >= 0:
                    places |= {2: [lambda: forward(h, 0)], 12: [lambda: forward(h, 1)],
                               35: [lambda: inverse(h, 0)], 38: [lambda: inverse(h, 1)]}
                if g < GROUPS:
                    if g == 0:
                        first_pair(S_HY_IN, a_hi, a_lo, a_hi_ready, a_lo_ready, 16)
                    for j in range(0 if g else 2, 6):
                        slab(S_HY_IN + 6 * g + j, a_hi, a_lo, {k: places.get(8 * j + k, ()) for k in range(KT)})
                else:
                    tiles = [(S_HY_OUT + n, k) for k in range(KT - 2) for n in range(2)]
                    forward(h, 0)
                    pe.wait_ge(y_hi_ready, KT - 2)
                    pe.wait_ge(y_lo_ready, KT - 2)
                    for n in range(6):
                        k_tile(*tiles.pop(0), h_hi, h_lo)
                    forward(h, 1)
                    while tiles:
                        k_tile(*tiles.pop(0), h_hi, h_lo)
                    inverse(h, 0)
                    inverse(h, 1)
            for k in (KT - 2, KT - 1):
                pe.wait_ge(y_hi_ready, k + 1)
                pe.wait_ge(y_lo_ready, k + 1)
                for n in range(2):
                    k_tile(S_HY_OUT + n, k, h_hi, h_lo)
            for n in range(2, KT):
                slab(S_HY_OUT + n, h_hi, h_lo)
            norm_mean(3)
            mlp(1, S_MLP1, False)

            for k in range(KT):
                pe.wait_ge(final_ready, k + 1)
                if k >= 2:
                    pe.wait_ge(o_copied, k - 1)
                for t in range(TT):
                    ins = pe.transpose(bank[2 + k % 2][:, t * P:(t + 1) * P], tmp_b[:, k % 2, t * P:(t + 1) * P],
                                       ident[:])
                ins.then_inc(o_turned, 1)

        @block.scalar
        def _(act):
            def run(out_, in_, func, **kw):
                return nc.scalar.activation(out_, in_, func, **kw)

            def square_x(m, k):
                j = 8 * m + k
                if j >= 2:
                    act.wait_ge(sum_ready, j - 1)
                run(sq[:, k % 2], xT[:, k], ACT.Square).then_inc(sq_ready, 1)

            def norm_std(m):
                act.wait_ge(mean_ready, m + 1)
                run(std_cols[:], bank[7][:, 0:TT], ACT.Sqrt, bias=eps[:, 0:1]).then_inc(std_ready, 1)

            def norm_apply(m):
                for k in range(KT):
                    act.wait_ge(scaled_ready, 8 * m + k + 1)
                    run(a_hi[:, k], tmp_a[:, k % 2], ACT.Identity, bias=mod[:, 24 * m + k:24 * m + k + 1]).then_inc(a_hi_ready, 1)

            def evict_wait(s):
                act.wait_ge(slab_done, v(s + 1))

            act.wait_ge(params_ready, 1)
            run(c_sig[:], p_a[:, A_C:A_C + 8], ACT.Sigmoid).then_inc(c_sig_ready, 1)
            act.wait_ge(lb_step, 1)
            run(lb_tmp[:, 1], lb_tmp[:, 0], ACT.Exp).then_inc(lb_exp, 1)

            def sine(layer):
                act.wait_ge(angle_step, 6 * layer + 6)
                run(hidden, angle[:, 1], ACT.Sin).then_inc(hidden_ready, 1)

            def take_x(k):
                act.wait_ge(x_turned, k + 1)
                nc.scalar.copy(xT[:, k], bank[2 + k % 2][:]).then_inc(x_ready, 1)

            sine(0)
            for k in range(4):
                take_x(k)
            sine(1)
            for k in range(4, 8):
                take_x(k)
            sine(2)
            for j in range(4):
                if j >= 2:
                    act.wait_ge(taps_ready, 4 * (j - 1))
                run(decay[:, j % 2], rates, ACT.Exp, scale=minus_t[:, j:j + 1]).then_inc(decay_ready, 1)
            for k in range(KT):
                if k == 0:
                    act.wait_ge(x_ready, 8)
                    act.wait_ge(decay_ready, 4)
                square_x(0, k)
            for n in range(8):
                act.wait_ge(spec_parts, 4 * (n // 2) + 2 * (n % 2) + 1)
                if n >= 2:
                    act.wait_ge(spec_ready, 2 * (n - 1))
                nc.scalar.copy(even_s[:, n % 2], bank[2 + 2 * (n % 2)][:]).then_inc(spec_even, 1)
                if n % 2:
                    half, m = n // 4, n // 2 % 2
                    act.wait_ge(spec_ready, 2 * (n + 1))
                    for gg in range(2):
                        act.dma_start(spectrum[2 * half + gg, :, m],
                                      h_out[:, :, gg * GC:(gg + 1) * GC]).then_inc(spec_stored, 16)
            norm_std(0)
            act.wait_ge(gain_ready, 1)
            norm_apply(0)

            def query_input(g):
                s = 5 * g
                evict_wait(s)
                if g:
                    act.wait_ge(evicted[(s - 5) % 2], (s - 5) // 2 + 1)
                else:
                    act.wait_ge(spec_stored, 16 * 8)
                run(q_sig, bank[s % 2][:], ACT.Sigmoid).then_inc(q_sig_ready, 1)

            def value_input(g):
                s = 5 * g + 1
                evict_wait(s)
                if g:
                    act.wait_ge(i_turned, g)
                nc.scalar.copy(i_T[:], bank[s % 2][:]).then_inc(evicted[s % 2], 1)

            def forget_input(g, way):
                s, n = 5 * g + 2 + way, 2 * g + way
                evict_wait(s)
                if n:
                    act.wait_ge(gate_ready, 3 * g + (1 if way else 0))
                    act.wait_ge(key_ready, n)
                run(f_pos[:], bank[s % 2][:], ACT.Sigmoid).then_inc(f_pos_ready, 1)
                run(f_neg[:], bank[s % 2][:], ACT.Sigmoid, scale=-1.0).then_inc(evicted[s % 2], 1)

            def take_values(g):
                act.wait_ge(i_turned, g + 1)
                if g >= 2:
                    act.wait_ge(mixed, g - 1)
                nc.scalar.copy(values[g % 2][:], bank[4][:].rearrange("p (t n) -> p t n", t=TT)).then_inc(
                    values_ready, 1)

            def head_gate(g):
                s = 5 * g + 4
                evict_wait(s)
                if g:
                    act.wait_ge(evicted[(s - 5) % 2], (s - 5) // 2 + 1)
                run(g_sig, bank[s % 2][:], ACT.Sigmoid).then_inc(g_sig_ready, 1)

            def head_far(h):
                act.wait_ge(far_scores, 3 * h + 1)
                if h:
                    act.wait_ge(mixed, h)
                nc.scalar.copy(view(scores, P, [2 * L + 256, 2], [L - P, 2], [1, P]),
                               bank[4][:].rearrange("p (a b n) -> p a b n", a=2, b=2)).then_inc(far_copied, 1)
                for back in range(2):
                    act.wait_ge(far_scores, 3 * h + 2 + back)
                    nc.scalar.copy(view(scores, 256 if back == 0 else 2 * L, [L, 2], [1, 256]),
                                   bank[2 + back][:].rearrange("p (a n) -> p a n", a=2)).then_inc(far_copied, 1)

            def head_square(h):
                act.wait_ge(mixed, h + 1)
                if h:
                    act.wait_ge(head_mean, h)
                run(std[:], bank[5][:], ACT.Square).then_inc(mixed_sq, 1)

            def head_std_cols(h):
                act.wait_ge(head_mean, h + 1)
                if h:
                    act.wait_ge(head_rstd, h)
                run(std_cols[:], bank[7][:, 0:TT], ACT.Sqrt, bias=eps[:, 0:1]).then_inc(head_std, 1)

            def head_split(h):
                act.wait_ge(gated_ready, h + 1)
                nc.scalar.copy(h_hi[:, h], tmp_b[:, h % 2]).then_inc(o_hi_ready, 1)

            def join_keys(h, n):
                if n == 0:
                    act.wait_ge(key_ready, 2 * h + 2)
                else:
                    act.wait_ge(level_keys, 8 * h + n)
                if h or n >= 2:
                    act.wait_ge(level_scores, 8 * h + (n if n >= 2 else 0))
                width = LEVELS[n]
                nc.scalar.copy(joined[n % 2].rearrange("p (a b n) -> p a b n", b=2, n=width),
                               view(KK[h % 2], 0, [2 * width, 256 // width], [L + width, 2], [1, width])).then_inc(
                    keys_joined, 1)

            def join_levels(g, first, last):
                if g:
                    for n in range(first, last):
                        join_keys(g - 1, n)

            for g in range(HEADS + 1):
                join_levels(g, 0, 3)
                if g < HEADS:
                    query_input(g)
                join_levels(g, 3, 5)
                if g < HEADS:
                    value_input(g)
                join_levels(g, 5, 7)
                if g < HEADS:
                    forget_input(g, 0)
                    take_values(g)
                if g:
                    head_far(g - 1)
                    head_square(g - 1)
                if g < HEADS:
                    forget_input(g, 1)
                if g:
                    head_std_cols(g - 1)
                    head_split(g - 1)
                if g < HEADS:
                    head_gate(g)

            def norm(m, s0):
                for n in range(KT):
                    s = s0 + n
                    act.wait_ge(evicted[s % 2], s // 2 + 1)
                    square_x(m, n)
                norm_std(m)
                if m < 4:
                    act.wait_ge(gain_ready, m + 1)
                    norm_apply(m)

            norm(1, S_HG_OUT)

            def mlp(i, s0):
                with act.Fori(0, CHUNKS) as chunk:
                    for n in range(8):
                        s, j = At(chunk, 16, s0 + n), At(chunk, 8, 8 * CHUNKS * i + n)
                        evict_wait(s)
                        if n >= 2 or i:
                            act.wait_ge(h_hi_ready, v(j - 1))
                        run(tmp_a[:, n % 2], bank[s % 2][:], ACT.Relu).then_inc(evicted[s % 2], 1)
                        act.wait_ge(evicted[s % 2], v(s // 2 + 1))
                        if n >= 2 or i:
                            act.wait_ge(h_lo_ready, v(j - 1))
                        run(tmp_b[:, n % 2], tmp_a[:, n % 2], ACT.Square).then_inc(relu_sq_ready, 1)
                norm(2 * i + 2, s0 + 16 * CHUNKS - 8)

            mlp(0, S_MLP0)

            def take_z(g, n):
                act.wait_ge(z_turned, 2 * g + n + 1)
                if g >= 2:
                    act.wait_ge(z_parts, 4 * (g - 1))
                nc.scalar.copy(z_t[g % 2][:, :, n * P:(n + 1) * P],
                               bank[4][:].rearrange("p (j n) -> p j n", j=4)).then_inc(z_t_ready, 1)

            def even_part(h, m):
                act.wait_ge(z_parts, 2 * (2 * h + m) + 1)
                if h or m:
                    act.wait_ge(Z_ready, 2 * (2 * h + m))
                nc.scalar.copy(even_z, bank[2][:].rearrange("p (a n) -> p a n", a=2)).then_inc(z_even, 1)

            def y_high(h, n):
                act.wait_ge(y_gated, 2 * h + n + 1)
                nc.scalar.copy(h_hi[:, 2 * h + n], tmp_b[:, n]).then_inc(y_hi_ready, 1)

            act.wait_ge(pad_set, 3)
            for g in range(GROUPS + 1):
                for j in range(6 if g < GROUPS else 0):
                    s = S_HY_IN + 6 * g + j
                    seg, n = HY_ORDER[j]
                    evict_wait(s)
                    act.wait_ge(group_ready, g + 1)
                    prior = 6 * g + (-4, -4, 0, 1, -1, 4)[j]
                    if prior >= 0:
                        act.wait_ge(conv_step, 3 * (prior + 1))
                    run(padded[seg][:, 1:L + 1], bank[s % 2][:], ACT.Identity,
                        bias=group_params[g % 2][:, 3, seg, n:n + 1]).then_inc(evicted[s % 2], 1)
                    if g and j == 0:
                        even_part(g - 1, 0)
                    if g and j == 2:
                        even_part(g - 1, 1)
                    if j == 3:
                        take_z(g, 0)
                    if g and j == 5:
                        y_high(g - 1, 0)
                        y_high(g - 1, 1)
                    if j == 5:
                        take_z(g, 1)
                if g == GROUPS:
                    even_part(g - 1, 0)
                    even_part(g - 1, 1)
                    y_high(g - 1, 0)
                    y_high(g - 1, 1)
            norm(3, S_HY_OUT)
            mlp(1, S_MLP1)
            for k in range(KT):
                act.wait_ge(o_turned, k + 1)
                nc.scalar.copy(o_nat[:, :, k * P:(k + 1) * P],
                               bank[2 + k % 2][:].rearrange("p (t n) -> p t n", t=TT)).then_inc(o_copied, 1)

        @block.vector
        def _(dve):
            tt, ts, stt = nc.vector.tensor_tensor, nc.vector.tensor_scalar, nc.vector.scalar_tensor_tensor

            def ada_piece(q, buffer, acc, first):
                c, k = q // 8, q % 8
                slots, accs = buffer[:].shape[1], acc[:].shape[1]
                dve.wait_ge(ada_landed[k], v((c + 1) * 16))
                if q >= 1:
                    dve.wait_ge(ada_summed, v(q))
                if k == 0 and c >= first // 8 + accs:
                    dve.wait_ge(ada_columns, v(c - accs + 1))
                w, total = buffer[:, (q - first) % slots], acc[:, c % accs]
                if k == 0:
                    ins = ts(total, w, c_silu[:, 0:1], None, ALU.mult)
                else:
                    ins = stt(out=total, in0=w, scalar=c_silu[:, k:k + 1], in1=total, op0=ALU.mult, op1=ALU.add)
                ins.then_inc(ada_summed, 1)

            def take_mod(c):
                dve.wait_ge(ada_columns, v(c + 1))
                tt(mod[:, bass.ds(v(8 * c), 8)], bank[6][:, 0:8], p_a[:, bass.ds(v(8 * c + A_ADA_B), 8)],
                   ALU.add).then_inc(mod_ready, 1)

            def make_gain(m):
                dve.wait_ge(mod_ready, 3 * m + 2)
                stt(out=gain[:, m], in0=mod[:, 24 * m + 8:24 * m + 16], scalar=1.0,
                    in1=p_b[:, B_NORM_G + 8 * m:B_NORM_G + 8 * m + 8], op0=ALU.add, op1=ALU.mult).then_inc(
                    gain_ready, 1)

            def add_square(m, k):
                dve.wait_ge(sq_ready, 8 * m + k + 1)
                if k == 0:
                    ins = nc.vector.tensor_copy(sum_sq[:], sq[:, 0])
                else:
                    dve.wait_ge(sum_ready, 8 * m + k)
                    ins = tt(sum_sq[:], sum_sq[:], sq[:, k % 2], ALU.add)
                ins.then_inc(sum_ready, 1)

            def norm_rstd(m):
                dve.wait_ge(std_ready, m + 1)
                nc.vector.reciprocal(rstd_cols[:], std_cols[:]).then_inc(rstd_ready, 1)
                if m < 4:
                    make_gain(m)
                dve.wait_ge(rstd_spread, m + 1)

            def norm_apply(m):
                def scale(k):
                    j = 8 * m + k
                    if k >= 2:
                        dve.wait_ge(a_hi_ready, j - 1)
                        dve.wait_ge(a_lo_ready, j - 1)
                    stt(out=tmp_a[:, k % 2], in0=xT[:, k], scalar=gain[:, m, k:k + 1], in1=bank[7][:],
                        op0=ALU.mult, op1=ALU.mult).then_inc(scaled_ready, 1)

                def low(k):
                    dve.wait_ge(a_hi_ready, 8 * m + k + 1)
                    stt(out=a_lo[:, k], in0=tmp_a[:, k % 2], scalar=mod[:, 24 * m + k:24 * m + k + 1], in1=a_hi[:, k].bitcast(F32),
                        op0=ALU.add, op1=ALU.subtract).then_inc(a_lo_ready, 1)

                dve.wait_ge(gain_ready, m + 1)
                scale(0)
                for k in range(KT):
                    if k + 1 < KT:
                        scale(k + 1)
                    low(k)

            for n, (tile, value) in enumerate(((ones, 1.0), (mean_d, 1.0 / D), (mean_head, 1.0 / P), (eps, EPS))):
                nc.vector.memset(tile[:], value).then_inc(consts_set, 1)
            dve.wait_ge(filt_landed, 16 * 8)
            nc.vector.memset(lb_tmp[:], 0.0).then_inc(consts_set, 1)
            for n, dst in enumerate((p_a, p_b, p_c, p_d)):
                dve.wait_ge(rows_turned, n + 1)
                w, r = dst[:].shape
                nc.vector.tensor_copy(dst[:], bank[2 + n][0:w, 0:r]).then_inc(params_ready, 1)
            dve.wait_ge(params_ready, 4)
            dve.wait_ge(consts_set, 5)
            bounds = p_b[:, B_LOWER:B_LOWER + 16]
            tt(lb_tmp[:, 0], bounds, bounds, ALU.subtract).then_inc(lb_step, 1)
            dve.wait_ge(c_sig_ready, 1)
            tt(c_silu[:], p_a[:, A_C:A_C + 8], c_sig[:], ALU.mult).then_inc(c_silu_ready, 1)
            dve.wait_ge(lb_exp, 1)
            nc.vector.reciprocal(lb_tmp[:, 2], lb_tmp[:, 1]).then_inc(lb_step, 1)
            dve.wait_ge(lb_step, 2)
            tt(lb_tmp[:, 3], lb_tmp[:, 1], lb_tmp[:, 2], ALU.mult).then_inc(lb_step, 1)
            dve.wait_ge(lb_step, 3)
            tt(lb[:], lb_tmp[:, 3], lb_tmp[:, 3], ALU.subtract).then_inc(lb_step, 1)
            dve.wait_ge(lb_step, 4)
            ts(one_m_lb[:], lb[:], -1.0, 1.0, ALU.mult, ALU.add).then_inc(lb_step, 1)
            dve.wait_ge(c_silu_ready, 1)
            tt(w_even[:], f_w_out[:, 0], f_w_out[:, 1], ALU.add).then_inc(w_even_ready, 1)
            dve.wait_ge(w_even_ready, 1)
            tt(f_w_out[:, 1], f_w_out[:, 0], f_w_out[:, 1], ALU.subtract).then_inc(w_even_ready, 1)

            def reduce_angle(layer):
                dve.wait_ge(pre_sine, layer + 1)
                n = 6 * layer
                steps = (
                    lambda: ts(angle[:, 0], bank[4][0:FW], p_d[:, layer:layer + 1], p_d[:, 3:4], ALU.add, ALU.mult),
                    lambda: ts(turns[0], angle[:, 0], 1.0 / (2.0 * math.pi), ROUNDER, ALU.mult, ALU.add),
                    lambda: ts(turns[1], turns[0], ROUNDER, None, ALU.subtract),
                    lambda: stt(out=angle[:, 1], in0=turns[1], scalar=-TWO_PI_HIGH, in1=angle[:, 0],
                                op0=ALU.mult, op1=ALU.add),
                    lambda: stt(out=turns[0], in0=turns[1], scalar=-TWO_PI_LOW,
                                in1=angle[:, 1], op0=ALU.mult, op1=ALU.add),
                    lambda: ts(angle[:, 1], turns[0], 3.1415925, -3.1415925, ALU.min, ALU.max),
                )
                for step in steps:
                    if n:
                        dve.wait_ge(angle_step, n)
                    step().then_inc(angle_step, 1)
                    n += 1

            q = 0
            for layer in range(3):
                if layer:
                    dve.wait_ge(hidden_ready, layer)
                reduce_angle(layer)
                for _ in range(2):
                    ada_piece(q, ada_w0, ada_acc0, 0)
                    q += 1
            n = 0
            for j in range(4):
                dve.wait_ge(decay_ready, j + 1)
                for part in range(2):
                    for half in range(2):
                        dve.wait_ge(taps_raw, n + 1)
                        cols = slice(half * 512, half * 512 + 512)
                        tt(taps[:, part, j, cols], bank[4 + n % 2][:], decay[:, j % 2, cols],
                           ALU.mult).then_inc(taps_ready, 1)
                        n += 1
                for _ in range(2):
                    ada_piece(q, ada_w0, ada_acc0, 0)
                    q += 1
            dve.wait_ge(taps_ready, 16)
            tt(taps0, taps[0:1, 0, 0], taps[0:1, 1, 0], ALU.add).then_inc(tap0_step, 1)
            dve.wait_ge(tap0_step, 1)
            stt(out=taps[0:1, 0, 0], in0=taps0, scalar=0.5, in1=skip_row[:], op0=ALU.mult,
                op1=ALU.add).then_inc(tap0_step, 1)
            def spectrum_quarter(quarter):
                for part in range(2):
                    dve.wait_ge(spec_even, 2 * quarter + part + 1)
                    dve.wait_ge(spec_parts, 4 * quarter + 2 * part + 2)
                    if quarter and part == 0:
                        dve.wait_ge(spec_stored, 32 * quarter)
                    for minus in range(2):
                        tt(h_out[:, 2 * minus + part], even_s[:, part], bank[3 + 2 * part][:],
                           ALU.subtract if minus else ALU.add).then_inc(spec_ready, 1)

            for quarter in range(4):
                spectrum_quarter(quarter)
                if q < 16:
                    ada_piece(q, ada_w0, ada_acc0, 0)
                    q += 1
            while q < 16:
                ada_piece(q, ada_w0, ada_acc0, 0)
                q += 1
            take_mod(0)
            take_mod(1)
            norm_rstd(0)
            norm_apply(0)

            def q_input(g):
                s = 5 * g
                dve.wait_ge(q_sig_ready, g + 1)
                tt(q_silu[:], bank[s % 2][:], q_sig, ALU.mult).then_inc(evicted[s % 2], 1)
                dve.wait_ge(evicted[s % 2], s // 2 + 1)

            def gate_input(g, way):
                s, b, col = 5 * g + 2 + way, g % 2, 8 * way + g
                if way == 0 and g >= 2:
                    dve.wait_ge(far_scores, 3 * (g - 1))
                    dve.wait_ge(level_scores, 8 * (g - 1))
                dve.wait_ge(f_pos_ready, 2 * g + way + 1)
                for place in ((1,) if way == 0 else (0, 2)):
                    ts(gates[:, place], f_pos[:], one_m_lb[:, col:col + 1], lb[:, col:col + 1], ALU.mult,
                       ALU.add).then_inc(gate_ready, 1)
                dve.wait_ge(evicted[s % 2], s // 2 + 1)
                ts(KK[b][:, way], f_neg[:], one_m_lb[:, col:col + 1], None, ALU.mult).then_inc(key_ready, 1)
                dve.wait_ge(gate_ready, 3 * g + (1 if way == 0 else 3))
                tt(QQ[b][:, 1 - way], q_silu[:], gates[:, 1 if way == 0 else 0],
                   ALU.mult).then_inc(query_ready, 1)

            def own_input(g):
                b = g % 2
                dve.wait_ge(key_ready, 2 * g + 2)
                tt(tmp_a[:, 0], KK[b][:, 0], KK[b][:, 1], ALU.add).then_inc(own_sum_ready, 1)
                dve.wait_ge(own_sum_ready, g + 1)
                if g:
                    dve.wait_ge(level_scores, 8 * g - 7)
                tt(own[:], q_silu[:], tmp_a[:, 0], ALU.mult).then_inc(own_ready, 1)

            def gate_output(g):
                s = 5 * g + 4
                dve.wait_ge(g_sig_ready, g + 1)
                stt(out=out_gate[:], in0=bank[s % 2][:], scalar=p_b[:, B_HEAD_G:B_HEAD_G + 1], in1=g_sig,
                    op0=ALU.mult, op1=ALU.mult).then_inc(evicted[s % 2], 1)
                dve.wait_ge(evicted[s % 2], s // 2 + 1)

            diag = view(scores, 0, [L + P, TT], [1, P])

            def take_level(h, n):
                dve.wait_ge(level_scores, 8 * h + n + 1)
                if n == 0:
                    if h:
                        dve.wait_ge(mixed, h)
                    ins = nc.vector.tensor_copy(diag, bank[2][:].rearrange("p (t n) -> p t n", t=TT))
                else:
                    dve.wait_ge(diag_scores, 8 * h + n)
                    m = view(mask, (n - 1) * P, [0, TT], [1, P])
                    ins = nc.vector.copy_predicated(diag, m,
                                                    bank[3 - (n - 1) % 2][:].rearrange("p (t n) -> p t n", t=TT))
                ins.then_inc(diag_scores, 1)

            def carry(h, n):
                b = h % 2
                width = 1 << n
                blocks = L // width
                t = gates if n == 0 else block_gates[width]
                if n:
                    dve.wait_ge(level_gates, 7 * h + n)
                    dve.wait_ge(level_keys, 8 * h + n)
                    dve.wait_ge(level_queries, 8 * h + n)
                if n == 7:
                    dve.wait_ge(far_scores, 3 * h + 1)
                else:
                    dve.wait_ge(keys_joined, 7 * h + n + 1)
                dims = ([2 * width, 256 // width], [L + width, 2], [1, width])
                gate_dims = ([2, 256 // width], [blocks - 1, 2], [0, width])
                tt(view(KK[b], 0, *dims), view(KK[b], 0, *dims), view(t, blocks + 1, *gate_dims),
                   ALU.mult).then_inc(level_keys, 1)
                if n < 7:
                    dve.wait_ge(level_scores, 8 * h + n + 2)
                tt(view(QQ[b], 0, *dims), view(QQ[b], 0, *dims), view(t, 1, *gate_dims),
                   ALU.mult).then_inc(level_queries, 1)
                if n < 7:
                    tt(block_gates[2 * width][:], t[:, :, 0:blocks:2], t[:, :, 1:blocks:2],
                       ALU.mult).then_inc(level_gates, 1)

            def head_output(h, g):
                dve.wait_ge(mixed_sq, h + 1)
                tt(tmp_a[:, 1], bank[5][:], out_gate[:], ALU.mult).then_inc(normed_ready, 1)
                dve.wait_ge(head_std, h + 1)
                nc.vector.reciprocal(rstd_cols[:], std_cols[:]).then_inc(head_rstd, 1)
                if g < HEADS:
                    gate_input(g, 1)
                    own_input(g)
                dve.wait_ge(normed_ready, h + 1)
                dve.wait_ge(head_spread, h + 1)
                tt(tmp_b[:, h % 2], tmp_a[:, 1], bank[7][:], ALU.mult).then_inc(gated_ready, 1)
                dve.wait_ge(gated_ready, h + 1)
                if g < HEADS:
                    gate_output(g)
                dve.wait_ge(o_hi_ready, h + 1)
                tt(h_lo[:, h], tmp_b[:, h % 2], h_hi[:, h].bitcast(F32), ALU.subtract).then_inc(o_lo_ready, 1)

            dve.wait_ge(mask_landed, 16)
            dve.wait_ge(spec_stored, 16 * 8)
            nc.vector.tensor_copy(mask[:].rearrange("p l n -> p (l n)"),
                                  scores[:, 0:2].rearrange("p a n -> p (a n)")[:, 0:len(LEVELS) * P]).then_inc(
                mask_set, 1)
            dve.wait_ge(mask_set, 1)
            for g in range(HEADS + 1):
                h = g - 1
                if h < 0:
                    q_input(g)
                    gate_input(g, 0)
                    gate_input(g, 1)
                    own_input(g)
                    gate_output(g)
                    continue
                if g >= 3 and g % 2:
                    take_mod(2 + (g - 3) // 2)
                for n in range(8):
                    if n:
                        carry(h, n - 1)
                    take_level(h, n)
                    if n == 3 and g < HEADS:
                        q_input(g)
                    if n in (3, 4, 5, 7):
                        ada_piece(16 + 4 * h + (3, 4, 5, 7).index(n), ada_w1, ada_acc1, 16)
                if g < HEADS:
                    gate_input(g, 0)
                carry(h, 7)
                head_output(h, g)

            def residual(m, s, n):
                dve.wait_ge(slab_done, v(s + 1))
                stt(out=xT[:, n], in0=bank[s % 2][:], scalar=mod[:, 24 * m + 16 + n:24 * m + 17 + n], in1=xT[:, n],
                    op0=ALU.mult, op1=ALU.add).then_inc(evicted[s % 2], 1)

            def norm(m, gate, s0):
                for n in range(KT):
                    residual(gate, s0 + n, n)
                    if n:
                        add_square(m, n - 1)
                    if m == 1 and n == 3:
                        take_mod(5)
                add_square(m, 7)
                norm_rstd(m)
                if m < 4:
                    norm_apply(m)

            norm(1, 0, S_HG_OUT)

            def chunk(i, s0, ch, first, last, with_ada):
                for n in range(8):
                    s, j = 16 * ch + (s0 + n), 8 * ch + (8 * CHUNKS * i + n)
                    dve.wait_ge(evicted[s % 2], v(s // 2 + 1))
                    r = tmp_a[:, n % 2]
                    tt(h_hi[:, n], r, r, ALU.mult).then_inc(h_hi_ready, 1)
                    dve.wait_ge(h_hi_ready, v(j + 1))
                    dve.wait_ge(relu_sq_ready, v(j + 1))
                    tt(h_lo[:, n], tmp_b[:, n % 2], h_hi[:, n].bitcast(F32), ALU.subtract).then_inc(h_lo_ready, 1)
                    if with_ada and not first and n == 2:
                        take_mod(2 * ch + 5)
                    if with_ada and not last:
                        ada_piece(16 * ch + (48 + n), ada_w2, ada_acc2, 48)
                for n in range(8):
                    residual(2 * i + 1, 16 * ch + (s0 + 8 + n), n)
                    if last and n:
                        add_square(2 * i + 2, n - 1)
                    if with_ada and not last:
                        if n == 2:
                            take_mod(2 * ch + 6)
                        ada_piece(16 * ch + (56 + n), ada_w2, ada_acc2, 48)

            def mlp(i, s0, with_ada):
                chunk(i, s0, 0, True, False, with_ada)
                with dve.Fori(1, CHUNKS - 1) as ch:
                    chunk(i, s0, At(ch), False, False, with_ada)
                chunk(i, s0, CHUNKS - 1, False, True, with_ada)
                m = 2 * i + 2
                add_square(m, 7)
                norm_rstd(m)
                if m < 4:
                    norm_apply(m)

            mlp(0, S_MLP0, True)

            for seg in range(3):
                nc.vector.memset(view(padded[seg], 0, [L + 1, 2]), 0.0).then_inc(pad_set, 1)

            def convolve(g, j):
                s = S_HY_IN + 6 * g + j
                seg, n = HY_ORDER[j]
                par = group_params[g % 2]
                dst = x0[:, n] if seg == 0 else conv[seg - 1][:]
                dve.wait_ge(evicted[s % 2], s // 2 + 1)
                if seg and 2 * g + n:
                    dve.wait_ge(z_ready, 2 * g + n)
                if seg == 0 and g:
                    dve.wait_ge(y_gated, 2 * g - 1 + n)
                c0 = 3 * (6 * g + j)
                ts(dst, padded[seg][:, 0:L], par[:, 0, seg, n:n + 1], par[:, 4, seg, n:n + 1], ALU.mult,
                   ALU.add).then_inc(conv_step, 1)
                for tap in (1, 2):
                    dve.wait_ge(conv_step, c0 + tap)
                    stt(out=dst, in0=padded[seg][:, tap:tap + L], scalar=par[:, tap, seg, n:n + 1], in1=dst,
                        op0=ALU.mult, op1=ALU.add).then_inc(conv_step, 1)
                dve.wait_ge(conv_step, c0 + 3)

            def make_z(g, n):
                if g:
                    dve.wait_ge(z_turned, 2 * g + n - 1)
                tt(z[n][:], conv[0][:], conv[1][:], ALU.mult).then_inc(z_ready, 1)

            def spectral(h, m):
                n = 2 * h + m
                dve.wait_ge((H_landed0, H_landed1)[m], 16 * (h + 1))
                dve.wait_ge(z_even, n + 1)
                dve.wait_ge(z_parts, 2 * n + 2)
                odd = bank[3][:].rearrange("p (a n) -> p a n", a=2)
                tt(Z[:, 0:2], even_z, odd, ALU.add).then_inc(Z_ready, 1)
                tt(Z[:, 2:4], even_z, odd, ALU.subtract).then_inc(Z_ready, 1)
                dve.wait_ge(Z_ready, 2 * n + 2)
                tt(ZH[:], Z, H[m][:], ALU.mult).then_inc(ZH_ready, 1)
                dve.wait_ge(ZH_ready, 2 * n + 1)
                tt(Y[:, 0:4:2], ZH[:, 0:4:2], ZH[:, 1:4:2], ALU.subtract).then_inc(Y_ready, 1)
                dve.wait_ge(Y_ready, 2 * n + 1)
                swapped = view(H[m], GC, [2 * GC, 2], [-GC, 2], [1, GC])
                tt(ZH[:].rearrange("p (a b) n -> p a b n", a=2), Z.rearrange("p (a b) n -> p a b n", a=2), swapped,
                   ALU.mult).then_inc(ZH_ready, 1)
                dve.wait_ge(ZH_ready, 2 * n + 2)
                tt(Y[:, 1:4:2], ZH[:, 0:4:2], ZH[:, 1:4:2], ALU.add).then_inc(Y_ready, 1)
                dve.wait_ge(Y_ready, 2 * n + 2)
                if h and m == 0:
                    dve.wait_ge(y_ready, 2 * h)
                tt(folded[:, m, 0], Y[:, 0:2], Y[:, 2:4], ALU.add).then_inc(folded_ready, 1)
                tt(folded[:, m, 1], Y[:, 0:2], Y[:, 2:4], ALU.subtract).then_inc(folded_ready, 1)

            def gate_y(h, n):
                dve.wait_ge(y_ready, 2 * h + n + 1)
                by_parity = [[1, 2], [2, 256]]
                tt(view(tmp_b, n * L, *by_parity), bank[5 + n][:].rearrange("p (a n) -> p a n", a=2),
                   view(x0, n * L, *by_parity), ALU.mult).then_inc(y_gated, 1)

            def low_y(h, n):
                dve.wait_ge(y_gated, 2 * h + n + 1)
                dve.wait_ge(y_hi_ready, 2 * h + n + 1)
                k = 2 * h + n
                tt(h_lo[:, k], tmp_b[:, n], h_hi[:, k].bitcast(F32), ALU.subtract).then_inc(y_lo_ready, 1)

            for g in range(GROUPS + 1):
                h = g - 1
                if g < GROUPS:
                    nc.vector.tensor_copy(group_params[g % 2][:],
                                          view(p_c, 2 * g, [24, 5], [8, 3], [1, 2])).then_inc(group_ready, 1)
                    dve.wait_ge(group_ready, g + 1)
                    convolve(g, 0)
                    if g:
                        spectral(h, 0)
                    convolve(g, 1)
                    make_z(g, 0)
                    convolve(g, 2)
                    if g:
                        spectral(h, 1)
                    convolve(g, 3)
                    make_z(g, 1)
                    if g:
                        gate_y(h, 0)
                        gate_y(h, 1)
                    convolve(g, 4)
                    convolve(g, 5)
                    if g:
                        low_y(h, 0)
                        low_y(h, 1)
                else:
                    spectral(h, 0)
                    spectral(h, 1)
                    gate_y(h, 0)
                    gate_y(h, 1)
                    low_y(h, 0)
                    low_y(h, 1)
            norm(3, 2, S_HY_OUT)
            mlp(1, S_MLP1, False)

            for k in range(KT):
                if k >= 2:
                    dve.wait_ge(o_turned, k - 1)
                stt(out=tmp_b[:, k % 2], in0=xT[:, k], scalar=p_b[:, B_FINAL_G + k:B_FINAL_G + k + 1],
                    in1=bank[7][:], op0=ALU.mult, op1=ALU.mult).then_inc(final_ready, 1)


INPUTS = ["x", "c", "ada_w", "ada_b", "norm_g", "hg_w_in", "hg_lower_bounds", "hg_norm_g", "hg_w_out",
          "hy_w_in", "hy_b_in", "hy_conv_w", "hy_conv_b", "hy_filt_w_in", "hy_filt_w_mid", "hy_filt_b",
          "hy_filt_freq", "hy_filt_w_out", "hy_skip", "hy_w_out", "mlp_w1", "mlp_w2", "final_g"]


def kernel(**inputs):
    import concourse.bacc as bacc
    from concourse.bass_utils import run_bass_kernel_spmd

    nc = bacc.Bacc("TRN2", target_bir_lowering=False, num_devices=1)
    arrays = {name: np.ascontiguousarray(inputs[name]) for name in INPUTS}
    forward, inverse = transform_tables()
    emb_t, rates, times = filter_constants()
    arrays |= {"fwd_table": forward, "inv_table": inverse, "emb_t": emb_t, "decay_rates": rates,
               "minus_times": times, "masks": level_masks(), "identity": np.eye(P, dtype=np.float32)}
    tensors = [nc.dram_tensor(n, a.shape, mybir.dt.from_np(a.dtype), kind="ExternalInput").ap()
               for n, a in arrays.items()]
    out = nc.dram_tensor("out", (1, L, D), F32, kind="ExternalOutput").ap()
    hybrid_encoder(nc, *tensors, out)
    result = run_bass_kernel_spmd(nc, [arrays], core_ids=[0])
    return result.results[0]["out"]
```

```python
import math
from contextlib import ExitStack

import numpy as np

import concourse.bass as bass
from concourse import mybir

F32 = mybir.dt.float32
F32R = mybir.dt.float32r
U8 = mybir.dt.uint8
ALU = mybir.AluOpType
ACT = mybir.ActivationFunctionType

P = 128
D = 1024
L = 512
KT = D // P
TT = L // P
HEADS = 8
D_FF = 4 * D
CHUNKS = D_FF // D
EPS = 1e-6
FW = 64
EMB = 33
BANDS = (EMB - 1) // 2
LEVELS = [1 << n for n in range(7)]
GROUPS = 4
GC = D // GROUPS
FT = L // 4 // P * 2

S_HG_IN = 0
S_HG_OUT = S_HG_IN + 5 * HEADS
S_MLP0 = S_HG_OUT + KT
S_HY_IN = S_MLP0 + 16 * CHUNKS
S_HY_OUT = S_HY_IN + 6 * GROUPS
S_MLP1 = S_HY_OUT + KT
N_SLABS = S_MLP1 + 16 * CHUNKS
STAGE_SLOTS = 6

HY_ORDER = ((1, 0), (2, 0), (1, 1), (2, 1), (0, 0), (0, 1))

TOKEN_TILES = [0, 256, 1, 257]

A_C, A_ADA_B = 0, 8
B_NORM_G, B_FINAL_G, B_LOWER, B_HEAD_G = 0, 32, 40, 56
TWO_PI_HIGH = 6.28125
SPEC_BANKS = ((2, 3), (4, 5), (0, 1))
TWO_PI_LOW = 2.0 * math.pi - TWO_PI_HIGH
ROUNDER = 12582912.0


class At:

    def __init__(self, i, k=1, c=0):
        self.i, self.k, self.c = i, k, c

    def __add__(self, n):
        return At(self.i, self.k, self.c + n)

    def __sub__(self, n):
        return self + -n

    def __mul__(self, n):
        return At(self.i, self.k * n, self.c * n)

    def __floordiv__(self, n):
        assert self.k % n == 0
        return At(self.i, self.k // n, self.c // n)

    def __mod__(self, n):
        assert self.k % n == 0
        return self.c % n

    def __lt__(self, n):
        return n == HEADS

    def __ge__(self, n):
        assert self.c >= n or self.c + self.k >= n
        return True

    __radd__, __rmul__ = __add__, __mul__


def v(x):
    return x.i * x.k + x.c if isinstance(x, At) else x


def view(tile, offset, *dims):
    whole = tile[:]
    return bass.AP(tensor=whole.tensor, offset=offset, ap=[list(whole.ap[0])] + [list(d) for d in dims])


def one_row(tile, index):
    return tile[:, bass.ds(v(index), 1)].rearrange("p a n -> p (a n)")


def transform_tables():
    p = np.arange(P)
    omega = np.pi * (2 * np.arange(256) + 1) / 1024
    forward = np.zeros((P, 4, 2, 256))
    for j, start in enumerate(TOKEN_TILES):
        phase = (start + 2 * p)[:, None] * omega[None]
        forward[:, j, 0], forward[:, j, 1] = np.cos(phase), np.sin(phase)
    inverse = np.zeros((P, 2, 2, 2, 256))
    for m in range(2):
        for parity in range(2):
            phase = omega[m * P + p][:, None] * (parity + 2 * np.arange(256))[None]
            inverse[:, m, 0, parity], inverse[:, m, 1, parity] = np.cos(phase) / 512, np.sin(phase) / 512
    return forward.astype(np.float32), inverse.astype(np.float32)


def filter_constants():
    f = np.float32
    t = np.linspace(0.0, 1.0, L, dtype=f)[:, None]
    bands = np.linspace(1e-4, BANDS - 1.0, BANDS, dtype=f)
    ang = f(2.0 * math.pi / L) * np.arange(L, dtype=f)[:, None] * bands
    emb = np.concatenate([t, np.cos(ang), -np.sin(ang)], axis=-1).astype(f)
    rates = np.abs(np.linspace(math.log(1e-2) / 1.5, math.log(1e-2) / 0.3, D, dtype=f))
    times = np.stack([-t[start + 2 * np.arange(P), 0] for start in TOKEN_TILES], axis=1)
    emb = np.concatenate([emb[0::2], emb[1::2]])
    return np.ascontiguousarray(emb.T), rates, np.ascontiguousarray(times.astype(f))


def level_masks():
    s, t = np.arange(P)[:, None], np.arange(P)[None]
    return np.stack([((s // (2 * h)) == (t // (2 * h))) & ((s // h) != (t // h)) for h in LEVELS],
                    axis=1).astype(np.float32)


def hybrid_encoder(nc, x, c, ada_w, ada_b, norm_g, hg_w_in, hg_lower_bounds, hg_norm_g, hg_w_out,
                   hy_w_in, hy_b_in, hy_conv_w, hy_conv_b, hy_filt_w_in, hy_filt_w_mid, hy_filt_b,
                   hy_filt_freq, hy_filt_w_out, hy_skip, hy_w_out, mlp_w1, mlp_w2, final_g,
                   fwd_table, inv_table, emb_t, decay_rates, minus_times, masks, identity, out):
    spectrum = nc.dram_tensor("filter_spectrum", (GROUPS, P, 2, 4, GC), F32, kind="Internal").ap()

    with ExitStack() as ctx:
        def sb(name, shape, dt=F32, stack=ctx):
            return stack.enter_context(nc.sbuf_tensor(name, shape, dt))

        def sem(name):
            return ctx.enter_context(nc.semaphore(name))

        bank = [ctx.enter_context(nc.psum_tensor(f"bank{b}", [P, 512], F32)) for b in range(8)]

        xT = sb("xT", [P, KT, L])
        a_hi = sb("a_hi", [P, KT, L], F32R)
        a_lo = sb("a_lo", [P, KT, L], F32R)
        stage = sb("stage", [P, STAGE_SLOTS, KT, P])
        w_hi = sb("w_hi", [P, 2, KT, P], F32R)
        w_lo = sb("w_lo", [P, 2, KT, P], F32R)
        ident = sb("ident", [P, P])
        ones = sb("ones", [P, P])
        mean_d = sb("mean_d", [P, P])
        mean_head = sb("mean_head", [P, P])
        eps = sb("eps", [P, 1])
        p_a = sb("p_a", [P, 104])
        p_b = sb("p_b", [P, 57])
        p_c = sb("p_c", [P, 120])
        mod = sb("mod", [P, 96])
        gain = sb("gain", [P, 4, 8])
        c_sig = sb("c_sig", [P, 8])
        c_silu = sb("c_silu", [P, 8])
        lb = sb("lb", [P, 16])
        one_m_lb = sb("one_m_lb", [P, 16])
        lb_tmp = sb("lb_tmp", [P, 4, 16])
        sum_sq = sb("sum_sq", [P, L])
        sq = sb("sq", [P, 2, L])
        std = sb("std", [P, L])
        std_cols = sb("std_cols", [P, TT])
        rstd_cols = sb("rstd_cols", [P, TT])
        tmp_a = sb("tmp_a", [P, 2, L])
        tmp_b = sb("tmp_b", [P, 2, L])

        with ExitStack() as st:
            x_nat = stage[:, 0:4].rearrange("p t k n -> p t (k n)")
            rows_a = sb("rows_a", [104, P], stack=st)
            rows_b = sb("rows_b", [57, P], stack=st)
            rows_c = sb("rows_c", [120, P], stack=st)
            rows_d = sb("rows_d", [4, FW], stack=st)
            p_d = sb("p_d", [FW, 4], stack=st)
            embT = sb("embT", [EMB, L], stack=st)
            f_w_in = sb("f_w_in", [EMB, FW], stack=st)
            f_w_mid = sb("f_w_mid", [FW, 2, FW], stack=st)
            f_w_out = sb("f_w_out", [FW, 2, D], stack=st)
            w_even = sb("w_even", [FW, D], stack=st)
            taps_tmp = sb("taps_tmp", [FW, L], stack=st)
            hidden, angle, turns = taps_tmp, tmp_b[0:FW], (std[0:FW], taps_tmp[:])
            rates = sq[:].rearrange("p a n -> p (a n)")
            minus_t = sb("minus_t", [P, 4], stack=st)
            skip_row = sb("skip_row", [1, D], stack=st)
            taps0 = tmp_b[0:1].rearrange("p a n -> p (a n)")
            decay = stage[:, 4:6].rearrange("p t k n -> p t (k n)")
            taps = sb("taps", [P, 2, 4, D], stack=st)
            tab_s = sb("tab_s", [P, 4, 2, 256], stack=st)
            even_s = tmp_a
            h_out = sb("h_out", [P, 2, 4, L], stack=st)
            ada_w0 = sb("ada_w0", [P, 3, D], stack=st)
            ada_acc0 = sb("ada_acc0", [P, 2, D], stack=st)

        h_hi = sb("h_hi", [P, KT, L], F32R)
        h_lo = sb("h_lo", [P, KT, L], F32R)

        with ExitStack() as st:
            KK = [sb(f"KK{b}", [P, 2, L], stack=st) for b in range(2)]
            QQ = [sb(f"QQ{b}", [P, 2, L], stack=st) for b in range(2)]
            joined = [stage[:, 5, 4 * b:4 * b + 4].rearrange("p k n -> p (k n)") for b in range(2)]
            gates = sb("gates", [P, 3, L], stack=st)
            own = sb("own", [P, L], stack=st)
            values = [sb(f"values{b}", [P, TT, P], stack=st) for b in range(2)]
            out_gate = sb("out_gate", [P, L], stack=st)
            block_gates = {h: sb(f"block_gates{h}", [P, 3, L // h], stack=st) for h in LEVELS[1:] + [128]}
            scores = sb("scores", [P, TT, L], stack=st)
            q_sig, g_sig = sq[:, 0], sq[:, 1]
            q_silu = sb("q_silu", [P, L], stack=st)
            i_T = sb("i_T", [P, L], stack=st)
            f_pos = sb("f_pos", [P, L], stack=st)
            f_neg = sb("f_neg", [P, L], stack=st)
            mask = sb("mask", [P, len(LEVELS), P], U8, stack=st)
            ada_w1 = sb("ada_w1", [P, 2, D], stack=st)
            ada_acc1 = sb("ada_acc1", [P, 1, D], stack=st)

        with ExitStack() as st:
            ada_w2 = sb("ada_w2", [P, 8, D], stack=st)
            ada_acc2 = sb("ada_acc2", [P, 2, D], stack=st)

        with ExitStack() as st:
            tab_f = sb("tab_f", [P, 4, 2, 256], stack=st)
            tab_i = sb("tab_i", [P, 2, 2, 2, 256], stack=st)
            group_params = [sb(f"group_params{b}", [P, 5, 3, 2], stack=st) for b in range(2)]
            padded = [sb(f"padded{b}", [P, L + 2], stack=st) for b in range(3)]
            conv = [sb(f"conv{b}", [P, L], stack=st) for b in range(2)]
            z = [sb(f"z{b}", [P, L], stack=st) for b in range(2)]
            x0 = sb("x0", [P, 2, L], stack=st)
            z_t = [sb(f"z_t{b}", [P, 4, GC], stack=st) for b in range(2)]
            H = [sb(f"H{b}", [P, 4, GC], stack=st) for b in range(2)]
            ZH = sb("ZH", [P, 4, GC], stack=st)
            even_z = std[:].rearrange("p (a n) -> p a n", a=2)
            Z = tmp_a[:].rearrange("p b (a n) -> p (b a) n", a=2)
            Y = sq[:].rearrange("p b (a n) -> p (b a) n", a=2)
            folded = sb("folded", [P, 2, 2, 2, GC], stack=st)

        with ExitStack() as st:
            o_nat = sb("o_nat", [P, TT, D], stack=st)

        weight_landed = [sem(f"weight_landed{j}") for j in range(STAGE_SLOTS)]
        weight_cast, weight_split = sem("weight_cast"), sem("weight_split")
        half_done, slab_done = sem("half_done"), sem("slab_done")
        evicted = [sem("evicted_even"), sem("evicted_odd")]
        sq_ready, sum_ready, mean_ready, std_ready, rstd_ready, rstd_spread = map(sem, (
            "sq_ready", "sum_ready", "mean_ready", "std_ready", "rstd_ready", "rstd_spread"))
        scaled_ready, a_hi_ready, a_lo_ready, final_ready = map(sem, (
            "scaled_ready", "a_hi_ready", "a_lo_ready", "final_ready"))
        relu_sq_ready, h_hi_ready, h_lo_ready = map(sem, ("relu_sq_ready", "h_hi_ready", "h_lo_ready"))
        ada_landed = [sem(f"ada_landed{n}") for n in range(8)]
        ada_summed, ada_columns, mod_ready, gain_ready = map(sem, (
            "ada_summed", "ada_columns", "mod_ready", "gain_ready"))
        consts_set, rows_landed, ident_landed, x_landed, filt_landed = map(sem, (
            "consts_set", "rows_landed", "ident_landed", "x_landed", "filt_landed"))
        rows_turned, params_ready, c_sig_ready, c_silu_ready = map(sem, (
            "rows_turned", "params_ready", "c_sig_ready", "c_silu_ready"))
        out_rates_landed, table_landed = sem("out_rates_landed"), sem("table_landed")
        lb_step, lb_exp = sem("lb_step"), sem("lb_exp")
        x_turned, x_ready = sem("x_turned"), sem("x_ready")
        w_even_ready, pre_sine, angle_step, hidden_ready = map(sem, (
            "w_even_ready", "pre_sine", "angle_step", "hidden_ready"))
        taps_raw, decay_ready, taps_ready, tap0_step = map(sem, (
            "taps_raw", "decay_ready", "taps_ready", "tap0_step"))
        spec_parts, spec_even, spec_ready = map(sem, (
            "spec_parts", "spec_even", "spec_ready"))
        spec_stored = [sem("spec_stored0"), sem("spec_stored1")]
        q_sig_ready, q_ready, i_turned, values_ready = map(sem, (
            "q_sig_ready", "q_ready", "i_turned", "values_ready"))
        f_pos_ready, gate_ready, key_ready, query_ready, own_ready = map(sem, (
            "f_pos_ready", "gate_ready", "key_ready", "query_ready", "own_ready"))
        g_sig_ready, own_sum_ready, keys_joined = map(sem, ("g_sig_ready", "own_sum_ready", "keys_joined"))
        level_scores, diag_scores, level_keys, level_queries, level_gates = map(sem, (
            "level_scores", "diag_scores", "level_keys", "level_queries", "level_gates"))
        far_scores, far_copied, mixed, mixed_sq, head_mean, head_std, head_rstd, head_spread = map(sem, (
            "far_scores", "far_copied", "mixed", "mixed_sq", "head_mean", "head_std", "head_rstd", "head_spread"))
        normed_ready, gated_ready, o_hi_ready, o_lo_ready = map(sem, (
            "normed_ready", "gated_ready", "o_hi_ready", "o_lo_ready"))
        mask_landed, mask_set = sem("mask_landed"), sem("mask_set")
        tables_landed, H_landed0, H_landed1, pad_set, group_ready = map(sem, (
            "tables_landed", "H_landed0", "H_landed1", "pad_set", "group_ready"))
        conv_step, z_ready, z_turned, z_t_ready = map(sem, ("conv_step", "z_ready", "z_turned", "z_t_ready"))
        z_parts, z_even, Z_ready, ZH_ready, Y_ready, folded_ready = map(sem, (
            "z_parts", "z_even", "Z_ready", "ZH_ready", "Y_ready", "folded_ready"))
        y_ready, y_gated, y_hi_ready, y_lo_ready = map(sem, ("y_ready", "y_gated", "y_hi_ready", "y_lo_ready"))
        o_turned, o_copied, stored = map(sem, ("o_turned", "o_copied", "stored"))

        hg_in, hy_in = hg_w_in[0], hy_w_in[0]

        def columns(w, first):
            return w[:, bass.ds(v(first), P)].rearrange("(k p) n -> p k n", p=P)

        block = ctx.enter_context(nc.Block())

        @block.sync
        def _(sp):
            sp.dma_start(ident[:], identity).then_inc(ident_landed, 16)
            for dst, src in (
                (rows_a[A_C:A_C + 8], c.rearrange("a (n p) -> (a n) p", p=P)),
                (rows_a[A_ADA_B:104], ada_b.rearrange("i s (n p) -> (i s n) p", p=P)),
                (rows_b[B_NORM_G:32], norm_g.rearrange("i s (n p) -> (i s n) p", p=P)),
                (rows_b[B_FINAL_G:40], final_g.rearrange("(n p) -> n p", p=P)),
                (rows_b[B_LOWER:56], hg_lower_bounds.rearrange("i s (n p) -> (i s n) p", p=P)),
                (rows_b[B_HEAD_G:57], hg_norm_g),
                (rows_c[0:72], hy_conv_w.rearrange("i s (n p) -> (i s n) p", p=P)),
                (rows_c[72:96], hy_b_in.rearrange("i (n p) -> (i n) p", p=P)),
                (rows_c[96:120], hy_conv_b.rearrange("i (n p) -> (i n) p", p=P)),
                (rows_d[0:3], hy_filt_b[0]),
                (rows_d[3:4], hy_filt_freq),
            ):
                sp.dma_start(dst, src).then_inc(rows_landed, 16)
            def load_ada(q, buffer, first):
                m, third, k = q // 24, q // 8 % 3, q % 8
                slots = buffer[:].shape[1]
                if q >= first + slots:
                    sp.wait_ge(ada_summed, q - slots + 1)
                src = ada_w[m // 2, m % 2, k * P:(k + 1) * P, third * D:(third + 1) * D]
                sp.dma_start(buffer[:, (q - first) % slots], src).then_inc(ada_landed[q % 8], 16)

            def load_slab(s, slot, src, wait=None):
                if wait is not None:
                    sp.wait_ge(weight_split, v(2 * wait))
                sp.dma_start(stage[:, slot], src).then_inc(weight_landed[slot], 16)

            sp.dma_start(x_nat, x[0].rearrange("(t p) d -> p t d", p=P)).then_inc(x_landed, 16)
            for q in range(16):
                load_ada(q, ada_w0, 0)
                if q == 2:
                    sp.dma_start(tab_s[:], fwd_table).then_inc(table_landed, 16)

            sp.wait_ge(x_turned, KT)
            for j in range(5):
                if j == 4:
                    sp.wait_ge(taps_ready, 16)
                load_slab(j, j, columns(hg_in, j * D))
            for parts_stored in spec_stored:
                sp.wait_ge(parts_stored, 64)
            sp.wait_ge(ada_columns, 2)
            sp.dma_start(scores[:, 0:2].rearrange("p a n -> p (a n)")[:, 0:len(LEVELS) * P],
                         masks.rearrange("p l n -> p (l n)")).then_inc(mask_landed, 16)
            for q in range(16, 18):
                load_ada(q, ada_w1, 16)
            def load_hg_out(n):
                load_slab(S_HG_OUT + n, n % 4, columns(hg_w_out[0], n * P), S_HG_OUT + n - 3)

            for h in range(1, HEADS + 1):
                for j in range(5 if h < HEADS else 0):
                    s = 5 * h + j
                    load_slab(s, j, columns(hg_in, j * D + h * P), s - 4)
                for n in range(4 if h == HEADS else 0):
                    load_hg_out(n)
                for n in range(4):
                    q = 16 + 4 * (h - 1) + n + 2
                    if q < 48:
                        load_ada(q, ada_w1, 16)
            for n in range(4, KT):
                load_hg_out(n)

            def mlp_slab(i, s0, ch, n):
                s = 16 * ch + (s0 + n)
                if n < 8:
                    src = columns(mlp_w1[i], D * ch + n * P)
                else:
                    src = columns(mlp_w2[i, bass.ds(v(D * ch), D)], (n - 8) * P)
                load_slab(s, n % 4, src, s - 3)

            sp.wait_ge(o_lo_ready, HEADS)
            sp.wait_ge(ada_columns, 6)
            for ch in range(CHUNKS):
                for n in range(16):
                    if ch < CHUNKS - 1:
                        load_ada(48 + 16 * ch + n, ada_w2, 48)
                    mlp_slab(0, S_MLP0, ch, n)

            for g in range(GROUPS):
                for j, (seg, n) in enumerate(HY_ORDER):
                    s = S_HY_IN + 6 * g + j
                    wait = s - 5 if g else (s - 3 if j < 4 else s - 5)
                    load_slab(s, j, columns(hy_in, seg * D + g * GC + n * P), wait)
                if g == 0:
                    sp.wait_ge(ada_columns, 12)
                    sp.dma_start(tab_f[:], fwd_table).then_inc(tables_landed, 16)
                    sp.dma_start(tab_i[:], inv_table).then_inc(tables_landed, 16)
                for h in ((), (0,), (1,), (2, 3))[g]:
                    for m in range(2):
                        if h:
                            sp.wait_ge(ZH_ready, 4 * (h - 1) + 2 * m + 2)
                        sp.dma_start(H[m][:], spectrum[h, :, m]).then_inc((H_landed0, H_landed1)[m], 16)
            for n in range(KT):
                s = S_HY_OUT + n
                load_slab(s, n % 4, columns(hy_w_out[0], n * P), s - 3)
            with sp.Fori(0, CHUNKS) as ch:
                for n in range(16):
                    mlp_slab(1, S_MLP1, At(ch), n)

            for half in range(2):
                sp.wait_ge(o_copied, 4 * (half + 1))
                cols = slice(half * 512, half * 512 + 512)
                sp.dma_start(out[0].rearrange("(t p) d -> p t d", p=P)[:, :, cols],
                             o_nat[:, :, cols]).then_inc(stored, 16)
            sp.wait_ge(stored, 32)

        @block.gpsimd
        def _(pool):
            def split_slab(s, slot, landed):
                side = s % 2
                pool.wait_ge(weight_landed[slot], v(landed * 16))
                for half in range(2):
                    k = slice(4 * half, 4 * half + 4)
                    if s >= 2:
                        pool.wait_ge((half_done, slab_done)[half], v(s - 1))
                    if isinstance(s, At):
                        pool.nop(nofuse=True)
                    nc.gpsimd.tensor_scalar(w_hi[:, side, k], stage[:, slot, k], 1.0, 0.0, ALU.mult,
                                            ALU.add).then_inc(weight_cast, 1)
                    pool.wait_ge(weight_cast, v(2 * s + half + 1))
                    nc.gpsimd.tensor_tensor(w_lo[:, side, k], stage[:, slot, k], w_hi[:, side, k].bitcast(F32),
                                            ALU.subtract).then_inc(weight_split, 1)

            for k in range(KT):
                pool.wait_ge(sq_ready, k + 1)
                if k == 0:
                    ins = nc.gpsimd.tensor_scalar(sum_sq[:], sq[:, 0], 1.0, 0.0, ALU.mult, ALU.add)
                else:
                    pool.wait_ge(sum_ready, k)
                    ins = nc.gpsimd.tensor_tensor(sum_sq[:], sum_sq[:], sq[:, k % 2], ALU.add)
                ins.then_inc(sum_ready, 1)
            landed = [0] * STAGE_SLOTS

            def split_phase(first, end, slots, body):
                with pool.Fori(0, (end - first) // body) as i:
                    for n in range(body):
                        split_slab(At(i, body, first + n), n % slots,
                                   At(i, body // slots, landed[n % slots] + n // slots + 1))
                for slot in range(slots):
                    landed[slot] += (end - first) // slots

            for s in range(10):
                split_slab(s, s % 5, s // 5 + 1)
            landed[0:5] = [2] * 5
            split_phase(10, S_HG_OUT, 5, 10)
            split_phase(S_HG_OUT, S_HY_IN, 4, 4)
            split_phase(S_HY_IN, S_HY_OUT, 6, 6)
            split_phase(S_HY_OUT, N_SLABS, 4, 4)

        @block.tensor
        def _(pe):
            def product(dst, pairs, after=None):
                for n, (lhs, rhs) in enumerate(pairs):
                    ins = pe.matmul(dst, lhs, rhs, start=n == 0, stop=n == len(pairs) - 1)
                return ins

            def k_tile(s, k, hi, lo):
                side = s % 2
                if k % 4 == 0:
                    pe.wait_ge(weight_split, v(2 * s + k // 4 + 1))
                if k == 0 and s >= 2:
                    pe.wait_ge(evicted[side], v(s // 2))
                acc = bank[side][:]
                pe.matmul(acc, w_hi[:, side, k], hi[:, k], start=k == 0, stop=False)
                pe.matmul(acc, w_lo[:, side, k], hi[:, k], start=False, stop=False)
                ins = pe.matmul(acc, w_hi[:, side, k], lo[:, k], start=False, stop=k == KT - 1)
                if k % 4 == 3:
                    ins.then_inc((half_done, slab_done)[k // 4], 1)

            def slab(s, hi, lo, between={}):
                for k in range(KT):
                    k_tile(s, k, hi, lo)
                    for work in between.get(k, ()):
                        work()

            def first_pair(s, hi, lo, hi_ready, lo_ready, before, between={}):
                for k in range(KT):
                    pe.wait_ge(hi_ready, v(before + k + 1))
                    pe.wait_ge(lo_ready, v(before + k + 1))
                    for n in range(2):
                        k_tile(s + n, k, hi, lo)
                        for work in between.get(2 * k + n, ()):
                            work()

            def ada_column(c, acc):
                pe.wait_ge(ada_summed, v(8 * (c + 1)))
                if c >= 1:
                    pe.wait_ge(mod_ready, v(c))
                for n in range(8):
                    ins = pe.matmul(bank[6][:, n:n + 1], acc[:, n * P:(n + 1) * P], ones[:, 0:1],
                                    start=True, stop=True)
                ins.then_inc(ada_columns, 1)

            def token_means(squares, weight):
                for t in range(TT):
                    ins = pe.matmul(bank[7][:, t:t + 1], squares[:, t * P:(t + 1) * P], weight[:, 0:1],
                                    start=True, stop=True)
                return ins

            def spread():
                for t in range(TT):
                    ins = pe.matmul(bank[7][:, t * P:(t + 1) * P], view(rstd_cols, t, [0, P]), ident[:],
                                    start=True, stop=True)
                return ins

            def norm_mean(m):
                pe.wait_ge(sum_ready, 8 * (m + 1))
                if m == 1:
                    pe.wait_ge(gated_ready, HEADS)
                if m:
                    pe.wait_ge(scaled_ready, 8 * m)
                token_means(sum_sq, mean_d).then_inc(mean_ready, 1)
                pe.wait_ge(rstd_ready, m + 1)
                spread().then_inc(rstd_spread, 1)

            pe.wait_ge(ident_landed, 16)
            pe.wait_ge(rows_landed, 16 * 11)
            pe.wait_ge(consts_set, 5)
            for n, rows in enumerate((rows_a, rows_b, rows_c, rows_d)):
                r, w = rows[:].shape
                pe.transpose(bank[2 + n][0:w, 0:r], rows[:], ident[0:r, 0:r]).then_inc(rows_turned, 1)
            pe.wait_ge(filt_landed, 16 * 5)
            pe.wait_ge(params_ready, 4)
            pe.matmul(bank[4][0:FW], f_w_in[:], embT[:], start=True, stop=True).then_inc(pre_sine, 1)
            def turn_x(k):
                if k == 0:
                    pe.wait_ge(x_landed, 16)
                if k >= 2:
                    pe.wait_ge(x_ready, k - 1)
                for t in range(TT):
                    ins = pe.transpose(bank[2 + k % 2][:, t * P:(t + 1) * P], x_nat[:, t, k * P:(k + 1) * P],
                                       ident[:])
                ins.then_inc(x_turned, 1)

            for m in range(2):
                pe.wait_ge(hidden_ready, m + 1)
                pe.matmul(bank[4][0:FW], f_w_mid[:, m], hidden[:], start=True, stop=True).then_inc(pre_sine, 1)
                for k in range(4 * m, 4 * m + 4):
                    turn_x(k)
            pe.wait_ge(hidden_ready, 3)
            pe.wait_ge(w_even_ready, 2)
            n = 0
            for j in range(TT):
                for part in range(2):
                    for half in range(2):
                        if n >= 2:
                            pe.wait_ge(taps_ready, n - 1)
                        pe.matmul(bank[4 + n % 2][:], hidden[:, j * P:(j + 1) * P],
                                  (w_even[:] if part == 0 else f_w_out[:, 1])[:, half * 512:half * 512 + 512],
                                  start=True, stop=True).then_inc(taps_raw, 1)
                        n += 1
            pe.wait_ge(x_ready, 8)
            pe.wait_ge(taps_ready, 16)
            pe.wait_ge(tap0_step, 2)
            pe.wait_ge(table_landed, 16)

            def spectrum_part(n):
                half, m, part = n // 4, n // 2 % 2, n % 2
                if n >= 3:
                    pe.wait_ge(spec_ready, 2 * (n - 2))
                for odd in range(2):
                    product(bank[SPEC_BANKS[n % 3][odd]][:], [
                        (tab_s[:, 2 * odd + j, part, m * P:(m + 1) * P],
                         taps[:, part, 2 * odd + j, half * 512:half * 512 + 512]) for j in range(2)]).then_inc(
                        spec_parts, 1)

            for n in range(3):
                spectrum_part(n)
            pe.wait_ge(sum_ready, 8)
            token_means(sum_sq, mean_d).then_inc(mean_ready, 1)
            spectrum_part(3)
            spectrum_part(4)
            ada_column(0, ada_acc0[:, 0])
            ada_column(1, ada_acc0[:, 1])
            for n in range(5, 8):
                spectrum_part(n)
            pe.wait_ge(rstd_ready, 1)
            spread().then_inc(rstd_spread, 1)
            pe.wait_ge(spec_ready, 16)

            def turn_values(h):
                pe.wait_ge(evicted[(5 * h + 1) % 2], v((5 * h + 1) // 2 + 1))
                if h >= 2:
                    pe.wait_ge(far_copied, v(3 * h - 5))
                for t in range(TT):
                    ins = pe.transpose(bank[4][:, t * P:(t + 1) * P], i_T[:, t * P:(t + 1) * P], ident[:])
                ins.then_inc(i_turned, 1)

            def own_scores(h):
                pe.wait_ge(own_ready, v(h + 1))
                if h:
                    pe.wait_ge(far_copied, v(3 * h))
                for t in range(TT):
                    ins = pe.matmul(bank[2][:, t * P:(t + 1) * P], own[:, t * P:(t + 1) * P], ones[:],
                                    start=True, stop=True)
                ins.then_inc(level_scores, 1)

            def level(h, n):
                width = LEVELS[n]
                pe.wait_ge(keys_joined, v(7 * h + n + 1))
                if n == 0:
                    pe.wait_ge(query_ready, v(2 * h + 2))
                else:
                    pe.wait_ge(level_queries, v(8 * h + n))
                    pe.wait_ge(diag_scores, v(8 * h + n))
                for t in range(TT):
                    queries = view(QQ[h % 2], t * P, [2 * width, 64 // width], [L + width, 2], [1, width])
                    ins = pe.matmul(bank[3 - n % 2][:, t * P:(t + 1) * P], joined[n % 2][:, t * P:(t + 1) * P],
                                    queries, start=True, stop=True)
                ins.then_inc(level_scores, 1)

            def far_128(h):
                pe.wait_ge(level_keys, v(8 * h + 7))
                pe.wait_ge(level_queries, v(8 * h + 7))
                pe.wait_ge(values_ready, v(h + 2 if h + 1 < HEADS else HEADS))
                for n, (s, t, back) in enumerate(((0, 1, 0), (1, 0, 1), (2, 3, 0), (3, 2, 1))):
                    ins = pe.matmul(bank[4][:, n * P:(n + 1) * P], KK[h % 2][:, back, s * P:(s + 1) * P],
                                    QQ[h % 2][:, 1 - back, t * P:(t + 1) * P], start=True, stop=True)
                ins.then_inc(far_scores, 1)

            def far_256(h):
                pe.wait_ge(level_keys, v(8 * h + 8))
                pe.wait_ge(level_queries, v(8 * h + 8))
                pe.wait_ge(diag_scores, v(8 * h + 8))
                for n in range(4):
                    back = n // 2
                    ins = pe.matmul(bank[2 + back][:, n % 2 * 256:n % 2 * 256 + 256],
                                    KK[h % 2][:, back, n * P:(n + 1) * P],
                                    QQ[h % 2][:, 1 - back, (1 - back) * 256:(1 - back) * 256 + 256],
                                    start=True, stop=True)
                    if n % 2:
                        ins.then_inc(far_scores, 1)

            def mix(h):
                pe.wait_ge(far_copied, v(3 * h + 3))
                pe.wait_ge(diag_scores, v(8 * h + 8))
                if h:
                    pe.wait_ge(normed_ready, v(h))
                product(bank[5][:], [(values[h % 2][:, t], scores[:, t]) for t in range(TT)]).then_inc(mixed, 1)

            def head_square(h):
                pe.wait_ge(mixed_sq, v(h + 1))
                if h:
                    pe.wait_ge(gated_ready, v(h))
                token_means(std, mean_head).then_inc(head_mean, 1)

            def spread_head(h):
                pe.wait_ge(head_rstd, v(h + 1))
                spread().then_inc(head_spread, 1)

            def head_step(g):
                h = g - 1
                places = {}

                def put(place, work):
                    places.setdefault(place, []).append(work)

                if g >= 1:
                    put(1 if g < HEADS else 0, lambda: own_scores(h))
                    for n in range(7):
                        put(3 * n + 2, lambda n=n: level(h, n))
                    for place, work in ((24, far_128), (28, far_256), (31, mix), (33, head_square), (36, spread_head)):
                        put(place, lambda work=work: work(h))
                if g % 2 and g >= 3:
                    put(0, lambda: ada_column(2 + (g - 3) // 2, ada_acc1[:, 0]))
                if g < HEADS:
                    places.setdefault(19, []).insert(0, lambda: turn_values(g))
                    first = isinstance(g, int) and g == 0
                    if first:
                        first_pair(0, a_hi, a_lo, a_hi_ready, a_lo_ready, 0)
                    for j in range(2 if first else 0, 5):
                        slab(5 * g + j, a_hi, a_lo, {k: places.get(8 * j + k, ()) for k in range(KT)})
                else:
                    tiles = [(S_HG_OUT + n, k) for k in range(KT - 1) for n in range(2)]
                    for place in range(40):
                        if place % 2 == 0 and tiles:
                            k_tile(*tiles.pop(0), h_hi, h_lo)
                        for work in places.get(place, ()):
                            work()
            head_step(0)
            head_step(1)
            with pe.Fori(0, HEADS // 2 - 1) as pair:
                head_step(At(pair, 2, 2))
                head_step(At(pair, 2, 3))
            head_step(HEADS)
            pe.wait_ge(o_hi_ready, HEADS)
            pe.wait_ge(o_lo_ready, HEADS)
            for n in range(2):
                k_tile(S_HG_OUT + n, KT - 1, h_hi, h_lo)
            for n in range(2, KT):
                slab(S_HG_OUT + n, h_hi, h_lo)
                if n == 2:
                    ada_column(5, ada_acc1[:, 0])
            norm_mean(1)

            def chunk(i, s0, ch, with_ada):
                s = s0 + 16 * ch
                if isinstance(ch, int) and ch == 0:
                    first_pair(s, a_hi, a_lo, a_hi_ready, a_lo_ready, 8 * (2 * i + 1))
                else:
                    for n in range(2):
                        slab(s + n, a_hi, a_lo)
                    if with_ada:
                        ada_column(2 * ch + 5, ada_acc2[:, 1])
                for n in range(2, 8):
                    slab(s + n, a_hi, a_lo)
                first_pair(s + 8, h_hi, h_lo, h_hi_ready, h_lo_ready, 8 * ch + 8 * CHUNKS * i)
                if with_ada and not (isinstance(ch, int) and ch == CHUNKS - 1):
                    ada_column(2 * ch + 6, ada_acc2[:, 0])
                for n in range(2, 8):
                    slab(s + 8 + n, h_hi, h_lo)

            def mlp(i, s0, with_ada):
                chunk(i, s0, 0, with_ada)
                with pe.Fori(1, CHUNKS - 1 if with_ada else CHUNKS) as ch:
                    chunk(i, s0, At(ch), with_ada)
                if with_ada:
                    chunk(i, s0, CHUNKS - 1, with_ada)
                norm_mean(2 * i + 2)

            mlp(0, S_MLP0, True)

            def turn_z(g, n):
                pe.wait_ge(z_ready, 2 * g + n + 1)
                if g or n:
                    pe.wait_ge(z_t_ready, 2 * g + n)
                for j in range(TT):
                    ins = pe.transpose(bank[4][:, j * P:(j + 1) * P], z[n][:, j * P:(j + 1) * P], ident[:])
                ins.then_inc(z_turned, 1)

            def forward(g, m):
                if m == 0:
                    pe.wait_ge(z_t_ready, 2 * g + 2)
                if g == m == 0:
                    pe.wait_ge(tables_landed, 32)
                if g or m:
                    pe.wait_ge(z_even, 2 * g + m)
                    pe.wait_ge(Z_ready, 2 * (2 * g + m))
                for odd in range(2):
                    for part in range(2):
                        ins = product(bank[2 + odd][:, part * GC:(part + 1) * GC], [
                            (tab_f[:, 2 * odd + j, part, m * P:(m + 1) * P], z_t[g % 2][:, 2 * odd + j])
                            for j in range(2)])
                    ins.then_inc(z_parts, 1)

            def inverse(g, n):
                pe.wait_ge(folded_ready, 4 * g + 4)
                if g == 0 and n == 1:
                    pe.wait_ge(mod_ready, 12)
                if g:
                    pe.wait_ge(y_gated, 2 * g - 1 + n)
                for parity in range(2):
                    ins = product(bank[5 + n][:, parity * 256:parity * 256 + 256], [
                        (folded[:, m, parity, part, n * P:(n + 1) * P], tab_i[:, m, part, parity])
                        for m in range(2) for part in range(2)])
                ins.then_inc(y_ready, 1)

            for g in range(GROUPS + 1):
                h = g - 1
                places = {26: [lambda: turn_z(g, 0)], 43: [lambda: turn_z(g, 1)]}
                if h >= 0:
                    places |= {2: [lambda: forward(h, 0)], 12: [lambda: forward(h, 1)],
                               35: [lambda: inverse(h, 0)], 38: [lambda: inverse(h, 1)]}
                if g < GROUPS:
                    if g == 0:
                        first_pair(S_HY_IN, a_hi, a_lo, a_hi_ready, a_lo_ready, 16)
                    for j in range(0 if g else 2, 6):
                        slab(S_HY_IN + 6 * g + j, a_hi, a_lo, {k: places.get(8 * j + k, ()) for k in range(KT)})
                else:
                    tiles = [(S_HY_OUT + n, k) for k in range(KT - 2) for n in range(2)]
                    forward(h, 0)
                    pe.wait_ge(y_hi_ready, KT - 2)
                    pe.wait_ge(y_lo_ready, KT - 2)
                    for n in range(6):
                        k_tile(*tiles.pop(0), h_hi, h_lo)
                    forward(h, 1)
                    while tiles:
                        k_tile(*tiles.pop(0), h_hi, h_lo)
                    inverse(h, 0)
                    inverse(h, 1)
            for k in (KT - 2, KT - 1):
                pe.wait_ge(y_hi_ready, k + 1)
                pe.wait_ge(y_lo_ready, k + 1)
                for n in range(2):
                    k_tile(S_HY_OUT + n, k, h_hi, h_lo)
            for n in range(2, KT):
                slab(S_HY_OUT + n, h_hi, h_lo)
            norm_mean(3)
            mlp(1, S_MLP1, False)

            for k in range(KT):
                pe.wait_ge(final_ready, k + 1)
                if k >= 2:
                    pe.wait_ge(o_copied, k - 1)
                for t in range(TT):
                    ins = pe.transpose(bank[2 + k % 2][:, t * P:(t + 1) * P], tmp_b[:, k % 2, t * P:(t + 1) * P],
                                       ident[:])
                ins.then_inc(o_turned, 1)

        @block.scalar
        def _(act):
            def run(out_, in_, func, **kw):
                return nc.scalar.activation(out_, in_, func, **kw)

            def square_x(m, k):
                j = 8 * m + k
                if j >= 2:
                    act.wait_ge(sum_ready, j - 1)
                run(sq[:, k % 2], xT[:, k], ACT.Square).then_inc(sq_ready, 1)

            def norm_std(m):
                act.wait_ge(mean_ready, m + 1)
                run(std_cols[:], bank[7][:, 0:TT], ACT.Sqrt, bias=eps[:, 0:1]).then_inc(std_ready, 1)

            def norm_apply(m):
                for k in range(KT):
                    act.wait_ge(scaled_ready, 8 * m + k + 1)
                    run(a_hi[:, k], tmp_a[:, k % 2], ACT.Identity, bias=mod[:, 24 * m + k:24 * m + k + 1]).then_inc(a_hi_ready, 1)

            def evict_wait(s):
                act.wait_ge(slab_done, v(s + 1))

            for dst, src in (
                (embT[:], emb_t), (f_w_in[:], hy_filt_w_in[0]),
                (f_w_mid[:], hy_filt_w_mid[0].rearrange("m a b -> a m b")),
                (minus_t[:], minus_times), (skip_row[:], hy_skip),
            ):
                act.dma_start(dst, src).then_inc(filt_landed, 16)
            act.dma_start(f_w_out[:], hy_filt_w_out[0].rearrange("w (s d) -> w s d", s=2)).then_inc(
                out_rates_landed, 16)
            act.dma_start(rates, decay_rates.partition_broadcast(P)).then_inc(out_rates_landed, 16)
            act.wait_ge(params_ready, 1)
            run(c_sig[:], p_a[:, A_C:A_C + 8], ACT.Sigmoid).then_inc(c_sig_ready, 1)
            act.wait_ge(lb_step, 1)
            run(lb_tmp[:, 1], lb_tmp[:, 0], ACT.Exp).then_inc(lb_exp, 1)

            def sine(layer):
                act.wait_ge(angle_step, 6 * layer + 6)
                run(hidden[:], angle[:, 1], ACT.Sin).then_inc(hidden_ready, 1)

            def take_x(k):
                act.wait_ge(x_turned, k + 1)
                nc.scalar.copy(xT[:, k], bank[2 + k % 2][:]).then_inc(x_ready, 1)

            sine(0)
            for k in range(4):
                take_x(k)
            sine(1)
            for k in range(4, 8):
                take_x(k)
            sine(2)
            act.wait_ge(out_rates_landed, 32)
            for j in range(4):
                if j >= 2:
                    act.wait_ge(taps_ready, 4 * (j - 1))
                run(decay[:, j % 2], rates, ACT.Exp, scale=minus_t[:, j:j + 1]).then_inc(decay_ready, 1)
            for k in range(KT):
                if k == 0:
                    act.wait_ge(x_ready, 8)
                    act.wait_ge(decay_ready, 4)
                square_x(0, k)
            for n in range(8):
                act.wait_ge(spec_parts, 2 * n + 1)
                if n >= 2:
                    act.wait_ge(spec_ready, 2 * (n - 1))
                nc.scalar.copy(even_s[:, n % 2], bank[SPEC_BANKS[n % 3][0]][:]).then_inc(spec_even, 1)
                if n % 2:
                    half, m = n // 4, n // 2 % 2
                    act.wait_ge(spec_ready, 2 * (n + 1))
                    for gg in range(2):
                        act.dma_start(spectrum[2 * half + gg, :, m],
                                      h_out[:, m, :, gg * GC:(gg + 1) * GC]).then_inc(spec_stored[m], 16)
                if n == 4:
                    norm_std(0)
            act.wait_ge(gain_ready, 1)
            norm_apply(0)

            def query_input(g):
                s = 5 * g
                evict_wait(s)
                if g:
                    act.wait_ge(evicted[(s - 5) % 2], v((s - 5) // 2 + 1))
                else:
                    for parts_stored in spec_stored:
                        act.wait_ge(parts_stored, 64)
                run(q_sig, bank[s % 2][:], ACT.Sigmoid).then_inc(q_sig_ready, 1)

            def value_input(g):
                s = 5 * g + 1
                evict_wait(s)
                if g:
                    act.wait_ge(i_turned, v(g))
                nc.scalar.copy(i_T[:], bank[s % 2][:]).then_inc(evicted[s % 2], 1)

            def forget_input(g, way):
                s, n = 5 * g + 2 + way, 2 * g + way
                evict_wait(s)
                if n:
                    act.wait_ge(gate_ready, v(3 * g + (1 if way else 0)))
                    act.wait_ge(key_ready, v(n))
                run(f_pos[:], bank[s % 2][:], ACT.Sigmoid).then_inc(f_pos_ready, 1)
                run(f_neg[:], bank[s % 2][:], ACT.Sigmoid, scale=-1.0).then_inc(evicted[s % 2], 1)

            def take_values(g):
                act.wait_ge(i_turned, v(g + 1))
                if g >= 2:
                    act.wait_ge(mixed, v(g - 1))
                nc.scalar.copy(values[g % 2][:], bank[4][:].rearrange("p (t n) -> p t n", t=TT)).then_inc(
                    values_ready, 1)

            def head_gate(g):
                s = 5 * g + 4
                evict_wait(s)
                if g:
                    act.wait_ge(evicted[(s - 5) % 2], v((s - 5) // 2 + 1))
                run(g_sig, bank[s % 2][:], ACT.Sigmoid).then_inc(g_sig_ready, 1)

            def head_far(h):
                act.wait_ge(far_scores, v(3 * h + 1))
                if h:
                    act.wait_ge(mixed, v(h))
                nc.scalar.copy(view(scores, P, [2 * L + 256, 2], [L - P, 2], [1, P]),
                               bank[4][:].rearrange("p (a b n) -> p a b n", a=2, b=2)).then_inc(far_copied, 1)
                for back in range(2):
                    act.wait_ge(far_scores, v(3 * h + 2 + back))
                    nc.scalar.copy(view(scores, 256 if back == 0 else 2 * L, [L, 2], [1, 256]),
                                   bank[2 + back][:].rearrange("p (a n) -> p a n", a=2)).then_inc(far_copied, 1)

            def head_square(h):
                act.wait_ge(mixed, v(h + 1))
                if h:
                    act.wait_ge(head_mean, v(h))
                run(std[:], bank[5][:], ACT.Square).then_inc(mixed_sq, 1)

            def head_std_cols(h):
                act.wait_ge(head_mean, v(h + 1))
                if h:
                    act.wait_ge(head_rstd, v(h))
                run(std_cols[:], bank[7][:, 0:TT], ACT.Sqrt, bias=eps[:, 0:1]).then_inc(head_std, 1)

            def head_split(h):
                act.wait_ge(gated_ready, v(h + 1))
                nc.scalar.copy(one_row(h_hi, h), tmp_b[:, h % 2]).then_inc(o_hi_ready, 1)

            def join_keys(h, n):
                if n == 0:
                    act.wait_ge(key_ready, v(2 * h + 2))
                else:
                    act.wait_ge(level_keys, v(8 * h + n))
                if h or n >= 2:
                    act.wait_ge(level_scores, v(8 * h + (n if n >= 2 else 0)))
                width = LEVELS[n]
                nc.scalar.copy(joined[n % 2].rearrange("p (a b n) -> p a b n", b=2, n=width),
                               view(KK[h % 2], 0, [2 * width, 256 // width], [L + width, 2], [1, width])).then_inc(
                    keys_joined, 1)

            def join_levels(g, first, last):
                if g:
                    for n in range(first, last):
                        join_keys(g - 1, n)

            def head_step(g):
                join_levels(g, 0, 3)
                if g < HEADS:
                    query_input(g)
                join_levels(g, 3, 5)
                if g < HEADS:
                    value_input(g)
                join_levels(g, 5, 7)
                if g < HEADS:
                    forget_input(g, 0)
                    take_values(g)
                if g >= 1:
                    head_far(g - 1)
                    head_square(g - 1)
                if g < HEADS:
                    forget_input(g, 1)
                if g >= 1:
                    head_std_cols(g - 1)
                    head_split(g - 1)
                if g < HEADS:
                    head_gate(g)

            head_step(0)
            head_step(1)
            with act.Fori(0, HEADS // 2 - 1) as pair:
                head_step(At(pair, 2, 2))
                head_step(At(pair, 2, 3))
            head_step(HEADS)

            def norm(m, s0):
                for n in range(KT):
                    s = s0 + n
                    act.wait_ge(evicted[s % 2], s // 2 + 1)
                    square_x(m, n)
                norm_std(m)
                if m < 4:
                    act.wait_ge(gain_ready, m + 1)
                    norm_apply(m)

            norm(1, S_HG_OUT)

            def mlp(i, s0):
                with act.Fori(0, CHUNKS) as chunk:
                    for n in range(8):
                        s, j = At(chunk, 16, s0 + n), At(chunk, 8, 8 * CHUNKS * i + n)
                        evict_wait(s)
                        if n >= 2 or i:
                            act.wait_ge(h_hi_ready, v(j - 1))
                        run(tmp_a[:, n % 2], bank[s % 2][:], ACT.Relu).then_inc(evicted[s % 2], 1)
                        act.wait_ge(evicted[s % 2], v(s // 2 + 1))
                        if n >= 2 or i:
                            act.wait_ge(h_lo_ready, v(j - 1))
                        run(tmp_b[:, n % 2], tmp_a[:, n % 2], ACT.Square).then_inc(relu_sq_ready, 1)
                norm(2 * i + 2, s0 + 16 * CHUNKS - 8)

            mlp(0, S_MLP0)

            def take_z(g, n):
                act.wait_ge(z_turned, 2 * g + n + 1)
                if g >= 2:
                    act.wait_ge(z_parts, 4 * (g - 1))
                nc.scalar.copy(z_t[g % 2][:, :, n * P:(n + 1) * P],
                               bank[4][:].rearrange("p (j n) -> p j n", j=4)).then_inc(z_t_ready, 1)

            def even_part(h, m):
                act.wait_ge(z_parts, 2 * (2 * h + m) + 1)
                if h or m:
                    act.wait_ge(Z_ready, 2 * (2 * h + m))
                nc.scalar.copy(even_z, bank[2][:].rearrange("p (a n) -> p a n", a=2)).then_inc(z_even, 1)

            def y_high(h, n):
                act.wait_ge(y_gated, 2 * h + n + 1)
                nc.scalar.copy(h_hi[:, 2 * h + n], tmp_b[:, n]).then_inc(y_hi_ready, 1)

            act.wait_ge(pad_set, 3)
            for g in range(GROUPS + 1):
                for j in range(6 if g < GROUPS else 0):
                    s = S_HY_IN + 6 * g + j
                    seg, n = HY_ORDER[j]
                    evict_wait(s)
                    act.wait_ge(group_ready, g + 1)
                    prior = 6 * g + (-4, -4, 0, 1, -1, 4)[j]
                    if prior >= 0:
                        act.wait_ge(conv_step, 3 * (prior + 1))
                    run(padded[seg][:, 1:L + 1], bank[s % 2][:], ACT.Identity,
                        bias=group_params[g % 2][:, 3, seg, n:n + 1]).then_inc(evicted[s % 2], 1)
                    if g and j == 0:
                        even_part(g - 1, 0)
                    if g and j == 2:
                        even_part(g - 1, 1)
                    if j == 3:
                        take_z(g, 0)
                    if g and j == 5:
                        y_high(g - 1, 0)
                        y_high(g - 1, 1)
                    if j == 5:
                        take_z(g, 1)
                if g == GROUPS:
                    even_part(g - 1, 0)
                    even_part(g - 1, 1)
                    y_high(g - 1, 0)
                    y_high(g - 1, 1)
            norm(3, S_HY_OUT)
            mlp(1, S_MLP1)
            for k in range(KT):
                act.wait_ge(o_turned, k + 1)
                nc.scalar.copy(o_nat[:, :, k * P:(k + 1) * P],
                               bank[2 + k % 2][:].rearrange("p (t n) -> p t n", t=TT)).then_inc(o_copied, 1)

        @block.vector
        def _(dve):
            tt, ts, stt = nc.vector.tensor_tensor, nc.vector.tensor_scalar, nc.vector.scalar_tensor_tensor

            def ada_piece(q, buffer, acc, first):
                c, k = q // 8, q % 8
                slots, accs = buffer[:].shape[1], acc[:].shape[1]
                dve.wait_ge(ada_landed[k], v((c + 1) * 16))
                if q >= 1:
                    dve.wait_ge(ada_summed, v(q))
                if k == 0 and c >= first // 8 + accs:
                    dve.wait_ge(ada_columns, v(c - accs + 1))
                w, total = buffer[:, (q - first) % slots], acc[:, c % accs]
                if k == 0:
                    ins = ts(total, w, c_silu[:, 0:1], None, ALU.mult)
                else:
                    ins = stt(out=total, in0=w, scalar=c_silu[:, k:k + 1], in1=total, op0=ALU.mult, op1=ALU.add)
                ins.then_inc(ada_summed, 1)

            def take_mod(c):
                dve.wait_ge(ada_columns, v(c + 1))
                tt(mod[:, bass.ds(v(8 * c), 8)], bank[6][:, 0:8], p_a[:, bass.ds(v(8 * c + A_ADA_B), 8)],
                   ALU.add).then_inc(mod_ready, 1)

            def make_gain(m):
                dve.wait_ge(mod_ready, 3 * m + 2)
                stt(out=gain[:, m], in0=mod[:, 24 * m + 8:24 * m + 16], scalar=1.0,
                    in1=p_b[:, B_NORM_G + 8 * m:B_NORM_G + 8 * m + 8], op0=ALU.add, op1=ALU.mult).then_inc(
                    gain_ready, 1)

            def add_square(m, k):
                dve.wait_ge(sq_ready, 8 * m + k + 1)
                if k == 0:
                    ins = nc.vector.tensor_copy(sum_sq[:], sq[:, 0])
                else:
                    dve.wait_ge(sum_ready, 8 * m + k)
                    ins = tt(sum_sq[:], sum_sq[:], sq[:, k % 2], ALU.add)
                ins.then_inc(sum_ready, 1)

            def norm_rstd(m):
                dve.wait_ge(std_ready, m + 1)
                nc.vector.reciprocal(rstd_cols[:], std_cols[:]).then_inc(rstd_ready, 1)
                if m < 4:
                    make_gain(m)
                dve.wait_ge(rstd_spread, m + 1)

            def norm_apply(m):
                def scale(k):
                    j = 8 * m + k
                    if k >= 2:
                        dve.wait_ge(a_hi_ready, j - 1)
                        dve.wait_ge(a_lo_ready, j - 1)
                    stt(out=tmp_a[:, k % 2], in0=xT[:, k], scalar=gain[:, m, k:k + 1], in1=bank[7][:],
                        op0=ALU.mult, op1=ALU.mult).then_inc(scaled_ready, 1)

                def low(k):
                    dve.wait_ge(a_hi_ready, 8 * m + k + 1)
                    stt(out=a_lo[:, k], in0=tmp_a[:, k % 2], scalar=mod[:, 24 * m + k:24 * m + k + 1], in1=a_hi[:, k].bitcast(F32),
                        op0=ALU.add, op1=ALU.subtract).then_inc(a_lo_ready, 1)

                dve.wait_ge(gain_ready, m + 1)
                scale(0)
                for k in range(KT):
                    if k + 1 < KT:
                        scale(k + 1)
                    low(k)

            for n, (tile, value) in enumerate(((ones, 1.0), (mean_d, 1.0 / D), (mean_head, 1.0 / P), (eps, EPS))):
                nc.vector.memset(tile[:], value).then_inc(consts_set, 1)
            dve.wait_ge(filt_landed, 16 * 5)
            nc.vector.memset(lb_tmp[:], 0.0).then_inc(consts_set, 1)
            for n, dst in enumerate((p_a, p_b, p_c, p_d)):
                dve.wait_ge(rows_turned, n + 1)
                w, r = dst[:].shape
                nc.vector.tensor_copy(dst[:], bank[2 + n][0:w, 0:r]).then_inc(params_ready, 1)
            dve.wait_ge(params_ready, 4)
            dve.wait_ge(consts_set, 5)
            bounds = p_b[:, B_LOWER:B_LOWER + 16]
            tt(lb_tmp[:, 0], bounds, bounds, ALU.subtract).then_inc(lb_step, 1)
            dve.wait_ge(c_sig_ready, 1)
            tt(c_silu[:], p_a[:, A_C:A_C + 8], c_sig[:], ALU.mult).then_inc(c_silu_ready, 1)
            dve.wait_ge(lb_exp, 1)
            nc.vector.reciprocal(lb_tmp[:, 2], lb_tmp[:, 1]).then_inc(lb_step, 1)
            dve.wait_ge(lb_step, 2)
            tt(lb_tmp[:, 3], lb_tmp[:, 1], lb_tmp[:, 2], ALU.mult).then_inc(lb_step, 1)
            dve.wait_ge(lb_step, 3)
            tt(lb[:], lb_tmp[:, 3], lb_tmp[:, 3], ALU.subtract).then_inc(lb_step, 1)
            dve.wait_ge(lb_step, 4)
            ts(one_m_lb[:], lb[:], -1.0, 1.0, ALU.mult, ALU.add).then_inc(lb_step, 1)
            dve.wait_ge(c_silu_ready, 1)

            def reduce_angle(layer):
                dve.wait_ge(pre_sine, layer + 1)
                n = 6 * layer
                steps = (
                    lambda: ts(angle[:, 0], bank[4][0:FW], p_d[:, layer:layer + 1], p_d[:, 3:4], ALU.add, ALU.mult),
                    lambda: ts(turns[0], angle[:, 0], 1.0 / (2.0 * math.pi), ROUNDER, ALU.mult, ALU.add),
                    lambda: ts(turns[1], turns[0], ROUNDER, None, ALU.subtract),
                    lambda: stt(out=angle[:, 1], in0=turns[1], scalar=-TWO_PI_HIGH, in1=angle[:, 0],
                                op0=ALU.mult, op1=ALU.add),
                    lambda: stt(out=turns[0], in0=turns[1], scalar=-TWO_PI_LOW,
                                in1=angle[:, 1], op0=ALU.mult, op1=ALU.add),
                    lambda: ts(angle[:, 1], turns[0], 3.1415925, -3.1415925, ALU.min, ALU.max),
                )
                for step in steps:
                    if n:
                        dve.wait_ge(angle_step, n)
                    step().then_inc(angle_step, 1)
                    n += 1

            q = 0
            for layer in range(3):
                if layer:
                    dve.wait_ge(hidden_ready, layer)
                reduce_angle(layer)
                if layer == 0:
                    dve.wait_ge(out_rates_landed, 32)
                    tt(w_even[:], f_w_out[:, 0], f_w_out[:, 1], ALU.add).then_inc(w_even_ready, 1)
                    dve.wait_ge(w_even_ready, 1)
                    tt(f_w_out[:, 1], f_w_out[:, 0], f_w_out[:, 1], ALU.subtract).then_inc(w_even_ready, 1)
                for _ in range((1, 2, 2)[layer]):
                    ada_piece(q, ada_w0, ada_acc0, 0)
                    q += 1
            n = 0
            for j in range(4):
                dve.wait_ge(decay_ready, j + 1)
                for part in range(2):
                    for half in range(2):
                        dve.wait_ge(taps_raw, n + 1)
                        cols = slice(half * 512, half * 512 + 512)
                        tt(taps[:, part, j, cols], bank[4 + n % 2][:], decay[:, j % 2, cols],
                           ALU.mult).then_inc(taps_ready, 1)
                        if n % 2 or n == 8:
                            ada_piece(q, ada_w0, ada_acc0, 0)
                            q += 1
                        n += 1
                if j == 0:
                    dve.wait_ge(taps_ready, 4)
                    tt(taps0, taps[0:1, 0, 0], taps[0:1, 1, 0], ALU.add).then_inc(tap0_step, 1)
                    dve.wait_ge(tap0_step, 1)
                    stt(out=taps[0:1, 0, 0], in0=taps0, scalar=0.5, in1=skip_row[:], op0=ALU.mult,
                        op1=ALU.add).then_inc(tap0_step, 1)
            def spectrum_part(n):
                quarter, part = n // 2, n % 2
                dve.wait_ge(spec_even, n + 1)
                dve.wait_ge(spec_parts, 2 * n + 2)
                if quarter >= 2 and part == 0:
                    dve.wait_ge(spec_stored[quarter % 2], 32)
                for minus in range(2):
                    tt(h_out[:, quarter % 2, 2 * minus + part], even_s[:, part], bank[SPEC_BANKS[n % 3][1]][:],
                       ALU.subtract if minus else ALU.add).then_inc(spec_ready, 1)

            while q < 16:
                spectrum_part(q - 14)
                ada_piece(q, ada_w0, ada_acc0, 0)
                q += 1
            spectrum_part(2)
            spectrum_part(3)
            take_mod(0)
            take_mod(1)
            spectrum_part(4)
            spectrum_part(5)
            dve.wait_ge(std_ready, 1)
            nc.vector.reciprocal(rstd_cols[:], std_cols[:]).then_inc(rstd_ready, 1)
            make_gain(0)
            spectrum_part(6)
            spectrum_part(7)
            dve.wait_ge(rstd_spread, 1)
            dve.wait_ge(spec_ready, 16)
            norm_apply(0)

            def q_input(g):
                s = 5 * g
                dve.wait_ge(q_sig_ready, v(g + 1))
                tt(q_silu[:], bank[s % 2][:], q_sig, ALU.mult).then_inc(evicted[s % 2], 1)
                dve.wait_ge(evicted[s % 2], v(s // 2 + 1))

            def gate_input(g, way):
                s, b, col = 5 * g + 2 + way, g % 2, g + 8 * way
                if way == 0 and g >= 2:
                    dve.wait_ge(far_scores, v(3 * (g - 1)))
                    dve.wait_ge(level_scores, v(8 * (g - 1)))
                dve.wait_ge(f_pos_ready, v(2 * g + way + 1))
                for place in ((1,) if way == 0 else (0, 2)):
                    ts(gates[:, place], f_pos[:], one_m_lb[:, bass.ds(v(col), 1)], lb[:, bass.ds(v(col), 1)], ALU.mult,
                       ALU.add).then_inc(gate_ready, 1)
                dve.wait_ge(evicted[s % 2], v(s // 2 + 1))
                ts(KK[b][:, way], f_neg[:], one_m_lb[:, bass.ds(v(col), 1)], None, ALU.mult).then_inc(key_ready, 1)
                dve.wait_ge(gate_ready, v(3 * g + (1 if way == 0 else 3)))
                tt(QQ[b][:, 1 - way], q_silu[:], gates[:, 1 if way == 0 else 0],
                   ALU.mult).then_inc(query_ready, 1)

            def own_input(g):
                b = g % 2
                dve.wait_ge(key_ready, v(2 * g + 2))
                tt(tmp_a[:, 0], KK[b][:, 0], KK[b][:, 1], ALU.add).then_inc(own_sum_ready, 1)
                dve.wait_ge(own_sum_ready, v(g + 1))
                if g:
                    dve.wait_ge(level_scores, v(8 * g - 7))
                tt(own[:], q_silu[:], tmp_a[:, 0], ALU.mult).then_inc(own_ready, 1)

            def gate_output(g):
                s = 5 * g + 4
                dve.wait_ge(g_sig_ready, v(g + 1))
                stt(out=out_gate[:], in0=bank[s % 2][:], scalar=p_b[:, B_HEAD_G:B_HEAD_G + 1], in1=g_sig,
                    op0=ALU.mult, op1=ALU.mult).then_inc(evicted[s % 2], 1)
                dve.wait_ge(evicted[s % 2], v(s // 2 + 1))

            diag = view(scores, 0, [L + P, TT], [1, P])

            def take_level(h, n):
                dve.wait_ge(level_scores, v(8 * h + n + 1))
                if n == 0:
                    if h:
                        dve.wait_ge(mixed, v(h))
                    ins = nc.vector.tensor_copy(diag, bank[2][:].rearrange("p (t n) -> p t n", t=TT))
                else:
                    dve.wait_ge(diag_scores, v(8 * h + n))
                    if isinstance(h, At):
                        dve.nop(nofuse=True)
                    m = view(mask, (n - 1) * P, [0, TT], [1, P])
                    ins = nc.vector.copy_predicated(diag, m,
                                                    bank[3 - (n - 1) % 2][:].rearrange("p (t n) -> p t n", t=TT))
                ins.then_inc(diag_scores, 1)

            def carry(h, n):
                b = h % 2
                width = 1 << n
                blocks = L // width
                t = gates if n == 0 else block_gates[width]
                if n:
                    dve.wait_ge(level_gates, v(7 * h + n))
                    dve.wait_ge(level_keys, v(8 * h + n))
                    dve.wait_ge(level_queries, v(8 * h + n))
                if n == 7:
                    dve.wait_ge(far_scores, v(3 * h + 1))
                else:
                    dve.wait_ge(keys_joined, v(7 * h + n + 1))
                dims = ([2 * width, 256 // width], [L + width, 2], [1, width])
                gate_dims = ([2, 256 // width], [blocks - 1, 2], [0, width])
                tt(view(KK[b], 0, *dims), view(KK[b], 0, *dims), view(t, blocks + 1, *gate_dims),
                   ALU.mult).then_inc(level_keys, 1)
                if n < 7:
                    dve.wait_ge(level_scores, v(8 * h + n + 2))
                tt(view(QQ[b], 0, *dims), view(QQ[b], 0, *dims), view(t, 1, *gate_dims),
                   ALU.mult).then_inc(level_queries, 1)
                if n < 7:
                    tt(block_gates[2 * width][:], t[:, :, 0:blocks:2], t[:, :, 1:blocks:2],
                       ALU.mult).then_inc(level_gates, 1)

            def head_output(h, g):
                dve.wait_ge(mixed_sq, v(h + 1))
                tt(tmp_a[:, 1], bank[5][:], out_gate[:], ALU.mult).then_inc(normed_ready, 1)
                dve.wait_ge(head_std, v(h + 1))
                nc.vector.reciprocal(rstd_cols[:], std_cols[:]).then_inc(head_rstd, 1)
                if g < HEADS:
                    gate_input(g, 1)
                    own_input(g)
                dve.wait_ge(normed_ready, v(h + 1))
                dve.wait_ge(head_spread, v(h + 1))
                tt(tmp_b[:, h % 2], tmp_a[:, 1], bank[7][:], ALU.mult).then_inc(gated_ready, 1)
                dve.wait_ge(gated_ready, v(h + 1))
                if g < HEADS:
                    gate_output(g)
                dve.wait_ge(o_hi_ready, v(h + 1))
                tt(one_row(h_lo, h), tmp_b[:, h % 2], one_row(h_hi, h).bitcast(F32), ALU.subtract).then_inc(
                    o_lo_ready, 1)

            dve.wait_ge(mask_landed, 16)
            for parts_stored in spec_stored:
                dve.wait_ge(parts_stored, 64)
            nc.vector.tensor_copy(mask[:].rearrange("p l n -> p (l n)"),
                                  scores[:, 0:2].rearrange("p a n -> p (a n)")[:, 0:len(LEVELS) * P]).then_inc(
                mask_set, 1)
            dve.wait_ge(mask_set, 1)
            def head_step(g):
                h = g - 1
                if isinstance(g, int) and g == 0:
                    q_input(g)
                    gate_input(g, 0)
                    gate_input(g, 1)
                    own_input(g)
                    gate_output(g)
                    return
                if g % 2 and g >= 3:
                    take_mod(2 + (g - 3) // 2)
                for n in range(8):
                    if n:
                        carry(h, n - 1)
                    take_level(h, n)
                    if n == 3 and g < HEADS:
                        q_input(g)
                    if n in (3, 4, 5, 7):
                        ada_piece(16 + 4 * h + (3, 4, 5, 7).index(n), ada_w1, ada_acc1, 16)
                if g < HEADS:
                    gate_input(g, 0)
                carry(h, 7)
                head_output(h, g)

            head_step(0)
            head_step(1)
            with dve.Fori(0, HEADS // 2 - 1) as pair:
                head_step(At(pair, 2, 2))
                head_step(At(pair, 2, 3))
            head_step(HEADS)

            def residual(m, s, n):
                dve.wait_ge(slab_done, v(s + 1))
                stt(out=xT[:, n], in0=bank[s % 2][:], scalar=mod[:, 24 * m + 16 + n:24 * m + 17 + n], in1=xT[:, n],
                    op0=ALU.mult, op1=ALU.add).then_inc(evicted[s % 2], 1)

            def norm(m, gate, s0):
                for n in range(KT):
                    residual(gate, s0 + n, n)
                    if n:
                        add_square(m, n - 1)
                    if m == 1 and n == 3:
                        take_mod(5)
                add_square(m, 7)
                norm_rstd(m)
                if m < 4:
                    norm_apply(m)

            norm(1, 0, S_HG_OUT)

            def chunk(i, s0, ch, first, last, with_ada):
                for n in range(8):
                    s, j = 16 * ch + (s0 + n), 8 * ch + (8 * CHUNKS * i + n)
                    dve.wait_ge(evicted[s % 2], v(s // 2 + 1))
                    r = tmp_a[:, n % 2]
                    tt(h_hi[:, n], r, r, ALU.mult).then_inc(h_hi_ready, 1)
                    dve.wait_ge(h_hi_ready, v(j + 1))
                    dve.wait_ge(relu_sq_ready, v(j + 1))
                    tt(h_lo[:, n], tmp_b[:, n % 2], h_hi[:, n].bitcast(F32), ALU.subtract).then_inc(h_lo_ready, 1)
                    if with_ada and not first and n == 2:
                        take_mod(2 * ch + 5)
                    if with_ada and not last:
                        ada_piece(16 * ch + (48 + n), ada_w2, ada_acc2, 48)
                for n in range(8):
                    residual(2 * i + 1, 16 * ch + (s0 + 8 + n), n)
                    if last and n:
                        add_square(2 * i + 2, n - 1)
                    if with_ada and not last:
                        if n == 2:
                            take_mod(2 * ch + 6)
                        ada_piece(16 * ch + (56 + n), ada_w2, ada_acc2, 48)

            def mlp(i, s0, with_ada):
                chunk(i, s0, 0, True, False, with_ada)
                with dve.Fori(1, CHUNKS - 1) as ch:
                    chunk(i, s0, At(ch), False, False, with_ada)
                chunk(i, s0, CHUNKS - 1, False, True, with_ada)
                m = 2 * i + 2
                add_square(m, 7)
                norm_rstd(m)
                if m < 4:
                    norm_apply(m)

            mlp(0, S_MLP0, True)

            for seg in range(3):
                nc.vector.memset(view(padded[seg], 0, [L + 1, 2]), 0.0).then_inc(pad_set, 1)

            def convolve(g, j):
                s = S_HY_IN + 6 * g + j
                seg, n = HY_ORDER[j]
                par = group_params[g % 2]
                dst = x0[:, n] if seg == 0 else conv[seg - 1][:]
                dve.wait_ge(evicted[s % 2], s // 2 + 1)
                if seg and 2 * g + n:
                    dve.wait_ge(z_ready, 2 * g + n)
                if seg == 0 and g:
                    dve.wait_ge(y_gated, 2 * g - 1 + n)
                c0 = 3 * (6 * g + j)
                ts(dst, padded[seg][:, 0:L], par[:, 0, seg, n:n + 1], par[:, 4, seg, n:n + 1], ALU.mult,
                   ALU.add).then_inc(conv_step, 1)
                for tap in (1, 2):
                    dve.wait_ge(conv_step, c0 + tap)
                    stt(out=dst, in0=padded[seg][:, tap:tap + L], scalar=par[:, tap, seg, n:n + 1], in1=dst,
                        op0=ALU.mult, op1=ALU.add).then_inc(conv_step, 1)
                dve.wait_ge(conv_step, c0 + 3)

            def make_z(g, n):
                if g:
                    dve.wait_ge(z_turned, 2 * g + n - 1)
                by_parity = "p (n a) -> p a n"
                tt(z[n][:].rearrange("p (a n) -> p a n", a=2), conv[0][:].rearrange(by_parity, a=2),
                   conv[1][:].rearrange(by_parity, a=2), ALU.mult).then_inc(z_ready, 1)

            def spectral(h, m):
                n = 2 * h + m
                dve.wait_ge((H_landed0, H_landed1)[m], 16 * (h + 1))
                dve.wait_ge(z_even, n + 1)
                dve.wait_ge(z_parts, 2 * n + 2)
                odd = bank[3][:].rearrange("p (a n) -> p a n", a=2)
                tt(Z[:, 0:2], even_z, odd, ALU.add).then_inc(Z_ready, 1)
                tt(Z[:, 2:4], even_z, odd, ALU.subtract).then_inc(Z_ready, 1)
                dve.wait_ge(Z_ready, 2 * n + 2)
                tt(ZH[:], Z, H[m][:], ALU.mult).then_inc(ZH_ready, 1)
                dve.wait_ge(ZH_ready, 2 * n + 1)
                tt(Y[:, 0:4:2], ZH[:, 0:4:2], ZH[:, 1:4:2], ALU.subtract).then_inc(Y_ready, 1)
                dve.wait_ge(Y_ready, 2 * n + 1)
                swapped = view(H[m], GC, [2 * GC, 2], [-GC, 2], [1, GC])
                tt(ZH[:].rearrange("p (a b) n -> p a b n", a=2), Z.rearrange("p (a b) n -> p a b n", a=2), swapped,
                   ALU.mult).then_inc(ZH_ready, 1)
                dve.wait_ge(ZH_ready, 2 * n + 2)
                tt(Y[:, 1:4:2], ZH[:, 0:4:2], ZH[:, 1:4:2], ALU.add).then_inc(Y_ready, 1)
                dve.wait_ge(Y_ready, 2 * n + 2)
                if h and m == 0:
                    dve.wait_ge(y_ready, 2 * h)
                tt(folded[:, m, 0], Y[:, 0:2], Y[:, 2:4], ALU.add).then_inc(folded_ready, 1)
                tt(folded[:, m, 1], Y[:, 0:2], Y[:, 2:4], ALU.subtract).then_inc(folded_ready, 1)

            def gate_y(h, n):
                dve.wait_ge(y_ready, 2 * h + n + 1)
                by_parity = [[1, 2], [2, 256]]
                tt(view(tmp_b, n * L, *by_parity), bank[5 + n][:].rearrange("p (a n) -> p a n", a=2),
                   view(x0, n * L, *by_parity), ALU.mult).then_inc(y_gated, 1)

            def low_y(h, n):
                dve.wait_ge(y_gated, 2 * h + n + 1)
                dve.wait_ge(y_hi_ready, 2 * h + n + 1)
                k = 2 * h + n
                tt(h_lo[:, k], tmp_b[:, n], h_hi[:, k].bitcast(F32), ALU.subtract).then_inc(y_lo_ready, 1)

            for g in range(GROUPS + 1):
                h = g - 1
                if g < GROUPS:
                    nc.vector.tensor_copy(group_params[g % 2][:],
                                          view(p_c, 2 * g, [24, 5], [8, 3], [1, 2])).then_inc(group_ready, 1)
                    dve.wait_ge(group_ready, g + 1)
                    convolve(g, 0)
                    if g:
                        spectral(h, 0)
                    convolve(g, 1)
                    make_z(g, 0)
                    convolve(g, 2)
                    if g:
                        spectral(h, 1)
                    convolve(g, 3)
                    make_z(g, 1)
                    if g:
                        gate_y(h, 0)
                        gate_y(h, 1)
                    convolve(g, 4)
                    convolve(g, 5)
                    if g:
                        low_y(h, 0)
                        low_y(h, 1)
                else:
                    spectral(h, 0)
                    spectral(h, 1)
                    gate_y(h, 0)
                    gate_y(h, 1)
                    low_y(h, 0)
                    low_y(h, 1)
            norm(3, 2, S_HY_OUT)
            mlp(1, S_MLP1, False)

            for k in range(KT):
                if k >= 2:
                    dve.wait_ge(o_turned, k - 1)
                stt(out=tmp_b[:, k % 2], in0=xT[:, k], scalar=p_b[:, B_FINAL_G + k:B_FINAL_G + k + 1],
                    in1=bank[7][:], op0=ALU.mult, op1=ALU.mult).then_inc(final_ready, 1)


INPUTS = ["x", "c", "ada_w", "ada_b", "norm_g", "hg_w_in", "hg_lower_bounds", "hg_norm_g", "hg_w_out",
          "hy_w_in", "hy_b_in", "hy_conv_w", "hy_conv_b", "hy_filt_w_in", "hy_filt_w_mid", "hy_filt_b",
          "hy_filt_freq", "hy_filt_w_out", "hy_skip", "hy_w_out", "mlp_w1", "mlp_w2", "final_g"]


def kernel(**inputs):
    import concourse.bacc as bacc
    from concourse.bass_utils import run_bass_kernel_spmd

    nc = bacc.Bacc("TRN2", target_bir_lowering=False, num_devices=1)
    arrays = {name: np.ascontiguousarray(inputs[name]) for name in INPUTS}
    forward, inverse = transform_tables()
    emb_t, rates, times = filter_constants()
    arrays |= {"fwd_table": forward, "inv_table": inverse, "emb_t": emb_t, "decay_rates": rates,
               "minus_times": times, "masks": level_masks(), "identity": np.eye(P, dtype=np.float32)}
    tensors = [nc.dram_tensor(n, a.shape, mybir.dt.from_np(a.dtype), kind="ExternalInput").ap()
               for n, a in arrays.items()]
    out = nc.dram_tensor("out", (1, L, D), F32, kind="ExternalOutput").ap()
    hybrid_encoder(nc, *tensors, out)
    result = run_bass_kernel_spmd(nc, [arrays], core_ids=[0])
    return result.results[0]["out"]
```
